# Optimizing a Trainium2 kernel written in Bass

```python
import jax, jax.numpy as jnp
from jax import lax
import numpy as np

D_MODEL = 1024
BATCH = 1
SEQ = 256
DEPTH = 1
DEC_BATCH = 1
DEC_SEQ = 1024
PAST_LEN = 512

GRID_W = 64
D_A = D_MODEL
A_GROUPS = 4
A_CHUNK = 128
D_B = D_MODEL
POOL_WINDOWS = (2, 4, 8, 16)
B_GROUPS = len(POOL_WINDOWS)
B_GW = D_B // B_GROUPS
RET_HEADS = 4
RET_DV = D_MODEL // RET_HEADS
RET_DK = RET_DV // 2
RET_CHUNK = 128
PEER_HEADS = 8
PEER_NKEYS = 128
PEER_EXPERTS = PEER_NKEYS * PEER_NKEYS
PEER_DKEY = 256
PEER_TOPK = 16
PEER_BLOCK = 128
N_BRANCH = 3
EPS = 1e-6

IN_SPLITS = (D_A, D_A, D_B, RET_HEADS * RET_DK, RET_HEADS * RET_DK, RET_HEADS * RET_DV,
             RET_HEADS * RET_DV, RET_HEADS * RET_DV, N_BRANCH * D_MODEL)
IN_COLS = sum(IN_SPLITS)
IN_OFFSETS = tuple(int(o) for o in np.cumsum(IN_SPLITS)[:-1])

kernel_name = 'hybrid_gmlp_pool_retention_peer_flow_step'

def _rmsnorm(x, g):
    xf = x.astype(jnp.float32)
    y = xf * lax.rsqrt(jnp.mean(xf * xf, axis=-1, keepdims=True) + EPS)
    return (y * g.astype(jnp.float32)).astype(x.dtype)

def _layernorm(x, g):
    xf = x.astype(jnp.float32)
    xc = xf - jnp.mean(xf, axis=-1, keepdims=True)
    y = xc * lax.rsqrt(jnp.mean(xc * xc, axis=-1, keepdims=True) + EPS)
    return (y * g.astype(jnp.float32)).astype(x.dtype)

def _head_norm(o):
    return o * lax.rsqrt(jnp.mean(o * o, axis=-1, keepdims=True) + EPS)

def _gmlp_mix(u, v, ws, bs, ln_g):
    b_, n, _ = v.shape
    nc = n // A_CHUNK
    vn = _layernorm(v, ln_g).reshape(b_, nc, A_CHUNK, A_GROUPS, D_A // A_GROUPS)
    sv = jnp.einsum('gij,bcjgd->bcigd', ws, vn) + bs.T[:, :, None]
    return u * sv.reshape(b_, n, D_A).astype(u.dtype)

def _box_sum(x, w, axis):
    a = w // 2
    b = w - 1 - a
    n = x.shape[axis]
    pad = [(0, 0)] * x.ndim
    pad[axis] = (a + 1, b)
    cs = jnp.cumsum(jnp.pad(x, pad), axis=axis)
    return lax.slice_in_dim(cs, w, w + n, axis=axis) - lax.slice_in_dim(cs, 0, n, axis=axis)

def _pool_mix(z, pool_w, pool_scale, grid):
    b_, n, _ = z.shape
    zf = z.astype(jnp.float32)
    outs = []
    for gi, w in enumerate(POOL_WINDOWS):
        zg = zf[..., gi * B_GW:(gi + 1) * B_GW]
        if grid:
            rows = n // GRID_W
            s = _box_sum(_box_sum(zg.reshape(b_, rows, GRID_W, B_GW), w, 1), w, 2)
            cnt_r = _box_sum(jnp.ones((rows,), jnp.float32), w, 0)
            cnt_c = _box_sum(jnp.ones((GRID_W,), jnp.float32), w, 0)
            cnt = cnt_r[:, None] * cnt_c[None, :]
            mean = (s / cnt[None, :, :, None]).reshape(b_, n, B_GW)
        else:
            s = _box_sum(zg, w, 1)
            cnt = _box_sum(jnp.ones((n,), jnp.float32), w, 0)
            mean = s / cnt[None, :, None]
        outs.append(jnp.einsum('bnc,cd->bnd', mean - zg, pool_w[gi].astype(jnp.float32)))
    return (jnp.concatenate(outs, axis=-1) * pool_scale.astype(jnp.float32)).astype(z.dtype)

def _retention_dir(q, k, v, log_gamma, s0):
    b_, n = q.shape[:2]
    nc = n // RET_CHUNK
    cl = RET_CHUNK
    q = q.reshape(b_, nc, cl, RET_HEADS, RET_DK)
    k = k.reshape(b_, nc, cl, RET_HEADS, RET_DK)
    v = v.reshape(b_, nc, cl, RET_HEADS, RET_DV)
    pos = jnp.arange(cl, dtype=jnp.float32)
    rel = pos[:, None] - pos[None, :]
    dmask = jnp.where(rel >= 0, jnp.exp(log_gamma[:, None, None] * jnp.maximum(rel, 0.0)), 0.0)
    scores = jnp.einsum('bcihk,bcjhk->bchij', q, k) * dmask
    o_in = jnp.einsum('bchij,bcjhv->bcihv', scores, v)
    k_dec = jnp.exp((cl - 1.0 - pos)[:, None] * log_gamma[None, :])
    kv = jnp.einsum('bcjhk,jh,bcjhv->cbhkv', k, k_dec, v)
    chunk_decay = jnp.exp(cl * log_gamma)[None, :, None, None]

    def step(s, kv_c):
        return chunk_decay * s + kv_c, s

    s_fin, s_prev = lax.scan(step, s0, kv)
    q_dec = jnp.exp((pos + 1.0)[:, None] * log_gamma[None, :])
    o_x = jnp.einsum('bcihk,ih,cbhkv->bcihv', q, q_dec, s_prev)
    return (o_in + o_x).reshape(b_, n, RET_HEADS, RET_DV), s_fin

def _retention(q, k, v, g_f, g_b, log_gamma, s0_f, s0_b):
    o_f, s_f = _retention_dir(q, k, v, log_gamma[0], s0_f)
    flip = lambda t: jnp.flip(t, axis=1)
    o_b, s_b = _retention_dir(flip(q), flip(k), flip(v), log_gamma[1], s0_b)
    o_b = flip(o_b)
    y = jax.nn.silu(g_f) * _head_norm(o_f) + jax.nn.silu(g_b) * _head_norm(o_b)
    b_, n = q.shape[:2]
    return y.reshape(b_, n, RET_HEADS * RET_DV), s_f, s_b

def _peer(h, wq, subkeys, u_tab, v_tab):
    b_, n, d = h.shape
    xb = h.reshape(-1, PEER_BLOCK, d)

    def block(xt):
        t = xt.shape[0]
        qp = (xt @ wq).reshape(t, PEER_HEADS, 2, PEER_DKEY // 2)
        sc = jnp.einsum('thsk,hsnk->thsn', qp, subkeys).astype(jnp.float32)
        top_s, top_i = lax.top_k(sc, PEER_TOPK)
        cand_s = (top_s[:, :, 0, :, None] + top_s[:, :, 1, None, :]).reshape(t, PEER_HEADS, PEER_TOPK * PEER_TOPK)
        cand_i = (top_i[:, :, 0, :, None] * PEER_NKEYS + top_i[:, :, 1, None, :]).reshape(t, PEER_HEADS, PEER_TOPK * PEER_TOPK)
        best_s, best_p = lax.top_k(cand_s, PEER_TOPK)
        expert = jnp.take_along_axis(cand_i, best_p, axis=-1)
        g = jax.nn.softmax(best_s, axis=-1)
        act = jax.nn.gelu(jnp.einsum('thkd,td->thk', u_tab[expert], xt).astype(jnp.float32))
        wgt = (g * act).astype(xt.dtype)
        return jnp.einsum('thk,thkd->td', wgt, v_tab[expert]).astype(xt.dtype)

    return lax.map(block, xb).reshape(b_, n, d)

def _layer(x, cond, lp, grid, s0_f, s0_b):
    b_, n, _ = x.shape
    mod = (jax.nn.silu(cond) @ lp['w_mod'] + lp['b_mod'])[:, None, :]
    sh1, sc1, gt1, sh2, sc2, gt2 = jnp.split(mod.astype(x.dtype), 6, axis=-1)
    h = _rmsnorm(x, lp['norm_g'][0]) * (1 + sc1) + sh1
    proj = h @ lp['w_in']
    u, v, zb, q, k, rv, rg_f, rg_b, gm = jnp.split(proj, IN_OFFSETS, axis=-1)
    y_a = _gmlp_mix(jax.nn.gelu(u), jax.nn.gelu(v), lp['gmlp_ws'], lp['gmlp_b'], lp['gmlp_ln_g'])
    y_b = _pool_mix(zb, lp['pool_w'], lp['pool_scale'], grid)
    heads = lambda t, dh: t.reshape(b_, n, RET_HEADS, dh).astype(jnp.float32)
    log_gamma = jax.nn.log_sigmoid(lp['ret_decay'].astype(jnp.float32))
    y_c, s_f, s_b = _retention(heads(q, RET_DK), heads(k, RET_DK) * (RET_DK ** -0.5), heads(rv, RET_DV),
                               heads(rg_f, RET_DV), heads(rg_b, RET_DV), log_gamma, s0_f, s0_b)
    ga, gb, gc = jnp.split(jax.nn.sigmoid(gm), N_BRANCH, axis=-1)
    merged = ga * y_a + gb * y_b + gc * y_c.astype(x.dtype)
    x = x + gt1 * (merged @ lp['w_out'])
    h2 = _rmsnorm(x, lp['norm_g'][1]) * (1 + sc2) + sh2
    x = x + gt2 * _peer(h2, lp['peer_wq'], lp['peer_subkeys'], lp['peer_u'], lp['peer_v'])
    return x, s_f, s_b

def setup_inputs(seed: int = 0) -> dict:
    key = jax.random.key(seed)
    ks = jax.random.split(key, 21)
    f32 = jnp.float32
    nrm = lambda k, shape, s: jax.random.normal(k, shape, f32) * s
    base_logit = jnp.log(2.0 ** (5.0 + jnp.arange(RET_HEADS, dtype=f32)) - 1.0)
    return {
        'x_prompt': nrm(ks[0], (BATCH, SEQ, D_MODEL), 1.0),
        'x_sample': nrm(ks[1], (DEC_BATCH, DEC_SEQ, D_MODEL), 1.0),
        'state_ret': nrm(ks[2], (DEC_BATCH, DEPTH, 2, RET_HEADS, RET_DK, RET_DV), 1.0),
        'c': nrm(ks[3], (DEC_BATCH, D_MODEL), 1.0),
        'c_ctx': nrm(ks[4], (D_MODEL,), 1.0),
        'w_mod': nrm(ks[5], (DEPTH, D_MODEL, 6 * D_MODEL), 0.5 * D_MODEL ** -0.5),
        'b_mod': nrm(ks[6], (DEPTH, 6 * D_MODEL), 0.01),
        'norm_g': 1.0 + nrm(ks[7], (DEPTH, 2, D_MODEL), 0.02),
        'w_in': nrm(ks[8], (DEPTH, D_MODEL, IN_COLS), D_MODEL ** -0.5),
        'w_out': nrm(ks[9], (DEPTH, D_MODEL, D_MODEL), D_MODEL ** -0.5),
        'gmlp_ws': nrm(ks[10], (DEPTH, A_GROUPS, A_CHUNK, A_CHUNK), 0.5 * A_CHUNK ** -0.5),
        'gmlp_b': 1.0 + nrm(ks[11], (DEPTH, A_GROUPS, A_CHUNK), 0.02),
        'gmlp_ln_g': 1.0 + nrm(ks[12], (DEPTH, D_A), 0.02),
        'pool_w': nrm(ks[13], (DEPTH, B_GROUPS, B_GW, B_GW), B_GW ** -0.5),
        'pool_scale': 1.0 + nrm(ks[14], (DEPTH, D_B), 0.02),
        'ret_decay': base_logit[None, None, :] + nrm(ks[15], (DEPTH, 2, RET_HEADS), 0.1),
        'peer_wq': nrm(ks[16], (DEPTH, D_MODEL, PEER_HEADS * PEER_DKEY), D_MODEL ** -0.5),
        'peer_subkeys': nrm(ks[17], (DEPTH, PEER_HEADS, 2, PEER_NKEYS, PEER_DKEY // 2), (PEER_DKEY // 2) ** -0.5),
        'peer_u': nrm(ks[18], (DEPTH, PEER_EXPERTS, D_MODEL), D_MODEL ** -0.5),
        'peer_v': nrm(ks[19], (DEPTH, PEER_EXPERTS, D_MODEL), 0.5),
        'final_norm_g': 1.0 + nrm(ks[20], (D_MODEL,), 0.02),
    }

def reference(x_prompt, x_sample, state_ret, c, c_ctx, w_mod, b_mod, norm_g, w_in, w_out,
              gmlp_ws, gmlp_b, gmlp_ln_g, pool_w, pool_scale, ret_decay, peer_wq, peer_subkeys,
              peer_u, peer_v, final_norm_g):
    xc = x_prompt
    xs = x_sample
    zero_state = jnp.zeros((x_prompt.shape[0], RET_HEADS, RET_DK, RET_DV), jnp.float32)
    cond_ctx = c_ctx[None, :]
    new_states = []
    for l in range(DEPTH):
        lp = {
            'w_mod': w_mod[l], 'b_mod': b_mod[l], 'norm_g': norm_g[l], 'w_in': w_in[l],
            'w_out': w_out[l], 'gmlp_ws': gmlp_ws[l], 'gmlp_b': gmlp_b[l], 'gmlp_ln_g': gmlp_ln_g[l],
            'pool_w': pool_w[l], 'pool_scale': pool_scale[l], 'ret_decay': ret_decay[l],
            'peer_wq': peer_wq[l], 'peer_subkeys': peer_subkeys[l], 'peer_u': peer_u[l],
            'peer_v': peer_v[l],
        }
        xc, s_f, s_b = _layer(xc, cond_ctx, lp, False, zero_state, zero_state)
        new_states.append(jnp.stack([s_f, s_b], axis=1))
        s0 = state_ret[:, l].astype(jnp.float32)
        xs, _, _ = _layer(xs, c, lp, True, s0[:, 0], s0[:, 1])
    new_state_ret = jnp.stack(new_states, axis=1).astype(x_prompt.dtype)
    y_prompt = _rmsnorm(xc, final_norm_g)
    y_sample = _rmsnorm(xs, final_norm_g)
    return (y_prompt, y_sample, new_state_ret)


_drawn_inputs = setup_inputs


def setup_inputs(seed=0):
    import zlib

    import numpy as np

    out = dict(_drawn_inputs(seed))
    spreads = {}
    factors = {'gmlp_b': 200.0,
     'gmlp_ln_g': 200.0,
     'pool_scale': 140.678,
     'final_norm_g': 26.975,
     'state_ret': 23.272,
     'peer_wq': 5.366,
     'peer_subkeys': 5.408,
     'peer_u': 6.06,
     'peer_v': 5.387}
    for name, (base, spread) in spreads.items():
        noise = np.random.default_rng([zlib.crc32(name.encode()), seed]).standard_normal(out[name].shape)
        drawn = base * np.exp(spread * noise) if base else spread * noise
        out[name] = __import__('jax').numpy.asarray(drawn.astype(out[name].dtype))
    for name, factor in factors.items():
        out[name] = (out[name] * factor).astype(out[name].dtype)
    return out
```

```python
from contextlib import ExitStack, contextmanager

import numpy as np

import concourse.bass as bass
from concourse import mybir

ALU = mybir.AluOpType
ACT = mybir.ActivationFunctionType
AX = mybir.AxisListType
F32 = mybir.dt.float32
U32 = mybir.dt.uint32
ds = bass.ds

P = 128
D = 1024
KD = D // P
CTX = 256
LAT = 1024
T = CTX + LAT
NC = T // P
CC = CTX // P
EPS = 1e-6
GRID_W = 64
WINDOWS = (2, 4, 8, 16)
G = len(WINDOWS)
GW = D // G
HEADS = 4
DK = 128
DV = 256
PH = 8
NK = 128
TOP = 16
SLOTS = 8
UW = 512
LOWEST = -3.0e38

U_MOD, U_A, U_HEAD, U_Z, U_POOL, U_GB, U_OUT = 0, 12, 18, 26, 28, 36, 38

T_HT = 0
T_A = T_HT + 24
T_C = T_A + 60
HEAD_TILES = 26
T_Z = T_C + HEADS * HEAD_TILES
T_POOL = T_Z + 20
T_GB = T_POOL + 20
T_BC = T_GB + 20
T_MT = T_BC + 16
T_END = T_MT + 24
D_MOD = 0
D_MIX = D_MOD + 12
D_PW = D_MIX + 20
D_OUT = D_PW + 20
D_END = D_OUT + 20
TMP_A = 0
TMP_C = TMP_A + 20
TMP_HEAD = 15
TMP_GB = TMP_C + HEADS * TMP_HEAD

SEGS = ((0, 2, 0), (2, 4, 1), (6, 4, 1))


def box_matrix(n, w):
    a, b = w // 2, w - 1 - w // 2
    at = np.arange(n)
    return ((at[:, None] >= at[None, :] - a) & (at[:, None] <= at[None, :] + b)).astype(np.float64)


def pool_constants():
    rows = LAT // GRID_W
    lat = np.zeros((G, 2, P, LAT // P, UW), np.float32)
    ctx = np.zeros((P, G, CC, CTX), np.float32)
    for g, w in enumerate(WINDOWS):
        r, c = box_matrix(rows, w), box_matrix(GRID_W, w)
        m = np.kron(r / r.sum(0), c / c.sum(0)) - np.eye(LAT)
        lat[g] = m.reshape(LAT // P, P, 2, UW).transpose(2, 1, 0, 3)
        m = box_matrix(CTX, w)
        m = m / m.sum(0) - np.eye(CTX)
        ctx[:, g] = m.reshape(CC, P, CTX).transpose(1, 0, 2)
    return lat.reshape(2 * G, P, KD * UW), ctx.reshape(P, G * CC * CTX)


def pool_sources(g, half):
    w = WINDOWS[g]
    a, b = w // 2, w - 1 - w // 2
    rows = LAT // GRID_W
    first, last = half * rows // 2 - a, (half + 1) * rows // 2 - 1 + b
    return range(max(first, 0) // 2, min(last, rows - 1) // 2 + 1)


class Steps:

    def __init__(self, eng, sem, gate):
        self.eng, self.sem, self.gate, self.base, self.n = eng, sem, gate, 0, 0

    def wait(self, sem, value):
        if isinstance(value, int):
            if value > 0:
                self.eng.wait_ge(sem, value)
        else:
            self.eng.wait_ge(sem, value)
            self.eng.sem_inc(self.gate, 1)

    def step(self, ins):
        self.n += 1
        return ins.then_inc(self.sem, 1)

    def settle(self):
        self.wait(self.sem, self.base + self.n)

    def link(self, ins):
        self.step(ins)
        self.settle()

    @contextmanager
    def loop(self, trips, per_trip):
        base, n = self.base, self.n
        with self.eng.Fori(0, trips) as i:
            if per_trip:
                self.base = base + i * per_trip
            yield i
            assert self.n - n == per_trip, (self.n - n, per_trip)
        self.base, self.n = base, n + per_trip * trips


def build(nc, a):
    with ExitStack() as ctx:
        def sb(name, shape, dt=F32):
            return ctx.enter_context(nc.sbuf_tensor(name, shape, dt))

        def sem(name):
            return ctx.enter_context(nc.semaphore(name))

        HT0, RING0, GC0, A0, R0, AEND = 0, 10240, 18432, 20480, 30720, 43776
        arena = sb("arena", [P, AEND])

        def view(at, n, text=None, **kw):
            v = arena[:, at:at + n]
            return v.rearrange(text, **kw) if text else v

        hT = view(HT0, KD * T, "p (k t) -> p k t", k=KD)
        ring = view(RING0, 2 * KD * UW, "p (s k n) -> p s k n", s=2, k=KD)
        gcb = view(GC0, KD * DV, "p (k n) -> p k n", k=KD)
        mctx = view(GC0, G * CC * CTX, "p (g s t) -> p g s t", g=G, s=CC)
        A = view(A0, NC * D, "p (c d) -> p c d", c=NC)
        Z = view(R0, NC * D, "p (c d) -> p c d", c=NC)
        PT = view(R0 + NC * D, 2 * T, "p (b t) -> p b t", b=2)
        qT = view(R0, T)
        kT = view(R0 + T, T)
        vv = view(R0 + 2 * T, NC * DV, "p (c d) -> p c d", c=NC)
        O = view(R0 + 2 * T + NC * DV, NC * 2 * DV, "p (c r d) -> p c r d", c=NC, r=2)
        r1 = R0 + 2 * T + 3 * NC * DV
        kd = view(r1, 2 * P, "p (r n) -> p r n", r=2)
        sm = view(r1 + 256, 2 * P, "p (r n) -> p r n", r=2)
        qd = view(r1 + 512, 2 * P, "p (r n) -> p r n", r=2)
        S = view(r1 + 768, 8 * DV, "p (g r b d) -> p g r b d", g=2, r=2, b=2)
        uslot = view(0, SLOTS * D, "p (s d) -> p s d", s=SLOTS)
        vslot = view(SLOTS * D, SLOTS * D, "p (s d) -> p s d", s=SLOTS)
        h2 = view(16384, 2 * D, "p (b d) -> p b d", b=2)
        subk = view(GC0, 2 * PH * NK)
        wq = view(A0, KD * 2 * D, "p (k n) -> p k n", k=KD)
        bc = view(A0 + KD * 2 * D, 6 * D, "p (v j d) -> p v j d", v=3, j=2)
        small = view(43008, 6 * P, "p (v n) -> p v n", v=6)
        logit, expd, gsm, wgt, act, gelud = (small[:, i, :] for i in range(6))

        ident = sb("ident", [P, P])
        ones = sb("ones", [P, P])
        zeros = sb("zeros", [P, UW])
        rowbc = sb("rowbc", [P, D])
        mix = sb("mix", [P, G * P])
        m8 = sb("m8", [P, 2 * D])
        mask = m8[:, 0:D].rearrange("p (r h n) -> p r h n", r=2, h=HEADS)
        qdec = m8[:, D:2 * D].rearrange("p (r h n) -> p r h n", r=2, h=HEADS)
        pw = m8[:, :].rearrange("p (g b n) -> p g b n", g=G, b=2)
        gt1 = m8[:, :].rearrange("p (j d) -> p j d", j=2)
        h2T = m8[:, 0:D].rearrange("p (k t) -> p k t", k=KD)
        qp = m8[:, D:D + 256]
        qpT = m8[:, D + 256:D + 512].rearrange("p (s t) -> p s t", s=2)
        hot = m8[:, D + 512:2 * D].rearrange("p (s a b) -> p s a b", s=2, a=TOP)
        tmp = sb("tmp", [P, 4, UW])
        xo = tmp[:, 0:2, :].rearrange("p a n -> p (a n)")
        yb = tmp[:, 2:4, :].rearrange("p a n -> p (a n)")
        diag = sb("diag", [P, SLOTS, P])
        scr = diag[:, 0:8, :]
        bst = scr[:, 0, 0:120].rearrange("p (c s) -> p c s", c=NC)
        mv = scr[:, 1, 0:20].rearrange("p (c s) -> p c s", c=NC)
        relf, relb, rowf, rowb = (scr[:, i, :] for i in range(2, 6))
        late = sb("late", [P, NC * P])
        idx = late[:, :].bitcast(U32).rearrange("p (c n) -> p c n", c=NC)
        stage = sb("stage", [P, 2, 2, TOP], U32)
        rest = ones[:, :]
        cand = mix[:, 0:256].rearrange("p (a b) -> p a b", a=TOP)
        cand2 = mix[:, 256:512]
        tv = sb("tv", [P, 2, TOP])
        ti = sb("ti", [P, 2, TOP], U32)
        tf = sb("tf", [P, 2, TOP])
        bv = sb("bv", [P, TOP])
        bp = sb("bp", [P, TOP], U32)
        ab = sb("ab", [P, 2, TOP], U32)
        abf = sb("abf", [P, 2, TOP])
        picked = sb("picked", [P, 2, TOP])
        iota16 = sb("iota16", [P, TOP])
        act16 = sb("act16", [P, TOP])
        early_at = [0]

        def early(n):
            early_at[0] += n
            assert early_at[0] <= NC * P
            return late[:, early_at[0] - n:early_at[0]]

        cond = early(KD * 2)
        scond = early(KD * 2).rearrange("p (k j) -> p k j", k=KD)
        bmod = early(48)
        ng = early(2 * KD)
        mod = early(96).rearrange("p (b j) -> p b j", b=48)
        s12 = early(4 * KD).rearrange("p (n k j) -> p n k j", n=2, k=KD)
        bsp = early(G)
        decay = early(2 * HEADS)
        lg = early(6 * 2 * HEADS).rearrange("p (v n) -> p v n", v=6)
        kdec = early(2 * HEADS)
        gch = early(2 * HEADS)
        colf = early(2)
        ssq = early(2 * NC)
        rms = early(2 * NC)
        rst = early(2 * NC)
        one = sb("one", [P, 12])
        rsum = sb("rsum", [P, 2, PH])
        ps = ctx.enter_context(nc.psum_tensor("ps", [P, 8, 512], F32))

        names = """in_x in_const ring_0 ring_1 in_gc in_mctx in_pw in_psc in_state in_xagain in_fg
            in_subk in_wq xo_in x1_stored state_out y_stored
            act_full act_emptied dve_full dve_emptied tmp_free
            silu_done mod_done x_squared x_ms x_std x_normed
            ln_var ln_std ln_done pool_consts decay_in lg_exp lg_u lg_ln lg_done rel_done exps_done
            mask_done gate_a_done s_init kt_full kd_done sc_full sm_done qd_done o_full o_done kv_full
            state_done o_ms o_std o_ready pt_ready diag_ready row_diag merged z_done
            x1_done bc_done credit idx_done u_free v_free v_diag act_done gelu_done ls_done exp_done
            w_done gsm_done vacc_full vacc_free y_ms y_std y_done h2_done h2_trans h2T_done h2_sq
            h2_ms h2_std qp_full qp_done qpT_full qpT_done sc2_full sc2_free staged
            pe_gate act_gate dve_gate pool_gate sp_gate act_step dve_step pool_step""".split()
        s = {n: sem(n) for n in names}
        u_in = [sem(f"u_in_{i}") for i in range(SLOTS)]
        v_in = [sem(f"v_in_{i}") for i in range(SLOTS)]
        x1_in = [sem(f"x1_in_{i}") for i in range(2)]
        ring_in = [s["ring_0"], s["ring_1"]]

        x1d = nc.dram_tensor("x1_scratch", [NC, P, D], F32, kind="Internal").ap()
        block = ctx.enter_context(nc.Block())

        def phases(eng_steps, phase, per_pair):
            for p in range(4):
                phase(p, p % 2, p // 2)
            with eng_steps.loop((NC - 4) // 2, per_pair) as m:
                for par in range(2):
                    phase(m * 2 + 4 + par, par, m + 2)
            for p in (NC, NC + 1):
                phase(p, p % 2, p // 2)

        def does(p):
            if not isinstance(p, int):
                return True, True, True
            return p < NC, 1 <= p <= NC, p >= 2

        @block.sync
        def _(sp):
            st = Steps(sp, s["sp_gate"], s["sp_gate"])
            for c in range(NC):
                sp.dma_start(A[:, c, :], a["x"][c]).then_inc(s["in_x"], 16)

            def unit(src, slot, used_by, count):
                if used_by is not None:
                    sp.wait_ge(s[used_by], count)
                sp.dma_start(ring[:, slot].rearrange("p k n -> p (k n)"), src).then_inc(ring_in[slot], 16)

            for slot in range(2):
                unit(a["wmod"][slot], slot, None, 0)
            with sp.Fori(0, 5) as i:
                for slot in range(2):
                    unit(a["wmod"][i * 2 + 2 + slot], slot, "dve_full", i * 2 + (D_MOD + slot + 1))
            for slot in range(2):
                unit(a["wa"][slot], slot, "dve_full", D_MOD + 10 + slot + 1)
            with sp.Fori(0, 2) as i:
                for slot in range(2):
                    unit(a["wa"][i * 2 + 2 + slot], slot, "act_full", i * 20 + (T_A + 10 * (slot + 1)))
            with sp.Fori(0, HEADS) as h:
                for slot in range(2):
                    unit(a["whead"][h * 2 + slot], slot, "act_full",
                         h * HEAD_TILES + (T_C - (10, 0)[slot]))
                sp.wait_ge(s["act_full"], h * HEAD_TILES + T_C)
                sp.dma_start(gcb.rearrange("p k n -> p (k n)"), a["wgc"][h]).then_inc(s["in_gc"], 16)
                sp.wait_ge(s["dve_emptied"], D_PW)
                for r in range(2):
                    sp.dma_start(S[:, 1, r, 0, :], a["state"][r, h]).then_inc(s["in_state"], 16)
                sp.wait_ge(s["state_done"], h * (2 * NC) + 2 * CC)
                for r in range(2):
                    sp.dma_start(a["new_state"][r, h], S[:, 0, r, 0, :]).then_inc(s["state_out"], 16)
            sp.wait_ge(s["ln_done"], 1)
            sp.dma_start(rowbc[:, :], a["psc"]).then_inc(s["in_psc"], 16)
            unit(a["wz"][0], 0, "act_full", T_Z - 5)
            unit(a["wz"][1], 1, "act_full", T_Z - 5)
            sp.wait_ge(s["act_full"], T_Z)
            sp.dma_start(mctx.rearrange("p g s t -> p (g s t)"), a["mctx"]).then_inc(s["in_mctx"], 16)
            sp.wait_ge(s["sm_done"], HEADS * 2 * NC)
            sp.wait_ge(s["qd_done"], HEADS * 2 * NC)
            sp.dma_start(m8[:, :], a["poolw"]).then_inc(s["in_pw"], 16)
            for g in range(G):
                for half in range(2):
                    unit(a["mlat"][2 * g + half], half, "act_full",
                         T_POOL + 5 * (g - 1) + 3 + 2 * half if g else T_Z + 10 * (half + 1))
            for slot in range(2):
                unit(a["wgb"][slot], slot, "act_full", T_POOL + 5 * (G - 1) + 3 + 2 * slot)
            for slot in range(2):
                unit(a["wout"][slot], slot, "act_full", T_GB + 10 * (slot + 1))
            sp.wait_ge(s["dve_emptied"], D_OUT)
            sp.dma_start(subk, a["subk"]).then_inc(s["in_subk"], 16)
            sp.dma_start(rowbc[:, :], a["fg"]).then_inc(s["in_fg"], 16)
            sp.wait_ge(s["act_emptied"], T_END)
            for c in range(NC):
                sp.dma_start(A[:, c, :], a["x"][c]).then_inc(s["in_xagain"], 16)
            for c in range(NC):
                sp.wait_ge(s["x1_done"], NC + c + 1)
                sp.dma_start(x1d[c], A[:, c, :]).then_inc(s["x1_stored"], 16)
            sp.wait_ge(s["x1_stored"], 16 * NC)
            for k in range(KD):
                sp.dma_start(wq[:, k, :], a["wq"][k]).then_inc(s["in_wq"], 16)

            def phase(p, par, k):
                prep, dots, sums = does(p)
                if prep:
                    if not isinstance(p, int) or p >= 2:
                        sp.wait_ge(s["act_done"], p - 1)
                    sp.dma_start(h2[:, par, :], x1d[p]).then_inc(x1_in[par], 16)
                if sums:
                    sp.wait_ge(s["y_done"], p - 2)
                    sp.dma_start(xo, x1d[p - 2]).then_inc(s["xo_in"], 16)
                    sp.wait_ge(s["y_done"], p - 1)
                    sp.dma_start(a["y"][p - 2], yb).then_inc(s["y_stored"], 16)

            phases(st, phase, 0)
            sp.wait_ge(s["y_stored"], 16 * NC)
            sp.wait_ge(s["state_out"], 16 * 2 * HEADS)

        @block.gpsimd
        def _(pool):
            st = Steps(pool, s["pool_step"], s["pool_gate"])
            g = nc.gpsimd
            st.step(g.memset(ident[:, :], 0.0))
            st.step(g.memset(ones[:, :], 1.0))
            st.step(g.memset(zeros[:, :], 0.0))
            st.step(g.iota(relf, [[1, P]], base=0, channel_multiplier=-1,
                           allow_small_or_imprecise_dtypes=True))
            st.step(g.iota(relb, [[-1, P]], base=0, channel_multiplier=1,
                           allow_small_or_imprecise_dtypes=True))
            st.step(g.iota(rowf, [[1, P]], base=1, channel_multiplier=0,
                           allow_small_or_imprecise_dtypes=True))
            st.step(g.iota(rowb, [[-1, P]], base=P, channel_multiplier=0,
                           allow_small_or_imprecise_dtypes=True))
            st.step(g.iota(colf[:, 0:1], [[0, 1]], base=P - 1, channel_multiplier=-1,
                           allow_small_or_imprecise_dtypes=True))
            st.step(g.iota(colf[:, 1:2], [[0, 1]], base=0, channel_multiplier=1,
                           allow_small_or_imprecise_dtypes=True))
            st.step(g.iota(iota16[:, :], [[1, TOP]], base=0, channel_multiplier=0,
                           allow_small_or_imprecise_dtypes=True))
            st.settle()
            st.step(g.affine_select(out=ident[:, :], in_=ident[:, :], compare_op=ALU.not_equal, fill=1.0,
                                    base=0, pattern=[[-1, P]], channel_multiplier=1))
            st.step(g.tensor_scalar(relf, relf, 0.0, None, ALU.max))
            st.step(g.tensor_scalar(relb, relb, 0.0, None, ALU.max))
            st.settle()
            pool.sem_inc(s["pool_consts"], 1)
            pool.wait_ge(s["exps_done"], 1)
            for h in range(HEADS):
                st.step(g.affine_select(out=mask[:, 0, h, :], in_=mask[:, 0, h, :], compare_op=ALU.is_ge,
                                        fill=0.0, base=0, pattern=[[1, P]], channel_multiplier=-1))
                st.step(g.affine_select(out=mask[:, 1, h, :], in_=mask[:, 1, h, :], compare_op=ALU.is_ge,
                                        fill=0.0, base=0, pattern=[[-1, P]], channel_multiplier=1))
            st.settle()
            pool.sem_inc(s["mask_done"], 1)

            pool.wait_ge(s["dve_full"], D_END)

            def gathers(p, tables):
                n_copies = len(tables)
                with st.loop(PH // 2, 2 * n_copies) as pair:
                    for odd in range(2):
                        for n, (side, chunk, *_) in enumerate(tables):
                            st.step(g.tensor_copy(
                                stage[:, odd, side, :],
                                idx[:, chunk, ds(pair * (2 * TOP) + odd * TOP, TOP)]))
                        st.settle()
                        for j in range(TOP):
                            for side, chunk, table, slot, free, landed in tables:
                                st.wait(free, chunk * P + pair * (2 * TOP) + (odd * TOP + j + 1))
                                g.indirect_dma_start(
                                    out=slot[:, j % SLOTS, :], out_offset=None, in_=table,
                                    in_offset=bass.IndirectOffsetOnAxis(
                                        ap=stage[:, odd, side, j:j + 1], axis=0),
                                ).then_inc(landed[j % SLOTS], 16)

            def phase(p, par, k):
                _, dots, sums = does(p)
                tables = []
                if dots:
                    st.wait(s["idx_done"], (p - 1) * PH + PH)
                    tables.append((0, p - 1, a["peer_u"], uslot, s["u_free"], u_in))
                if sums:
                    tables.append((1, p - 2, a["peer_v"], vslot, s["v_free"], v_in))
                if tables:
                    gathers(p, tables)

            phases(st, phase, 2 * 2 * PH)

        @block.scalar
        def _(eng):
            st = Steps(eng, s["act_step"], s["act_gate"])
            A_ = nc.scalar.activation
            for dst, name in ((cond[:, :], "cond"), (bmod[:, :], "bmod"), (ng[:, :], "ng"),
                              (decay[:, :], "decay"), (rowbc[:, :], "lng"), (mix[:, :], "mix"),
                              (bsp[:, :], "bsp")):
                eng.dma_start(dst, a[name]).then_inc(s["in_const"], 16)
            eng.wait_ge(s["in_const"], 16 * 7)
            A_(scond.rearrange("p k j -> p (k j)"), cond[:, :], ACT.Silu).then_inc(s["silu_done"], 1)

            eng.wait_ge(s["decay_in"], 1)
            A_(lg[:, 1, :], lg[:, 0, :], ACT.Exp, scale=-1.0).then_inc(s["lg_exp"], 1)
            eng.wait_ge(s["lg_u"], 1)
            A_(lg[:, 3, :], lg[:, 2, :], ACT.Ln).then_inc(s["lg_ln"], 1)
            eng.wait_ge(s["lg_done"], 1)
            eng.wait_ge(s["pool_consts"], 1)
            for r in range(2):
                for h in range(HEADS):
                    at = r * HEADS + h
                    col = lg[:, 5, at:at + 1]
                    st.step(A_(mask[:, r, h, :], (relf, relb)[r], ACT.Exp, scale=col))
                    st.step(A_(qdec[:, r, h, :], (rowf, rowb)[r], ACT.Exp, scale=col))
                    st.step(A_(kdec[:, at:at + 1], colf[:, r:r + 1], ACT.Exp, scale=col))
            st.step(A_(gch[:, :], lg[:, 5, :], ACT.Exp, scale=float(P)))
            st.settle()
            eng.sem_inc(s["exps_done"], 1)

            eng.wait_ge(s["in_x"], 16 * NC)
            for c in range(NC):
                st.step(A_(Z[:, c, :], A[:, c, :], ACT.Square, accum_out=ssq[:, c:c + 1]))
            st.settle()
            eng.sem_inc(s["x_squared"], 1)
            eng.wait_ge(s["x_ms"], 1)
            A_(rms[:, 0:NC], rms[:, NC:2 * NC], ACT.Sqrt).then_inc(s["x_std"], 1)

            def full(t):
                st.wait(s["act_full"], t + 1)

            eng.wait_ge(s["mod_done"], 1)
            for k in range(KD):
                for n, (c0, cn, j) in enumerate(SEGS):
                    t = T_HT + 3 * k + n
                    full(t)
                    A_(hT[:, k, c0 * P:(c0 + cn) * P], ps[:, t % 4, 0:cn * P], ACT.Identity,
                       scale=s12[:, 0, k, j:j + 1], bias=mod[:, k, j:j + 1]).then_inc(s["act_emptied"], 1)

            for j in range(2):
                for c in range(NC):
                    t = T_A + j * NC + c
                    full(t)
                    A_(Z[:, c, j * UW:(j + 1) * UW], ps[:, t % 4, :],
                       ACT.Gelu_apprx_tanh).then_inc(s["act_emptied"], 1)
            for j in range(2):
                for c in range(NC):
                    t = T_A + 20 + j * NC + c
                    full(t)
                    A_(A[:, c, j * UW:(j + 1) * UW], ps[:, t % 4, :],
                       ACT.Gelu_apprx_tanh).then_inc(s["act_emptied"], 1)
            eng.wait_ge(s["ln_var"], 1)
            A_(rms[:, 0:NC], rms[:, NC:2 * NC], ACT.Sqrt).then_inc(s["ln_std"], 1)

            def gates(t0, m0, units, func, drain=False):
                for n in range(units * NC):
                    full(t0 + n)
                    if isinstance(m0, int) and m0 + n < 4:
                        pass
                    elif drain and n < 4:
                        st.wait(s["tmp_free"], m0)
                    else:
                        st.wait(s["tmp_free"], m0 + n - 3)
                    bank = (t0 + n) % 4 if isinstance(t0, int) else None
                    A_(tmp[:, n % 4, :], ps[:, bank, :], func).then_inc(s["act_emptied"], 1)

            gates(T_A + 40, TMP_A, 2, ACT.Sigmoid)

            per_scan = NC * 2
            with st.loop(HEADS, 0) as h:
                base = h * HEAD_TILES + T_C
                eng.wait_ge(s["dve_emptied"], D_PW)
                st.wait(s["tmp_free"], h * TMP_HEAD + TMP_C)
                for n in range(6):
                    c0, cn, _ = SEGS[n % 3]
                    full(base + n)
                    if n < 3:
                        A_(qT[:, c0 * P:(c0 + cn) * P], ps[:, n % 4, 0:cn * P],
                           ACT.Copy).then_inc(s["act_emptied"], 1)
                    else:
                        A_(kT[:, c0 * P:(c0 + cn) * P], ps[:, n % 4, 0:cn * P],
                           ACT.Copy, scale=float(DK ** -0.5)).then_inc(s["act_emptied"], 1)
                for n in range(6, 11):
                    c = 2 * (n - 6)
                    full(base + n)
                    A_(vv[:, c:c + 2, :], ps[:, n % 4, :].rearrange("p (c d) -> p c d", c=2),
                       ACT.Copy).then_inc(s["act_emptied"], 1)
                for it in range(NC):
                    for r in range(2):
                        n = h * per_scan + (2 * it + r)
                        st.wait(s["kt_full"], n + 1)
                        if it >= 1:
                            st.wait(s["kv_full"], n - 1)
                        A_(kd[:, r, :], ps[:, r, 0:P], ACT.Copy,
                           scale=kdec[:, ds(h + r * HEADS, 1)]).then_inc(s["kd_done"], 1)
                    for r in range(2):
                        n = h * per_scan + (2 * it + r)
                        c = scan_chunk(it, r)
                        st.wait(s["o_full"], n + 1)
                        A_(O[:, c, r, :], ps[:, 2 + r, 0:DV], ACT.Copy)
                        A_(ps[:, 2 + r, 0:DV], ps[:, 2 + r, 0:DV], ACT.Square,
                           accum_out=ssq[:, 2 * c + r:2 * c + r + 1]).then_inc(s["o_done"], 1)
                st.wait(s["o_ms"], h + 1)
                A_(rms[:, :], rms[:, :], ACT.Sqrt).then_inc(s["o_std"], 1)
                for n in range(15):
                    loc = 11 + n
                    full(base + loc)
                    if n >= 4:
                        st.wait(s["tmp_free"], h * TMP_HEAD + (TMP_C + n - 3))
                    A_(tmp[:, n % 4, :], ps[:, loc % 4, :],
                       ACT.Silu if n < 10 else ACT.Sigmoid).then_inc(s["act_emptied"], 1)

            eng.wait_ge(s["o_ready"], 1)
            eng.wait_ge(s["state_out"], 16 * 2 * HEADS)
            for n in range(20):
                full(T_Z + n)
                A_(Z[:, n % NC, (n // NC) * UW:(n // NC + 1) * UW], ps[:, n % 4, :],
                   ACT.Copy).then_inc(s["act_emptied"], 1)
            for g in range(G):
                for n in range(5):
                    full(T_POOL + 5 * g + n)
                    if n == 0 and g:
                        st.wait(s["dve_full"], D_PW + 5 * g)
                    src = ps[:, (T_POOL + 5 * g + n) % 4, :]
                    if n == 0:
                        dst, src = PT[:, :, 0:CTX], src.rearrange("p (b t) -> p b t", b=2)
                    else:
                        half, b = (n - 1) // 2, (n - 1) % 2
                        dst = PT[:, b, CTX + half * UW:CTX + (half + 1) * UW]
                    A_(dst, src, ACT.Copy).then_inc(s["act_emptied"], 1)
            gates(T_GB, TMP_GB, 2, ACT.Sigmoid, drain=True)

            st.wait(s["tmp_free"], TMP_GB + 20)
            for n in range(16):
                v, j, half = n // 4, (n // 2) % 2, n % 2
                full(T_BC + n)
                dst = gt1[:, j, half * UW:(half + 1) * UW] if v == 0 else \
                    bc[:, v - 1, j, half * UW:(half + 1) * UW]
                A_(dst, ps[:, n % 4, :], ACT.Copy).then_inc(s["act_emptied"], 1)
            for k in range(KD):
                for n, (c0, cn, _) in enumerate(SEGS):
                    t = T_MT + 3 * k + n
                    full(t)
                    A_(hT[:, k, c0 * P:(c0 + cn) * P], ps[:, t % 4, 0:cn * P],
                       ACT.Copy).then_inc(s["act_emptied"], 1)

            eng.sem_inc(s["qp_done"], 1)
            eng.sem_inc(s["qpT_done"], 1)
            eng.wait_ge(s["dve_emptied"], D_END)

            def phase(p, par, k):
                prep, dots, sums = does(p)
                if prep:
                    st.wait(x1_in[par], (k + 1) * 16)
                    st.wait(s["h2_done"], p)
                    for half in range(2):
                        A_(ps[:, 6 + half, :], h2[:, par, half * UW:(half + 1) * UW], ACT.Square,
                           accum_out=one[:, half:half + 1]).then_inc(s["h2_sq"], 1)
                    st.wait(s["h2_ms"], p + 1)
                    A_(one[:, 3:4], one[:, 2:3], ACT.Sqrt).then_inc(s["h2_std"], 1)
                    for half in range(2):
                        st.wait(s["h2_trans"], p * 2 + (half + 1))
                        A_(h2T[:, 4 * half:4 * half + 4, :],
                           ps[:, 6 + half, :].rearrange("p (k t) -> p k t", k=4),
                           ACT.Copy).then_inc(s["h2T_done"], 1)
                if sums:
                    st.wait(s["w_done"], p - 1)

                def diags(hd, j0):
                    for j in range(j0, j0 + 8):
                        st.wait(s["v_free"], (p - 2) * P + hd * TOP + (j + 1))
                        A_(diag[:, j % SLOTS, :], ident[:, :], ACT.Copy,
                           scale=wgt[:, ds(hd * TOP + j, 1)]).then_inc(s["v_diag"], 1)

                if prep or sums:
                    with st.loop(PH, 0) as hd:
                        if sums:
                            diags(hd, 0)
                        if prep:
                            st.wait(s["qp_full"], p * PH + hd + 1)
                            A_(qp, ps[:, 2, 0:256], ACT.Copy).then_inc(s["qp_done"], 1)
                        if sums:
                            diags(hd, 8)
                        if prep:
                            st.wait(s["qpT_full"], p * PH + hd + 1)
                            A_(qpT.rearrange("p s t -> p (s t)"), ps[:, 3, 0:256],
                               ACT.Copy).then_inc(s["qpT_done"], 1)
                if dots:
                    st.wait(s["act_done"], p)
                    A_(gelud, act, ACT.Gelu_apprx_tanh).then_inc(s["gelu_done"], 1)
                if prep:
                    st.wait(s["ls_done"], p + 1)
                    A_(expd, expd, ACT.Exp).then_inc(s["exp_done"], 1)
                if sums:
                    st.wait(s["y_ms"], p - 1)
                    A_(one[:, 7:8], one[:, 6:7], ACT.Sqrt).then_inc(s["y_std"], 1)

            phases(st, phase, 0)

        @block.tensor
        def _(pe):
            st = Steps(pe, s["pe_gate"], s["pe_gate"])
            mm = nc.tensor.matmul

            def group(out, pairs):
                for n, (lhs, rhs) in enumerate(pairs):
                    last = mm(out, lhs, rhs, start=n == 0, stop=n == len(pairs) - 1)
                return last

            def unit_in(slot, pair):
                st.wait(ring_in[slot], (pair + 1) * 16)

            def act_tile(t, n=None, drain=False):
                if isinstance(t, int) and t < 4:
                    return
                st.wait(s["act_emptied"], t if drain else t - 3)

            def dve_tile(t):
                if isinstance(t, int) and t < 4:
                    return
                st.wait(s["dve_emptied"], t - 3)

            def transposed(src, t0):
                for k in range(KD):
                    for n, (c0, cn, _) in enumerate(SEGS):
                        t = t0 + 3 * k + n
                        act_tile(t)
                        for c in range(cn):
                            last = nc.tensor.transpose(ps[:, t % 4, c * P:(c + 1) * P],
                                                       src[:, c0 + c, k * P:(k + 1) * P], ident[:, :])
                        last.then_inc(s["act_full"], 1)

            def project(t0, pair, drain=False, dve=False):
                for slot in range(2):
                    unit_in(slot, pair)
                    for c in range(NC):
                        n = slot * NC + c
                        if dve:
                            dve_tile(t0 + n)
                        elif drain and n < 4:
                            act_tile(t0, drain=True)
                        else:
                            act_tile(t0 + n)
                        last = group(ps[:, (4 if dve else 0) + n % 4, :],
                                     [(hT[:, k, c * P:(c + 1) * P], ring[:, slot, k, :])
                                      for k in range(KD)])
                        last.then_inc(s["dve_full" if dve else "act_full"], 1)

            pe.wait_ge(s["silu_done"], 1)
            for pair in range(6):
                for slot in range(2):
                    t = D_MOD + 2 * pair + slot
                    unit_in(slot, pair)
                    dve_tile(t)
                    for b in range(4):
                        last = group(ps[:, 4 + t % 4, 2 * b:2 * b + 2],
                                     [(ring[:, slot, k, b * P:(b + 1) * P], scond[:, k, :])
                                      for k in range(KD)])
                    last.then_inc(s["dve_full"], 1)
            pe.wait_ge(s["pool_consts"], 1)
            pe.wait_ge(s["x_normed"], 1)
            transposed(A, T_HT)
            pe.wait_ge(s["act_emptied"], T_A)
            with st.loop(3, 0) as i:
                project(i * 20 + T_A, i + 6)
            pe.wait_ge(s["ln_done"], 1)
            for c in range(NC):
                for j in range(2):
                    t = D_MIX + 2 * c + j
                    dve_tile(t)
                    for b in range(2):
                        g = 2 * j + b
                        last = mm(ps[:, 4 + t % 4, b * GW:(b + 1) * GW], mix[:, g * P:(g + 1) * P],
                                  Z[:, c, g * GW:(g + 1) * GW], start=True, stop=True)
                    last.then_inc(s["dve_full"], 1)
            pe.wait_ge(s["dve_emptied"], D_PW)
            with st.loop(HEADS, 0) as h:
                base = h * HEAD_TILES + T_C
                sbase = h * (2 * NC)
                unit_in(0, h + 9)
                for n in range(6):
                    c0, cn, _ = SEGS[n % 3]
                    act_tile(base if n < 4 else base + n, drain=n < 4)
                    group(ps[:, n % 4, 0:cn * P],
                          [(ring[:, 0, k, (n // 3) * P:(n // 3 + 1) * P], hT[:, k, c0 * P:(c0 + cn) * P])
                           for k in range(KD)]).then_inc(s["act_full"], 1)
                for n in range(6, 11):
                    act_tile(base + n)
                    for c in (2 * (n - 6), 2 * (n - 6) + 1):
                        last = group(ps[:, n % 4, (c % 2) * DV:(c % 2 + 1) * DV],
                                     [(hT[:, k, c * P:(c + 1) * P], ring[:, 0, k, 2 * P:4 * P])
                                      for k in range(KD)])
                    last.then_inc(s["act_full"], 1)
                st.wait(s["act_emptied"], base + 11)
                for it in range(NC):
                    for r in range(2):
                        n = sbase + (2 * it + r)
                        c = scan_chunk(it, r)
                        if it >= 1:
                            st.wait(s["kd_done"], n - 1)
                        nc.tensor.transpose(ps[:, r, 0:P], kT[:, c * P:(c + 1) * P],
                                            ident[:, :]).then_inc(s["kt_full"], 1)
                        if it >= 1:
                            st.wait(s["sm_done"], n - 1)
                        mm(ps[:, 4 + r, 0:P], kT[:, c * P:(c + 1) * P], qT[:, c * P:(c + 1) * P],
                           start=True, stop=True).then_inc(s["sc_full"], 1)
                    for r in range(2):
                        n = sbase + (2 * it + r)
                        c = scan_chunk(it, r)
                        seg = 0 if it < CC else 1
                        st.wait(s["sm_done"], n + 1)
                        st.wait(s["qd_done"], n + 1)
                        if it == 0:
                            st.wait(s["s_init"], h + 1)
                        elif it == CC:
                            st.wait(s["in_state"], (h + 1) * 32)
                        if it >= 1:
                            st.wait(s["state_done"], n - 1)
                            st.wait(s["o_done"], n - 1)
                        mm(ps[:, 2 + r, 0:DV], sm[:, r, :], vv[:, c, :], start=True, stop=False)
                        mm(ps[:, 2 + r, 0:DV], qd[:, r, :], S[:, seg, r, it % 2, :],
                           start=False, stop=True).then_inc(s["o_full"], 1)
                        st.wait(s["kd_done"], n + 1)
                        mm(ps[:, 6 + r, 0:DV], kd[:, r, :], vv[:, c, :],
                           start=True, stop=True).then_inc(s["kv_full"], 1)
                st.wait(s["kd_done"], sbase + 2 * NC)
                st.wait(s["o_done"], sbase + 2 * NC)
                st.wait(s["state_done"], sbase + 2 * NC)
                unit_in(1, h + 9)
                for c in range(NC):
                    n = 11 + c
                    if c >= 4:
                        act_tile(base + n)
                    group(ps[:, n % 4, :], [(hT[:, k, c * P:(c + 1) * P], ring[:, 1, k, :])
                                            for k in range(KD)]).then_inc(s["act_full"], 1)
                st.wait(s["in_gc"], (h + 1) * 16)
                for n in range(21, 26):
                    act_tile(base + n)
                    for c in (2 * (n - 21), 2 * (n - 21) + 1):
                        last = group(ps[:, n % 4, (c % 2) * DV:(c % 2 + 1) * DV],
                                     [(hT[:, k, c * P:(c + 1) * P], gcb[:, k, :]) for k in range(KD)])
                    last.then_inc(s["act_full"], 1)
            project(T_Z, 13, drain=True)
            pe.wait_ge(s["act_emptied"], T_POOL)
            pe.wait_ge(s["in_mctx"], 16)
            pe.wait_ge(s["in_pw"], 16)
            pe.wait_ge(s["state_done"], HEADS * 2 * NC)
            for g in range(G):
                t = T_POOL + 5 * g
                act_tile(t)
                for b in range(2):
                    ch = slice(g * GW + b * P, g * GW + (b + 1) * P)
                    last = group(ps[:, t % 4, b * CTX:(b + 1) * CTX],
                                 [(Z[:, c, ch], mctx[:, g, c, :]) for c in range(CC)])
                last.then_inc(s["act_full"], 1)
                for half in range(2):
                    unit_in(half, U_POOL // 2 + g)
                    for b in range(2):
                        t = T_POOL + 5 * g + 1 + 2 * half + b
                        ch = slice(g * GW + b * P, g * GW + (b + 1) * P)
                        act_tile(t)
                        group(ps[:, t % 4, :],
                              [(Z[:, CC + c, ch], ring[:, half, c, :]) for c in pool_sources(g, half)]
                              ).then_inc(s["act_full"], 1)
                pe.wait_ge(s["act_emptied"], T_POOL + 5 * g + 5)
                for n in range(5):
                    t = D_PW + 5 * g + n
                    dve_tile(t)
                    for c in (2 * n, 2 * n + 1):
                        last = group(ps[:, 4 + t % 4, (c % 2) * GW:(c % 2 + 1) * GW],
                                     [(PT[:, b, c * P:(c + 1) * P], pw[:, g, b, :]) for b in range(2)])
                    last.then_inc(s["dve_full"], 1)
            project(T_GB, U_GB // 2)
            for n in range(16):
                act_tile(T_BC + n)
                pe.wait_ge(s["row_diag"], n + 1)
                mm(ps[:, n % 4, :], ones[:, :], tmp[:, n % 4, :], start=True,
                   stop=True).then_inc(s["act_full"], 1)
            pe.wait_ge(s["merged"], 1)
            transposed(A, T_MT)
            pe.wait_ge(s["act_emptied"], T_END)
            project(D_OUT, U_OUT // 2, dve=True)

            pe.sem_inc(s["v_free"], SLOTS)
            pe.wait_ge(s["in_wq"], 16 * KD)
            pe.wait_ge(s["in_subk"], 16)
            pe.wait_ge(s["dve_emptied"], D_END)

            def phase(p, par, k):
                prep, dots, sums = does(p)
                if sums:
                    st.wait(s["vacc_free"], p - 2)
                    for half in range(2):
                        mm(ps[:, half, :], ident[:, :], zeros[:, :], start=True, stop=False)
                if prep:
                    st.wait(s["h2_done"], p + 1)
                    st.wait(s["h2T_done"], p * 2)
                    for k in range(KD):
                        last = nc.tensor.transpose(ps[:, 6 + k // 4, (k % 4) * P:(k % 4 + 1) * P],
                                                   h2[:, par, k * P:(k + 1) * P], ident[:, :])
                        if k % 4 == 3:
                            last.then_inc(s["h2_trans"], 1)
                    st.wait(s["h2T_done"], p * 2 + 2)

                def sum_rows(hd, j0):
                    for j in range(j0, j0 + 8):
                        st.wait(v_in[j % SLOTS], ((p - 2) * (P // SLOTS) + hd * 2 + (j // SLOTS + 1)) * 16)
                        st.wait(s["v_diag"], (p - 2) * P + hd * TOP + (j + 1))
                        for half in range(2):
                            last = mm(ps[:, half, :], diag[:, j % SLOTS, :],
                                      vslot[:, j % SLOTS, half * UW:(half + 1) * UW],
                                      start=False, stop=False)
                        last.then_inc(s["v_free"], 1)

                if prep or sums:
                    with st.loop(PH // 2, 0) as pair:
                        for odd in range(2):
                            hd = pair * 2 + odd
                            n = p * PH + hd
                            if prep:
                                st.wait(s["qp_done"], n + 1)
                                group(ps[:, 2, 0:256], [(h2T[:, k, :], wq[:, k, ds(hd * 256, 256)])
                                                        for k in range(KD)]).then_inc(s["qp_full"], 1)
                            if sums:
                                sum_rows(hd, 0)
                            if prep:
                                st.wait(s["qp_done"], n + 2)
                                st.wait(s["qpT_done"], n + 1)
                                for side in range(2):
                                    last = nc.tensor.transpose(ps[:, 3, side * P:(side + 1) * P],
                                                               qp[:, side * P:(side + 1) * P], ident[:, :])
                                last.then_inc(s["qpT_full"], 1)
                            if sums:
                                sum_rows(hd, 8)
                            if prep:
                                st.wait(s["qpT_done"], n + 2)
                                st.wait(s["sc2_free"], n + 1)
                                for side in range(2):
                                    last = mm(ps[:, 4 + odd, side * NK:(side + 1) * NK], qpT[:, side, :],
                                              subk[:, ds(hd * 256 + side * NK, NK)], start=True, stop=True)
                                last.then_inc(s["sc2_full"], 1)
                if sums:
                    for half in range(2):
                        last = mm(ps[:, half, :], ident[:, :], zeros[:, :], start=False, stop=True)
                    last.then_inc(s["vacc_full"], 1)

            phases(st, phase, 0)

        @block.vector
        def _(dve):
            st = Steps(dve, s["dve_step"], s["dve_gate"])
            v = nc.vector

            def full(t):
                st.wait(s["dve_full"], t + 1)

            dve.wait_ge(s["in_const"], 16 * 7)
            st.link(v.tensor_scalar(lg[:, 4, :], decay[:, :], -1.0, None, ALU.mult))
            st.link(v.tensor_tensor(lg[:, 0, :], lg[:, 4, :], decay[:, :], ALU.max))
            dve.sem_inc(s["decay_in"], 1)
            dve.wait_ge(s["lg_exp"], 1)
            st.link(v.tensor_scalar(lg[:, 2, :], lg[:, 1, :], 1.0, None, ALU.add))
            dve.sem_inc(s["lg_u"], 1)
            st.link(v.tensor_scalar(lg[:, 4, :], lg[:, 2, :], 1.0, None, ALU.subtract))
            st.link(v.tensor_tensor(lg[:, 4, :], lg[:, 1, :], lg[:, 4, :], ALU.subtract))
            st.link(v.reciprocal(lg[:, 0, :], lg[:, 2, :]))
            st.link(v.tensor_tensor(lg[:, 4, :], lg[:, 4, :], lg[:, 0, :], ALU.mult))
            dve.wait_ge(s["lg_ln"], 1)
            st.link(v.tensor_tensor(lg[:, 4, :], lg[:, 4, :], lg[:, 3, :], ALU.add))
            st.link(v.tensor_scalar(lg[:, 0, :], decay[:, :], 0.0, None, ALU.min))
            st.link(v.tensor_tensor(lg[:, 5, :], lg[:, 0, :], lg[:, 4, :], ALU.subtract))
            dve.sem_inc(s["lg_done"], 1)

            dve.wait_ge(s["x_squared"], 1)
            v.tensor_scalar(rms[:, NC:2 * NC], ssq[:, 0:NC], 1.0 / D, EPS, ALU.mult,
                            ALU.add).then_inc(s["x_ms"], 1)
            dve.wait_ge(s["x_std"], 1)
            st.link(v.reciprocal(rst[:, 0:NC], rms[:, 0:NC]))
            for c in range(NC):
                st.step(v.tensor_scalar(A[:, c, :], A[:, c, :], rst[:, c:c + 1], None, ALU.mult))
            st.settle()
            dve.sem_inc(s["x_normed"], 1)

            for t in range(12):
                full(D_MOD + t)
                v.tensor_tensor(mod[:, 4 * t:4 * t + 4, :],
                                ps[:, 4 + t % 4, 0:8].rearrange("p (b j) -> p b j", b=4),
                                bmod[:, 4 * t:4 * t + 4].unsqueeze(2).to_broadcast([P, 4, 2]),
                                ALU.add).then_inc(s["dve_emptied"], 1)
            dve.wait_ge(s["dve_emptied"], 12)
            for n in range(2):
                st.step(v.scalar_tensor_tensor(
                    out=s12[:, n], in0=mod[:, 8 + 24 * n:16 + 24 * n, :], scalar=1.0,
                    in1=ng[:, 8 * n:8 * n + 8].unsqueeze(2).to_broadcast([P, KD, 2]),
                    op0=ALU.add, op1=ALU.mult))
            st.settle()
            dve.sem_inc(s["mod_done"], 1)

            for j in range(2):
                for c in range(NC):
                    dve.wait_ge(s["act_emptied"], T_A + j * NC + c + 1)
                    st.step(v.bn_stats(bst[:, c, 6 * j:6 * j + 6], Z[:, c, j * UW:(j + 1) * UW]))
            st.settle()
            for c in range(NC):
                st.step(v.bn_aggr(mv[:, c, :], bst[:, c, :]))
            st.settle()
            v.tensor_scalar(rms[:, NC:2 * NC], mv[:, :, 1], EPS, None, ALU.add).then_inc(s["ln_var"], 1)
            dve.wait_ge(s["ln_std"], 1)
            st.link(v.reciprocal(rst[:, 0:NC], rms[:, 0:NC]))
            for c in range(NC):
                st.step(v.tensor_scalar(Z[:, c, :], Z[:, c, :], mv[:, c, 0:1], rst[:, c:c + 1],
                                        ALU.subtract, ALU.mult))
            st.settle()
            for c in range(NC):
                st.step(v.tensor_tensor(Z[:, c, :], Z[:, c, :], rowbc[:, :], ALU.mult))
            st.settle()
            dve.sem_inc(s["ln_done"], 1)
            for n in range(20):
                j, c = n // NC, n % NC
                dve.wait_ge(s["act_emptied"], T_A + 40 + n + 1)
                dst = A[:, c, j * UW:(j + 1) * UW]
                v.tensor_tensor(dst, dst, tmp[:, n % 4, :], ALU.mult).then_inc(s["tmp_free"], 1)
            dve.wait_ge(s["tmp_free"], 20)
            for c in range(NC):
                for j in range(2):
                    t = D_MIX + 2 * c + j
                    full(t)
                    for b in range(2):
                        g = 2 * j + b
                        dst = A[:, c, g * GW:(g + 1) * GW]
                        last = v.scalar_tensor_tensor(out=dst, in0=ps[:, 4 + t % 4, b * GW:(b + 1) * GW],
                                                      scalar=bsp[:, g:g + 1], in1=dst,
                                                      op0=ALU.add, op1=ALU.mult)
                    last.then_inc(s["dve_emptied"], 1)

            dve.wait_ge(s["dve_emptied"], D_PW)
            dve.wait_ge(s["mask_done"], 1)
            with st.loop(HEADS, 1 + NC + NC // 2) as h:
                base = h * HEAD_TILES + T_C
                sbase = h * (2 * NC)
                for r in range(2):
                    last = v.memset(S[:, 0, r, 0, :], 0.0)
                last.then_inc(s["s_init"], 1)
                st.wait(s["act_emptied"], base + 6)
                for it in range(NC):
                    for r in range(2):
                        n = sbase + (2 * it + r)
                        c = scan_chunk(it, r)
                        if it >= 1:
                            st.wait(s["o_full"], n - 1)
                        at = ds(h + r * HEADS, 1)
                        v.tensor_tensor(qd[:, r, :], qT[:, c * P:(c + 1) * P],
                                        m8[:, ds(h * P + (D + r * HEADS * P), P)],
                                        ALU.mult).then_inc(s["qd_done"], 1)
                        st.wait(s["sc_full"], n + 1)
                        v.tensor_tensor(sm[:, r, :], ps[:, 4 + r, 0:P],
                                        m8[:, ds(h * P + r * HEADS * P, P)],
                                        ALU.mult).then_inc(s["sm_done"], 1)
                    for r in range(2):
                        n = sbase + (2 * it + r)
                        seg = 0 if it < CC else 1
                        st.wait(s["kv_full"], n + 1)
                        if it == 0:
                            st.wait(s["s_init"], h + 1)
                        elif it == CC:
                            st.wait(s["in_state"], (h + 1) * 32)
                        else:
                            st.wait(s["state_done"], n - 1)
                        v.scalar_tensor_tensor(out=S[:, seg, r, (it + 1) % 2, :],
                                               in0=S[:, seg, r, it % 2, :],
                                               scalar=gch[:, ds(h + r * HEADS, 1)],
                                               in1=ps[:, 6 + r, 0:DV], op0=ALU.mult,
                                               op1=ALU.add).then_inc(s["state_done"], 1)
                st.wait(s["o_done"], sbase + 2 * NC)
                v.tensor_scalar(rms[:, :], ssq[:, :], 1.0 / DV, EPS, ALU.mult,
                                ALU.add).then_inc(s["o_ms"], 1)
                st.wait(s["o_std"], h + 1)
                st.link(v.reciprocal(rst[:, :], rms[:, :]))
                for c in range(NC):
                    st.wait(s["act_emptied"], base + (11 + c + 1))
                    for r in range(2):
                        last = v.scalar_tensor_tensor(
                            out=O[:, c, r, :], in0=O[:, c, r, :], scalar=rst[:, 2 * c + r:2 * c + r + 1],
                            in1=tmp[:, c % 4, r * DV:(r + 1) * DV], op0=ALU.mult, op1=ALU.mult)
                    last.then_inc(s["tmp_free"], 1)
                    st.wait(s["tmp_free"], h * TMP_HEAD + (TMP_C + c + 1))
                    st.step(v.tensor_tensor(O[:, c, 0, :], O[:, c, 0, :], O[:, c, 1, :], ALU.add))
                st.settle()
                for n in range(5):
                    c = 2 * n
                    slot = (10 + n) % 4
                    st.wait(s["act_emptied"], base + (21 + n + 1))
                    dst = A[:, c:c + 2, ds(h * DV, DV)]
                    gate = tmp[:, slot, :].rearrange("p (c d) -> p c d", c=2)
                    v.tensor_tensor(O[:, c:c + 2, 0, :], O[:, c:c + 2, 0, :], gate,
                                    ALU.mult).then_inc(s["tmp_free"], 1)
                    st.wait(s["tmp_free"], h * TMP_HEAD + (TMP_C + 10 + n + 1))
                    st.step(v.tensor_tensor(dst, dst, O[:, c:c + 2, 0, :], ALU.add))
                st.wait(s["state_out"], h * 32 + 32)
            st.settle()
            dve.sem_inc(s["o_ready"], 1)

            dve.wait_ge(s["in_psc"], 16)
            for g in range(G):
                for n in range(5):
                    t = D_PW + 5 * g + n
                    full(t)
                    scale = rowbc[:, g * GW:(g + 1) * GW].unsqueeze(1).to_broadcast([P, 2, GW])
                    v.tensor_tensor(Z[:, 2 * n:2 * n + 2, g * GW:(g + 1) * GW],
                                    ps[:, 4 + t % 4, :].rearrange("p (c d) -> p c d", c=2),
                                    scale, ALU.mult).then_inc(s["dve_emptied"], 1)
            dve.wait_ge(s["dve_emptied"], D_OUT)
            for n in range(20):
                j, c = n // NC, n % NC
                dve.wait_ge(s["act_emptied"], T_GB + n + 1)
                gate, dst = tmp[:, n % 4, :], A[:, c, j * UW:(j + 1) * UW]
                st.link(v.tensor_tensor(gate, gate, Z[:, c, j * UW:(j + 1) * UW], ALU.mult))
                v.tensor_tensor(dst, dst, gate, ALU.add).then_inc(s["tmp_free"], 1)
            dve.wait_ge(s["tmp_free"], TMP_GB + 20)
            dve.sem_inc(s["merged"], 1)

            for n in range(16):
                vec, j, half = n // 4, (n // 2) % 2, n % 2
                b0 = 4 * half
                src = (mod[:, 16 + b0:20 + b0, j], s12[:, 1, b0:b0 + 4, j],
                       mod[:, 24 + b0:28 + b0, j], mod[:, 40 + b0:44 + b0, j])[vec]
                if n >= 4:
                    dve.wait_ge(s["act_full"], T_BC + n - 3)
                v.tensor_tensor(tmp[:, n % 4, :].rearrange("p (b n) -> p b n", b=4),
                                ident[:, :].unsqueeze(1).to_broadcast([P, 4, P]),
                                src.unsqueeze(2).to_broadcast([P, 4, P]),
                                ALU.mult).then_inc(s["row_diag"], 1)

            dve.wait_ge(s["in_xagain"], 16 * NC)
            dve.wait_ge(s["act_emptied"], T_END)
            for n in range(20):
                j, c = n // NC, n % NC
                full(D_OUT + n)
                if n >= 4:
                    dve.wait_ge(s["x1_done"], n - 3)
                slot, dst = tmp[:, n % 4, :], A[:, c, j * UW:(j + 1) * UW]
                v.tensor_tensor(slot, ps[:, 4 + n % 4, :],
                                gt1[:, 0 if c < CC else 1, j * UW:(j + 1) * UW],
                                ALU.mult).then_inc(s["dve_emptied"], 1)
                dve.wait_ge(s["dve_emptied"], D_OUT + n + 1)
                v.tensor_tensor(dst, dst, slot, ALU.add).then_inc(s["x1_done"], 1)

            dve.sem_inc(s["u_free"], SLOTS)
            dve.sem_inc(s["sc2_free"], 2)
            dve.wait_ge(s["in_fg"], 16)

            def top16(values, spare, out_v, out_i):
                st.link(v.max(out_v[:, 0:8], values))
                st.step(v.max_index(out_i[:, 0:8], out_v[:, 0:8], values))
                st.link(v.match_replace(spare, out_v[:, 0:8], values, LOWEST))
                st.link(v.max(out_v[:, 8:16], spare))
                st.link(v.max_index(out_i[:, 8:16], out_v[:, 8:16], spare))

            def dots_of(p, par, hd):
                for j in range(TOP):
                    st.wait(u_in[j % SLOTS], ((p - 1) * (P // SLOTS) + hd * 2 + (j // SLOTS + 1)) * 16)
                    row = uslot[:, j % SLOTS, :]
                    v.tensor_tensor_reduce(out=row, in0=row, in1=h2[:, 1 - par, :], scale=1.0, scalar=0.0,
                                           op0=ALU.mult, op1=ALU.add,
                                           accum_out=act16[:, j:j + 1]).then_inc(s["u_free"], 1)
                st.wait(s["u_free"], (p - 1) * P + hd * TOP + (SLOTS + TOP))
                st.link(v.tensor_copy(act[:, ds(hd * TOP, TOP)], act16[:, :]))

            def experts_of(p, hd, odd):
                n = p * PH + hd
                st.wait(s["sc2_full"], n + 1)
                for side in range(2):
                    top16(ps[:, 4 + odd, side * NK:(side + 1) * NK], rest, tv[:, side, :],
                          ti[:, side, :])
                dve.sem_inc(s["sc2_free"], 1)
                st.step(v.tensor_copy(tf[:, :, :], ti[:, :, :]))
                st.link(v.tensor_tensor(cand, tv[:, 0, :].unsqueeze(2).to_broadcast([P, TOP, TOP]),
                                        tv[:, 1, :].unsqueeze(1).to_broadcast([P, TOP, TOP]), ALU.add))
                flat = cand.rearrange("p a b -> p (a b)")
                top16(flat, cand2, bv[:, :], bp[:, :])
                st.step(v.tensor_copy(logit[:, ds(hd * TOP, TOP)], bv[:, :]))
                st.step(v.tensor_scalar(ab[:, 0, :], bp[:, :], 4, None, ALU.logical_shift_right))
                st.link(v.tensor_scalar(ab[:, 1, :], bp[:, :], 15, None, ALU.bitwise_and))
                st.link(v.tensor_copy(abf[:, :, :], ab[:, :, :]))
                st.link(v.tensor_tensor(hot, abf[:, :, :].unsqueeze(3).to_broadcast([P, 2, TOP, TOP]),
                                        iota16[:, :].unsqueeze(1).unsqueeze(1).to_broadcast(
                                            [P, 2, TOP, TOP]), ALU.is_equal))
                st.link(v.tensor_tensor(hot, hot, tf[:, :, :].unsqueeze(2).to_broadcast([P, 2, TOP, TOP]),
                                        ALU.mult))
                st.link(v.tensor_reduce(picked[:, :, :], hot, AX.X, ALU.add))
                v.scalar_tensor_tensor(out=idx[:, p, ds(hd * TOP, TOP)], in0=picked[:, 0, :],
                                       scalar=float(NK), in1=picked[:, 1, :], op0=ALU.mult,
                                       op1=ALU.add).then_inc(s["idx_done"], 1)
                st.wait(s["idx_done"], n + 1)

            OWN_PREP_FRONT, OWN_HEAD_PREP, OWN_HEAD_DOTS = 4, 3 * 5 + 2 + 1 + 2 + 1 + 3, 1

            def phase(p, par, k):
                prep, dots, sums = does(p)
                j = 1 if not isinstance(p, int) else (0 if p < CC else 1)
                if prep:
                    st.wait(s["h2_sq"], p * 2 + 2)
                    st.link(v.tensor_tensor(one[:, 8:9], one[:, 0:1], one[:, 1:2], ALU.add))
                    v.tensor_scalar(one[:, 2:3], one[:, 8:9], 1.0 / D, EPS, ALU.mult,
                                    ALU.add).then_inc(s["h2_ms"], 1)
                    st.wait(s["h2_std"], p + 1)
                    st.link(v.reciprocal(one[:, 9:10], one[:, 3:4]))
                    st.link(v.scalar_tensor_tensor(out=h2[:, par, :], in0=h2[:, par, :],
                                                   scalar=one[:, 9:10], in1=bc[:, 0, j, :],
                                                   op0=ALU.mult, op1=ALU.mult))
                    v.tensor_tensor(h2[:, par, :], h2[:, par, :], bc[:, 1, j, :],
                                    ALU.add).then_inc(s["h2_done"], 1)
                    st.wait(s["h2_done"], p + 1)
                if prep or dots:
                    with st.loop(PH // 2, 2 * (HEAD_PREP * prep + 1 * dots)) as pair:
                        for odd in range(2):
                            hd = pair * 2 + odd
                            if dots:
                                dots_of(p, par, hd)
                            if prep:
                                experts_of(p, hd, odd)
                if dots:
                    dve.sem_inc(s["act_done"], 1)
                if prep:
                    lv = logit.rearrange("p (h k) -> p h k", h=PH)
                    v.tensor_tensor(expd.rearrange("p (h k) -> p h k", h=PH), lv,
                                    lv[:, :, 0:1].to_broadcast([P, PH, TOP]),
                                    ALU.subtract).then_inc(s["ls_done"], 1)
                if sums:
                    jo = 1 if not isinstance(p, int) else (0 if p - 2 < CC else 1)
                    st.wait(s["y_stored"], (p - 2) * 16)
                    st.wait(s["vacc_full"], p - 1)
                    st.link(v.tensor_tensor(yb, ps[:, 0:2, :].rearrange("p b n -> p (b n)"),
                                            bc[:, 2, jo, :], ALU.mult))
                    dve.sem_inc(s["vacc_free"], 1)
                if dots:
                    if sums:
                        st.wait(s["v_diag"], (p - 1) * P)
                    st.wait(s["gelu_done"], p)
                    v.tensor_tensor(wgt, gsm, gelud, ALU.mult).then_inc(s["w_done"], 1)
                    st.wait(s["w_done"], p)
                if prep:
                    ev = expd.rearrange("p (h k) -> p h k", h=PH)
                    st.wait(s["exp_done"], p + 1)
                    st.link(v.tensor_reduce(rsum[:, 0, :], ev, AX.X, ALU.add))
                    st.link(v.reciprocal(rsum[:, 1, :], rsum[:, 0, :]))
                    st.link(v.tensor_tensor(gsm.rearrange("p (h k) -> p h k", h=PH), ev,
                                            rsum[:, 1, :].unsqueeze(2).to_broadcast([P, PH, TOP]),
                                            ALU.mult))
                if sums:
                    st.wait(s["xo_in"], (p - 1) * 16)
                    st.link(v.tensor_tensor(yb, yb, xo, ALU.add))
                    st.link(v.tensor_tensor_reduce(out=xo, in0=yb, in1=yb, scale=1.0, scalar=0.0,
                                                   op0=ALU.mult, op1=ALU.add, accum_out=one[:, 4:5]))
                    v.tensor_scalar(one[:, 6:7], one[:, 4:5], 1.0 / D, EPS, ALU.mult,
                                    ALU.add).then_inc(s["y_ms"], 1)
                    st.wait(s["y_std"], p - 1)
                    st.link(v.reciprocal(one[:, 5:6], one[:, 7:8]))
                    v.scalar_tensor_tensor(out=yb, in0=yb, scalar=one[:, 5:6], in1=rowbc[:, :],
                                           op0=ALU.mult, op1=ALU.mult).then_inc(s["y_done"], 1)
                    st.wait(s["y_done"], p - 1)

            HEAD_PREP = 3 * 5 + 2 + 1 + 2 + 1 + 3
            per_phase = 3 + PH * (HEAD_PREP + 1) + 1 + 3 + 3
            phases(st, phase, 2 * per_phase)


def scan_chunk(it, r):
    if it < CC:
        return it if r == 0 else CC - 1 - it
    return it if r == 0 else NC - 1 + CC - it


def units_of(w):
    n = w.shape[1] // UW
    return np.ascontiguousarray(w.reshape(KD, P, n, UW).transpose(2, 1, 0, 3)).reshape(n, P, KD * UW)


def columns_of(x):
    x = x.reshape(-1, x.shape[-1] // P, P)
    return np.ascontiguousarray(x.transpose(2, 0, 1)).reshape(P, -1)


def spread(x):
    return np.ascontiguousarray(np.broadcast_to(x.reshape(1, -1), (P, x.size)))


def kernel(x_prompt, x_sample, state_ret, c, c_ctx, w_mod, b_mod, norm_g, w_in, w_out,
           gmlp_ws, gmlp_b, gmlp_ln_g, pool_w, pool_scale, ret_decay, peer_wq, peer_subkeys,
           peer_u, peer_v, final_norm_g):
    import concourse.bacc as bacc
    from concourse.bass_utils import run_bass_kernel_spmd

    arr = np.asarray
    w = arr(w_in)[0]
    u0, v0, z0, q0, k0, rv0, rf0, rb0, gm0 = (0, 1024, 2048, 3072, 3584, 4096, 5120, 6144, 7168)
    wa = np.concatenate([w[:, v0:v0 + D], w[:, u0:u0 + D], w[:, gm0:gm0 + D]], axis=1)
    heads, gcs = [], []
    for h in range(HEADS):
        heads += [w[:, q0 + h * DK:q0 + (h + 1) * DK], w[:, k0 + h * DK:k0 + (h + 1) * DK],
                  w[:, rv0 + h * DV:rv0 + (h + 1) * DV], w[:, rf0 + h * DV:rf0 + (h + 1) * DV],
                  w[:, rb0 + h * DV:rb0 + (h + 1) * DV]]
        at = gm0 + 2 * D + h * DV
        gcs.append(w[:, at:at + DV].reshape(KD, P, DV).transpose(1, 0, 2).reshape(P, KD * DV))
    mlat, mctx = pool_constants()
    x = np.concatenate([arr(x_prompt).reshape(CTX, D), arr(x_sample).reshape(LAT, D)])
    conds = np.stack([arr(c_ctx).reshape(D), arr(c).reshape(D)])
    host = {
        "x": x.reshape(NC, P, D),
        "cond": np.ascontiguousarray(conds.reshape(2, KD, P).transpose(2, 1, 0)).reshape(P, KD * 2),
        "wmod": units_of(arr(w_mod)[0]),
        "bmod": columns_of(arr(b_mod)[0]),
        "ng": columns_of(arr(norm_g)[0]),
        "decay": spread(arr(ret_decay)[0]),
        "lng": spread(arr(gmlp_ln_g)[0]),
        "mix": np.ascontiguousarray(arr(gmlp_ws)[0].transpose(2, 0, 1)).reshape(P, G * P),
        "bsp": np.ascontiguousarray(arr(gmlp_b)[0].T),
        "wa": units_of(wa),
        "whead": units_of(np.concatenate(heads, axis=1)),
        "wgc": np.ascontiguousarray(np.stack(gcs)),
        "state": arr(state_ret)[0, 0],
        "wz": units_of(w[:, z0:z0 + D]),
        "mctx": mctx,
        "mlat": mlat,
        "poolw": np.ascontiguousarray(arr(pool_w)[0].reshape(G, 2, P, GW).transpose(2, 0, 1, 3)
                                      ).reshape(P, G * 2 * GW),
        "psc": spread(arr(pool_scale)[0]),
        "wgb": units_of(w[:, gm0 + D:gm0 + 2 * D]),
        "wout": units_of(arr(w_out)[0]),
        "subk": np.ascontiguousarray(arr(peer_subkeys)[0].transpose(3, 0, 1, 2)).reshape(P, 2 * PH * NK),
        "fg": spread(arr(final_norm_g)),
        "wq": arr(peer_wq)[0].reshape(KD, P, 2 * D),
        "peer_u": arr(peer_u)[0],
        "peer_v": arr(peer_v)[0],
    }
    nc = bacc.Bacc("TRN2", target_bir_lowering=False, num_devices=1)
    a = {}
    for name, value in host.items():
        host[name] = np.ascontiguousarray(value)
        a[name] = nc.dram_tensor(f"in_{name}", value.shape, F32, kind="ExternalInput").ap()
    a["y"] = nc.dram_tensor("out_y", [NC, P, D], F32, kind="ExternalOutput").ap()
    a["new_state"] = nc.dram_tensor("out_state", [2, HEADS, DK, DV], F32, kind="ExternalOutput").ap()
    build(nc, a)
    r = run_bass_kernel_spmd(nc, [{f"in_{n}": v for n, v in host.items()}], core_ids=[0])
    y = r.results[0]["out_y"].reshape(T, D)
    new_state = r.results[0]["out_state"].reshape(1, 1, 2, HEADS, DK, DV)
    return (np.ascontiguousarray(y[:CTX]).reshape(1, CTX, D),
            np.ascontiguousarray(y[CTX:]).reshape(1, LAT, D), new_state)
```

```python
from contextlib import ExitStack, contextmanager

import numpy as np

import concourse.bass as bass
from concourse import mybir

ALU = mybir.AluOpType
ACT = mybir.ActivationFunctionType
AX = mybir.AxisListType
F32 = mybir.dt.float32
U32 = mybir.dt.uint32
ds = bass.ds

P = 128
D = 1024
KD = D // P
CTX = 256
LAT = 1024
T = CTX + LAT
NC = T // P
CC = CTX // P
EPS = 1e-6
GRID_W = 64
WINDOWS = (2, 4, 8, 16)
G = len(WINDOWS)
GW = D // G
HEADS = 4
DK = 128
DV = 256
PH = 8
NK = 128
TOP = 16
SLOTS = 8
UW = 512
LOWEST = -3.0e38

U_MOD, U_A, U_HEAD, U_Z, U_POOL, U_GB, U_OUT = 0, 2, 8, 16, 18, 26, 28

T_HT = 0
T_A = T_HT + 24
T_C = T_A + 60
HEAD_TILES = 26
T_Z = T_C + HEADS * HEAD_TILES
T_POOL = T_Z + 20
T_GB = T_POOL + 20
T_BC = T_GB + 20
T_MT = T_BC + 16
T_END = T_MT + 24
D_MOD = 0
D_LATE = D_MOD + 4
D_MIX = D_LATE + 16
D_PW = D_MIX + 20
D_OUT = D_PW + 20
D_END = D_OUT + 20
TMP_A = 0
TMP_C = TMP_A + 20
TMP_HEAD = 15
TMP_GB = TMP_C + HEADS * TMP_HEAD

LATE_AFTER = (1, 3, 5, 7)
SEGS = ((0, 2, 0), (2, 4, 1), (6, 4, 1))


def box_matrix(n, w):
    a, b = w // 2, w - 1 - w // 2
    at = np.arange(n)
    return ((at[:, None] >= at[None, :] - a) & (at[:, None] <= at[None, :] + b)).astype(np.float64)


def pool_constants():
    rows = LAT // GRID_W
    lat = np.zeros((G, 2, P, LAT // P, UW), np.float32)
    ctx = np.zeros((P, G, CC, CTX), np.float32)
    for g, w in enumerate(WINDOWS):
        r, c = box_matrix(rows, w), box_matrix(GRID_W, w)
        m = np.kron(r / r.sum(0), c / c.sum(0)) - np.eye(LAT)
        lat[g] = m.reshape(LAT // P, P, 2, UW).transpose(2, 1, 0, 3)
        m = box_matrix(CTX, w)
        m = m / m.sum(0) - np.eye(CTX)
        ctx[:, g] = m.reshape(CC, P, CTX).transpose(1, 0, 2)
    return lat.reshape(2 * G, P, KD * UW), ctx.reshape(P, G * CC * CTX)


def pool_sources(g, half):
    w = WINDOWS[g]
    a, b = w // 2, w - 1 - w // 2
    rows = LAT // GRID_W
    first, last = half * rows // 2 - a, (half + 1) * rows // 2 - 1 + b
    return range(max(first, 0) // 2, min(last, rows - 1) // 2 + 1)


class Steps:

    def __init__(self, eng, sem, gate):
        self.eng, self.sem, self.gate, self.base, self.n = eng, sem, gate, 0, 0

    def wait(self, sem, value):
        if isinstance(value, int):
            if value > 0:
                self.eng.wait_ge(sem, value)
        else:
            self.eng.wait_ge(sem, value)
            self.eng.sem_inc(self.gate, 1)

    def step(self, ins):
        self.n += 1
        return ins.then_inc(self.sem, 1)

    def settle(self):
        self.wait(self.sem, self.base + self.n)

    def link(self, ins):
        self.step(ins)
        self.settle()

    @contextmanager
    def loop(self, trips, per_trip):
        base, n = self.base, self.n
        with self.eng.Fori(0, trips) as i:
            if per_trip:
                self.base = base + i * per_trip
            yield i
            assert self.n - n == per_trip, (self.n - n, per_trip)
        self.base, self.n = base, n + per_trip * trips


def build(nc, a):
    with ExitStack() as ctx:
        def sb(name, shape, dt=F32):
            return ctx.enter_context(nc.sbuf_tensor(name, shape, dt))

        def sem(name):
            return ctx.enter_context(nc.semaphore(name))

        HT0, RING0, GC0, A0, R0, AEND = 0, 10240, 18432, 20480, 30720, 43776
        arena = sb("arena", [P, AEND])

        def view(at, n, text=None, **kw):
            v = arena[:, at:at + n]
            return v.rearrange(text, **kw) if text else v

        hT = view(HT0, KD * T, "p (k t) -> p k t", k=KD)
        ring = view(RING0, 2 * KD * UW, "p (s k n) -> p s k n", s=2, k=KD)
        gcb = view(GC0, KD * DV, "p (k n) -> p k n", k=KD)
        late_mod = view(GC0, KD * UW // 2, "p (k n) -> p k n", k=KD)
        mctx = view(GC0, G * CC * CTX, "p (g s t) -> p g s t", g=G, s=CC)
        A = view(A0, NC * D, "p (c d) -> p c d", c=NC)
        Z = view(R0, NC * D, "p (c d) -> p c d", c=NC)
        PT = view(R0 + NC * D, 2 * T, "p (b t) -> p b t", b=2)
        qT = view(R0, T)
        kT = view(R0 + T, T)
        vv = view(R0 + 2 * T, NC * DV, "p (c d) -> p c d", c=NC)
        O = view(R0 + 2 * T + NC * DV, NC * 2 * DV, "p (c r d) -> p c r d", c=NC, r=2)
        r1 = R0 + 2 * T + 3 * NC * DV
        kd = view(r1, 2 * P, "p (r n) -> p r n", r=2)
        sm = view(r1 + 256, 2 * P, "p (r n) -> p r n", r=2)
        qd = view(r1 + 512, 2 * P, "p (r n) -> p r n", r=2)
        S = view(r1 + 768, 8 * DV, "p (g r b d) -> p g r b d", g=2, r=2, b=2)
        uslot = view(0, SLOTS * D, "p (s d) -> p s d", s=SLOTS)
        vslot = view(SLOTS * D, SLOTS * D, "p (s d) -> p s d", s=SLOTS)
        h2 = view(16384, 2 * D, "p (b d) -> p b d", b=2)
        subk = view(GC0, 2 * PH * NK)
        wq = view(A0, KD * 2 * D, "p (k n) -> p k n", k=KD)
        bc = view(A0 + KD * 2 * D, 6 * D, "p (v j d) -> p v j d", v=3, j=2)
        small = view(43008, 6 * P, "p (v n) -> p v n", v=6)
        logit, expd, gsm, wgt, act, gelud = (small[:, i, :] for i in range(6))

        ident = sb("ident", [P, P])
        ones = sb("ones", [P, P])
        zeros = sb("zeros", [P, UW])
        rowbc = sb("rowbc", [P, D])
        mix = sb("mix", [P, G * P])
        m8 = sb("m8", [P, 2 * D])
        mask = m8[:, 0:D].rearrange("p (r h n) -> p r h n", r=2, h=HEADS)
        qdec = m8[:, D:2 * D].rearrange("p (r h n) -> p r h n", r=2, h=HEADS)
        pw = m8[:, :].rearrange("p (g b n) -> p g b n", g=G, b=2)
        h2T = m8[:, 0:D].rearrange("p (k t) -> p k t", k=KD)
        qp = m8[:, D:D + 256]
        qpT = m8[:, D + 256:D + 512].rearrange("p (s t) -> p s t", s=2)
        hot = m8[:, D + 512:2 * D].rearrange("p (s a b) -> p s a b", s=2, a=TOP)
        tmp = sb("tmp", [P, 4, UW])
        early_slots = view(HT0, 2 * KD * UW, "p (s k n) -> p s k n", s=2, k=KD)
        mod_slots = [early_slots[:, 0], early_slots[:, 1], ring[:, 0], ring[:, 1]]
        xo = tmp[:, 0:2, :].rearrange("p a n -> p (a n)")
        yb = tmp[:, 2:4, :].rearrange("p a n -> p (a n)")
        diag = sb("diag", [P, SLOTS, P])
        xr = diag[:, :, :].rearrange("p (s a) n -> p s (a n)", s=2)
        scr = diag[:, 0:8, :]
        bst = scr[:, 0, 0:120].rearrange("p (c s) -> p c s", c=NC)
        mv = scr[:, 1, 0:20].rearrange("p (c s) -> p c s", c=NC)
        relf, relb, rowf, rowb = (scr[:, i, :] for i in range(2, 6))
        late = sb("late", [P, NC * P])
        idx = late[:, :].bitcast(U32).rearrange("p (c n) -> p c n", c=NC)
        stage = sb("stage", [P, 2, 2, TOP], U32)
        rest = ones[:, :]
        cand = mix[:, 0:256].rearrange("p (a b) -> p a b", a=TOP)
        cand2 = mix[:, 256:512]
        tv = sb("tv", [P, 2, TOP])
        ti = sb("ti", [P, 2, TOP], U32)
        tf = sb("tf", [P, 2, TOP])
        bv = sb("bv", [P, TOP])
        bp = sb("bp", [P, TOP], U32)
        ab = sb("ab", [P, 2, TOP], U32)
        abf = sb("abf", [P, 2, TOP])
        picked = sb("picked", [P, 2, TOP])
        iota16 = sb("iota16", [P, TOP])
        act16 = sb("act16", [P, TOP])
        early_at = [0]

        def early(n):
            early_at[0] += n
            assert early_at[0] <= NC * P
            return late[:, early_at[0] - n:early_at[0]]

        cond = early(KD * 2)
        scond = early(KD * 2).rearrange("p (k j) -> p k j", k=KD)
        bmod = early(48)
        ng = early(2 * KD)
        mod = early(96).rearrange("p (b j) -> p b j", b=48)
        s12 = early(4 * KD).rearrange("p (n k j) -> p n k j", n=2, k=KD)
        bsp = early(G)
        decay = early(2 * HEADS)
        lg = early(6 * 2 * HEADS).rearrange("p (v n) -> p v n", v=6)
        kdec = early(2 * HEADS)
        gch = early(2 * HEADS)
        colf = early(2)
        ssq = early(2 * NC)
        rms = early(2 * NC)
        rst = early(2 * NC)
        one = sb("one", [P, 12])
        rsum = sb("rsum", [P, 2, PH])
        ps = ctx.enter_context(nc.psum_tensor("ps", [P, 8, 512], F32))

        names = """in_x in_const ring_0 ring_1 mod_0 mod_1 late_in in_gc in_mctx in_pw in_psc in_state in_fg
            in_subk in_wq xo_in state_out y_stored gt2_stored gt2_back y_sum y_sq
            act_full act_emptied dve_full dve_emptied tmp_free
            silu_done mod_done x_squared x_ms x_std x_normed
            ln_var ln_std ln_done pool_consts decay_in lg_exp lg_u lg_ln lg_done rel_done exps_done
            mask_done gate_a_done s_init kt_full kd_done sc_full sm_done qd_done o_full o_done kv_full
            state_done o_ms o_std o_ready pt_ready diag_ready row_diag merged z_done
            x1_done bc_done credit idx_done u_free v_free v_diag act_done gelu_done ls_done exp_done
            w_done gsm_done vacc_full vacc_free y_ms y_std y_done h2_done h2_trans h2T_done h2_sq
            h2_ms h2_std qp_full qp_done qpT_full qpT_done sc2_full sc2_free staged
            pe_gate act_gate dve_gate pool_gate sp_gate act_step dve_step pool_step""".split()
        s = {n: sem(n) for n in names}
        u_in = [sem(f"u_in_{i}") for i in range(SLOTS)]
        v_in = [sem(f"v_in_{i}") for i in range(SLOTS)]
        xr_in = [sem(f"xr_in_{i}") for i in range(2)]
        x1_stored = [sem(f"x1_stored_{i}") for i in range(4)]
        x1_in = [sem(f"x1_in_{i}") for i in range(2)]
        ring_in = [s["ring_0"], s["ring_1"]]
        mod_in = [s["mod_0"], s["mod_1"]] + ring_in

        x1d = nc.dram_tensor("x1_scratch", [NC, P, D], F32, kind="Internal").ap()
        gt2d = nc.dram_tensor("gt2_scratch", [P, 2 * D], F32, kind="Internal").ap()
        block = ctx.enter_context(nc.Block())

        def phases(eng_steps, phase, per_pair):
            for p in range(4):
                phase(p, p % 2, p // 2)
            with eng_steps.loop((NC - 6) // 2, per_pair) as m:
                for par in range(2):
                    phase(m * 2 + 4 + par, par, m + 2)
            for p in range(NC - 2, NC + 2):
                phase(p, p % 2, p // 2)

        def does(p):
            if not isinstance(p, int):
                return True, True, True
            return p < NC, 1 <= p <= NC, p >= 2

        def hbuf(p, par):
            return rowbc[:, :] if isinstance(p, int) and p == 0 else h2[:, par, :]

        @block.sync
        def _(sp):
            st = Steps(sp, s["sp_gate"], s["sp_gate"])
            def unit(src, slot, used_by, count):
                sp.wait_ge(s[used_by], count)
                sp.dma_start(ring[:, slot].rearrange("p k n -> p (k n)"), src).then_inc(ring_in[slot], 16)

            def mod_unit(n):
                sp.dma_start(mod_slots[n].rearrange("p k n -> p (k n)"), a["wmod"][n]).then_inc(mod_in[n], 16)

            mod_unit(0)
            for c in range(NC):
                sp.dma_start(A[:, c, :], a["x"][c]).then_inc(s["in_x"], 16)
            for n in range(1, 4):
                mod_unit(n)

            def late(m):
                sp.wait_ge(s["dve_full"], D_LATE + m)
                sp.dma_start(late_mod.rearrange("p k n -> p (k n)"), a["wlate"][m]).then_inc(s["late_in"], 16)

            for slot in range(2):
                unit(a["wa"][slot], slot, "dve_full", D_MOD + 3 + slot)
            unit(a["wa"][2], 0, "act_full", T_A + 10)
            late(0)
            for n in range(3, 6):
                unit(a["wa"][n], n % 2, "act_full", T_A + 10 * (n - 1))
                for m in range(4 * n - 11, 4 * n - 7):
                    late(m)
            for m in range(13, 16):
                late(m)
            with sp.Fori(0, HEADS) as h:
                for slot in range(2):
                    unit(a["whead"][h * 2 + slot], slot, "act_full",
                         h * HEAD_TILES + (T_C - (10, 0)[slot]))
                sp.wait_ge(s["act_full"], h * HEAD_TILES + T_C)
                sp.dma_start(gcb.rearrange("p k n -> p (k n)"), a["wgc"][h]).then_inc(s["in_gc"], 16)
                sp.wait_ge(s["dve_emptied"], D_PW)
                for r in range(2):
                    sp.dma_start(S[:, 1, r, 0, :], a["state"][r, h]).then_inc(s["in_state"], 16)
                sp.wait_ge(s["state_done"], h * (2 * NC) + 2 * CC)
                for r in range(2):
                    sp.dma_start(a["new_state"][r, h], S[:, 0, r, 0, :]).then_inc(s["state_out"], 16)
            sp.wait_ge(s["ln_done"], 1)
            sp.dma_start(rowbc[:, :], a["psc"]).then_inc(s["in_psc"], 16)
            unit(a["wz"][0], 0, "act_full", T_Z - 5)
            unit(a["wz"][1], 1, "act_full", T_Z - 5)
            sp.wait_ge(s["act_full"], T_Z)
            sp.dma_start(mctx.rearrange("p g s t -> p (g s t)"), a["mctx"]).then_inc(s["in_mctx"], 16)
            sp.wait_ge(s["sm_done"], HEADS * 2 * NC)
            sp.wait_ge(s["qd_done"], HEADS * 2 * NC)
            sp.dma_start(m8[:, :], a["poolw"]).then_inc(s["in_pw"], 16)
            for g in range(G):
                for half in range(2):
                    unit(a["mlat"][2 * g + half], half, "act_full",
                         T_POOL + 5 * (g - 1) + 3 + 2 * half if g else T_Z + 10 * (half + 1))
            for slot in range(2):
                unit(a["wgb"][slot], slot, "act_full", T_POOL + 5 * (G - 1) + 3 + 2 * slot)
            for slot in range(2):
                unit(a["wout"][slot], slot, "act_full", T_GB + 10 * (slot + 1))
            sp.wait_ge(s["dve_emptied"], D_OUT)
            sp.dma_start(subk, a["subk"]).then_inc(s["in_subk"], 16)
            sp.wait_ge(s["act_emptied"], T_BC + 4)
            sp.dma_start(gt2d, bc[:, 2].rearrange("p j d -> p (j d)")).then_inc(s["gt2_stored"], 16)

            def load_xr(n):
                sp.dma_start(xr[:, n % 2, :], a["x"][n // 2][:, (n % 2) * UW:(n % 2 + 1) * UW]
                             ).then_inc(xr_in[n % 2], 16)

            def store_x1(n):
                sp.wait_ge(s["x1_done"], n + 1)
                sp.dma_start(x1d[n // 2][:, (n % 2) * UW:(n % 2 + 1) * UW],
                             tmp[:, n % 4, :]).then_inc(x1_stored[n % 4], 16)
                if n + 2 < 2 * NC:
                    load_xr(n + 2)

            sp.wait_ge(s["act_emptied"], T_END)
            load_xr(0)
            load_xr(1)
            for k in range(KD):
                sp.dma_start(wq[:, k, :], a["wq"][k]).then_inc(s["in_wq"], 16)
            for n in range(2):
                store_x1(n)
            for n in range(2):
                sp.wait_ge(x1_stored[n], 16)
            sp.dma_start(hbuf(0, 0), x1d[0]).then_inc(x1_in[0], 16)
            for n in range(2, 2 * NC):
                store_x1(n)
            for n in range(4):
                sp.wait_ge(x1_stored[n], 16 * 2 * NC // 4)
            sp.dma_start(bc[:, 2].rearrange("p j d -> p (j d)"), gt2d).then_inc(s["gt2_back"], 16)

            def phase(p, par, k):
                prep, dots, sums = does(p)
                if sums:
                    sp.wait_ge(s["y_done"], p - 2) if not isinstance(p, int) or p > 2 else None
                    sp.dma_start(xo, x1d[p - 2]).then_inc(s["xo_in"], 16)
                if not isinstance(p, int) or p + 1 < NC:
                    if not isinstance(p, int) or p >= 1:
                        sp.wait_ge(s["act_done"], p)
                    sp.dma_start(h2[:, 1 - par, :], x1d[p + 1]).then_inc(x1_in[1 - par], 16)
                if isinstance(p, int) and p == 1:
                    sp.dma_start(rowbc[:, :], a["fg"]).then_inc(s["in_fg"], 16)
                if sums:
                    sp.wait_ge(s["y_done"], p - 1)
                    sp.dma_start(a["y"][p - 2], yb).then_inc(s["y_stored"], 16)

            phases(st, phase, 0)
            sp.wait_ge(s["y_stored"], 16 * NC)
            sp.wait_ge(s["state_out"], 16 * 2 * HEADS)

        @block.gpsimd
        def _(pool):
            st = Steps(pool, s["pool_step"], s["pool_gate"])
            g = nc.gpsimd
            st.step(g.memset(ident[:, :], 0.0))
            st.step(g.memset(ones[:, :], 1.0))
            st.step(g.memset(zeros[:, :], 0.0))
            st.step(g.iota(relf, [[1, P]], base=0, channel_multiplier=-1,
                           allow_small_or_imprecise_dtypes=True))
            st.step(g.iota(relb, [[-1, P]], base=0, channel_multiplier=1,
                           allow_small_or_imprecise_dtypes=True))
            st.step(g.iota(rowf, [[1, P]], base=1, channel_multiplier=0,
                           allow_small_or_imprecise_dtypes=True))
            st.step(g.iota(rowb, [[-1, P]], base=P, channel_multiplier=0,
                           allow_small_or_imprecise_dtypes=True))
            st.step(g.iota(colf[:, 0:1], [[0, 1]], base=P - 1, channel_multiplier=-1,
                           allow_small_or_imprecise_dtypes=True))
            st.step(g.iota(colf[:, 1:2], [[0, 1]], base=0, channel_multiplier=1,
                           allow_small_or_imprecise_dtypes=True))
            st.step(g.iota(iota16[:, :], [[1, TOP]], base=0, channel_multiplier=0,
                           allow_small_or_imprecise_dtypes=True))
            st.settle()
            st.step(g.affine_select(out=ident[:, :], in_=ident[:, :], compare_op=ALU.not_equal, fill=1.0,
                                    base=0, pattern=[[-1, P]], channel_multiplier=1))
            st.step(g.tensor_scalar(relf, relf, 0.0, None, ALU.max))
            st.step(g.tensor_scalar(relb, relb, 0.0, None, ALU.max))
            st.settle()
            pool.sem_inc(s["pool_consts"], 1)
            pool.wait_ge(s["exps_done"], 1)
            for h in range(HEADS):
                st.step(g.affine_select(out=mask[:, 0, h, :], in_=mask[:, 0, h, :], compare_op=ALU.is_ge,
                                        fill=0.0, base=0, pattern=[[1, P]], channel_multiplier=-1))
                st.step(g.affine_select(out=mask[:, 1, h, :], in_=mask[:, 1, h, :], compare_op=ALU.is_ge,
                                        fill=0.0, base=0, pattern=[[-1, P]], channel_multiplier=1))
            st.settle()
            pool.sem_inc(s["mask_done"], 1)

            pool.wait_ge(s["dve_full"], D_END)

            def gathers(p, tables):
                n_copies = len(tables)
                with st.loop(PH // 2, 2 * n_copies) as pair:
                    for odd in range(2):
                        for n, (side, chunk, *_) in enumerate(tables):
                            st.step(g.tensor_copy(
                                stage[:, odd, side, :],
                                idx[:, chunk, ds(pair * (2 * TOP) + odd * TOP, TOP)]))
                        st.settle()
                        for j in range(TOP):
                            for side, chunk, table, slot, free, landed in tables:
                                st.wait(free, chunk * P + pair * (2 * TOP) + (odd * TOP + j + 1))
                                g.indirect_dma_start(
                                    out=slot[:, j % SLOTS, :], out_offset=None, in_=table,
                                    in_offset=bass.IndirectOffsetOnAxis(
                                        ap=stage[:, odd, side, j:j + 1], axis=0),
                                ).then_inc(landed[j % SLOTS], 16)

            def phase(p, par, k):
                _, dots, sums = does(p)
                tables = []
                if dots:
                    st.wait(s["idx_done"], (p - 1) * PH + PH)
                    tables.append((0, p - 1, a["peer_u"], uslot, s["u_free"], u_in))
                if sums:
                    tables.append((1, p - 2, a["peer_v"], vslot, s["v_free"], v_in))
                if tables:
                    gathers(p, tables)

            phases(st, phase, 2 * 2 * PH)

        @block.scalar
        def _(eng):
            st = Steps(eng, s["act_step"], s["act_gate"])
            A_ = nc.scalar.activation
            for dst, name in ((cond[:, :], "cond"), (bmod[:, :], "bmod"), (ng[:, :], "ng"),
                              (decay[:, :], "decay"), (rowbc[:, :], "lng"), (mix[:, :], "mix"),
                              (bsp[:, :], "bsp")):
                eng.dma_start(dst, a[name]).then_inc(s["in_const"], 16)
            eng.wait_ge(s["in_const"], 16 * 7)
            A_(scond.rearrange("p k j -> p (k j)"), cond[:, :], ACT.Silu).then_inc(s["silu_done"], 1)

            eng.wait_ge(s["in_x"], 16 * NC)
            for c in range(NC):
                st.step(A_(Z[:, c, :], A[:, c, :], ACT.Square, accum_out=ssq[:, c:c + 1]))
            st.settle()
            eng.sem_inc(s["x_squared"], 1)
            eng.wait_ge(s["x_ms"], 1)
            A_(rms[:, 0:NC], rms[:, NC:2 * NC], ACT.Sqrt).then_inc(s["x_std"], 1)

            def full(t):
                st.wait(s["act_full"], t + 1)

            eng.wait_ge(s["mod_done"], 1)
            for k in range(KD):
                for n, (c0, cn, j) in enumerate(SEGS):
                    t = T_HT + 3 * k + n
                    full(t)
                    A_(hT[:, k, c0 * P:(c0 + cn) * P], ps[:, t % 4, 0:cn * P], ACT.Identity,
                       scale=s12[:, 0, k, j:j + 1], bias=mod[:, k, j:j + 1]).then_inc(s["act_emptied"], 1)

            eng.wait_ge(s["decay_in"], 1)
            A_(lg[:, 1, :], lg[:, 0, :], ACT.Exp, scale=-1.0).then_inc(s["lg_exp"], 1)
            eng.wait_ge(s["lg_u"], 1)
            A_(lg[:, 3, :], lg[:, 2, :], ACT.Ln).then_inc(s["lg_ln"], 1)
            eng.wait_ge(s["lg_done"], 1)
            eng.wait_ge(s["pool_consts"], 1)
            for r in range(2):
                for h in range(HEADS):
                    at = r * HEADS + h
                    col = lg[:, 5, at:at + 1]
                    st.step(A_(mask[:, r, h, :], (relf, relb)[r], ACT.Exp, scale=col))
                    st.step(A_(qdec[:, r, h, :], (rowf, rowb)[r], ACT.Exp, scale=col))
                    st.step(A_(kdec[:, at:at + 1], colf[:, r:r + 1], ACT.Exp, scale=col))
            st.step(A_(gch[:, :], lg[:, 5, :], ACT.Exp, scale=float(P)))
            st.settle()
            eng.sem_inc(s["exps_done"], 1)

            for j in range(2):
                for c in range(NC):
                    t = T_A + j * NC + c
                    full(t)
                    A_(Z[:, c, j * UW:(j + 1) * UW], ps[:, t % 4, :],
                       ACT.Gelu_apprx_tanh).then_inc(s["act_emptied"], 1)
            eng.wait_ge(s["ln_var"], 1)
            A_(rms[:, 0:NC], rms[:, NC:2 * NC], ACT.Sqrt).then_inc(s["ln_std"], 1)
            for j in range(2):
                for c in range(NC):
                    t = T_A + 20 + j * NC + c
                    full(t)
                    A_(A[:, c, j * UW:(j + 1) * UW], ps[:, t % 4, :],
                       ACT.Gelu_apprx_tanh).then_inc(s["act_emptied"], 1)

            def gates(t0, m0, units, func, drain=False):
                for n in range(units * NC):
                    full(t0 + n)
                    if isinstance(m0, int) and m0 + n < 4:
                        pass
                    elif drain and n < 4:
                        st.wait(s["tmp_free"], m0)
                    else:
                        st.wait(s["tmp_free"], m0 + n - 3)
                    bank = (t0 + n) % 4 if isinstance(t0, int) else None
                    A_(tmp[:, n % 4, :], ps[:, bank, :], func).then_inc(s["act_emptied"], 1)

            gates(T_A + 40, TMP_A, 2, ACT.Sigmoid)

            per_scan = NC * 2
            with st.loop(HEADS, 0) as h:
                base = h * HEAD_TILES + T_C
                eng.wait_ge(s["dve_emptied"], D_PW)
                st.wait(s["tmp_free"], h * TMP_HEAD + TMP_C)
                for n in range(6):
                    c0, cn, _ = SEGS[n % 3]
                    full(base + n)
                    if n < 3:
                        A_(qT[:, c0 * P:(c0 + cn) * P], ps[:, n % 4, 0:cn * P],
                           ACT.Copy).then_inc(s["act_emptied"], 1)
                    else:
                        A_(kT[:, c0 * P:(c0 + cn) * P], ps[:, n % 4, 0:cn * P],
                           ACT.Copy, scale=float(DK ** -0.5)).then_inc(s["act_emptied"], 1)
                for n in range(6, 11):
                    c = 2 * (n - 6)
                    full(base + n)
                    A_(vv[:, c:c + 2, :], ps[:, n % 4, :].rearrange("p (c d) -> p c d", c=2),
                       ACT.Copy).then_inc(s["act_emptied"], 1)
                for it in range(NC):
                    for r in range(2):
                        n = h * per_scan + (2 * it + r)
                        st.wait(s["kt_full"], n + 1)
                        if it >= 1:
                            st.wait(s["kv_full"], n - 1)
                        A_(kd[:, r, :], ps[:, r, 0:P], ACT.Copy,
                           scale=kdec[:, ds(h + r * HEADS, 1)]).then_inc(s["kd_done"], 1)
                    for r in range(2):
                        n = h * per_scan + (2 * it + r)
                        c = scan_chunk(it, r)
                        st.wait(s["o_full"], n + 1)
                        A_(O[:, c, r, :], ps[:, 2 + r, 0:DV], ACT.Copy)
                        A_(ps[:, 2 + r, 0:DV], ps[:, 2 + r, 0:DV], ACT.Square,
                           accum_out=ssq[:, 2 * c + r:2 * c + r + 1]).then_inc(s["o_done"], 1)
                st.wait(s["o_ms"], h + 1)
                A_(rms[:, :], rms[:, :], ACT.Sqrt).then_inc(s["o_std"], 1)
                for n in range(15):
                    loc = 11 + n
                    full(base + loc)
                    if n >= 4:
                        st.wait(s["tmp_free"], h * TMP_HEAD + (TMP_C + n - 3))
                    A_(tmp[:, n % 4, :], ps[:, loc % 4, :],
                       ACT.Silu if n < 10 else ACT.Sigmoid).then_inc(s["act_emptied"], 1)

            eng.wait_ge(s["o_ready"], 1)
            eng.wait_ge(s["state_out"], 16 * 2 * HEADS)
            for n in range(20):
                full(T_Z + n)
                A_(Z[:, n % NC, (n // NC) * UW:(n // NC + 1) * UW], ps[:, n % 4, :],
                   ACT.Copy).then_inc(s["act_emptied"], 1)
            for g in range(G):
                for n in range(5):
                    full(T_POOL + 5 * g + n)
                    if n == 0 and g:
                        st.wait(s["dve_full"], D_PW + 5 * g)
                    src = ps[:, (T_POOL + 5 * g + n) % 4, :]
                    if n == 0:
                        dst, src = PT[:, :, 0:CTX], src.rearrange("p (b t) -> p b t", b=2)
                    else:
                        half, b = (n - 1) // 2, (n - 1) % 2
                        dst = PT[:, b, CTX + half * UW:CTX + (half + 1) * UW]
                    A_(dst, src, ACT.Copy).then_inc(s["act_emptied"], 1)
            gates(T_GB, TMP_GB, 2, ACT.Sigmoid, drain=True)

            st.wait(s["tmp_free"], TMP_GB + 20)
            for n in range(16):
                v, j, half = n // 4, (n // 2) % 2, n % 2
                full(T_BC + n)
                if n == 12:
                    eng.wait_ge(s["gt2_stored"], 16)
                dst = bc[:, (2, 0, 1, 2)[v], j, half * UW:(half + 1) * UW]
                A_(dst, ps[:, n % 4, :], ACT.Copy).then_inc(s["act_emptied"], 1)
            for k in range(KD):
                for n, (c0, cn, _) in enumerate(SEGS):
                    t = T_MT + 3 * k + n
                    full(t)
                    A_(hT[:, k, c0 * P:(c0 + cn) * P], ps[:, t % 4, 0:cn * P],
                       ACT.Copy).then_inc(s["act_emptied"], 1)

            eng.sem_inc(s["qp_done"], 1)
            eng.sem_inc(s["qpT_done"], 1)
            eng.wait_ge(s["dve_emptied"], D_OUT)

            def phase(p, par, k):
                prep, dots, sums = does(p)
                if prep:
                    st.wait(x1_in[par], (k + 1) * 16)
                    st.wait(s["h2_done"], p)
                    for half in range(2):
                        A_(ps[:, 6 + half, :], hbuf(p, par)[:, half * UW:(half + 1) * UW], ACT.Square,
                           accum_out=one[:, half:half + 1]).then_inc(s["h2_sq"], 1)
                    st.wait(s["h2_ms"], p + 1)
                    A_(one[:, 3:4], one[:, 2:3], ACT.Sqrt).then_inc(s["h2_std"], 1)
                    for half in range(2):
                        st.wait(s["h2_trans"], p * 2 + (half + 1))
                        A_(h2T[:, 4 * half:4 * half + 4, :],
                           ps[:, 6 + half, :].rearrange("p (k t) -> p k t", k=4),
                           ACT.Copy).then_inc(s["h2T_done"], 1)
                if sums:
                    st.wait(s["w_done"], p - 1)

                def diags(hd, j0, j1):
                    for j in range(j0, j1):
                        st.wait(s["v_free"], (p - 2) * P + hd * TOP + (j + 1))
                        A_(diag[:, j % SLOTS, :], ident[:, :], ACT.Copy,
                           scale=wgt[:, ds(hd * TOP + j, 1)]).then_inc(s["v_diag"], 1)

                if prep or sums:
                    with st.loop(PH, 0) as hd:
                        if sums:
                            diags(hd, 0, 4)
                        if prep:
                            st.wait(s["qp_full"], p * PH + hd + 1)
                            A_(qp, ps[:, 2, 0:256], ACT.Copy).then_inc(s["qp_done"], 1)
                        if sums:
                            diags(hd, 4, 8)
                        if prep:
                            st.wait(s["qpT_full"], p * PH + hd + 1)
                            A_(qpT.rearrange("p s t -> p (s t)"), ps[:, 3, 0:256],
                               ACT.Copy).then_inc(s["qpT_done"], 1)
                        if sums:
                            diags(hd, 8, TOP)
                if dots:
                    st.wait(s["act_done"], p)
                    A_(gelud, act, ACT.Gelu_apprx_tanh).then_inc(s["gelu_done"], 1)
                if prep:
                    st.wait(s["ls_done"], p + 1)
                    A_(expd, expd, ACT.Exp).then_inc(s["exp_done"], 1)
                if sums:
                    st.wait(s["y_sum"], p - 1)
                    A_(xo, yb, ACT.Square, accum_out=one[:, 4:5]).then_inc(s["y_sq"], 1)
                    st.wait(s["y_ms"], p - 1)
                    A_(one[:, 7:8], one[:, 6:7], ACT.Sqrt).then_inc(s["y_std"], 1)

            phases(st, phase, 0)

        @block.tensor
        def _(pe):
            st = Steps(pe, s["pe_gate"], s["pe_gate"])
            mm = nc.tensor.matmul

            def group(out, pairs):
                for n, (lhs, rhs) in enumerate(pairs):
                    last = mm(out, lhs, rhs, start=n == 0, stop=n == len(pairs) - 1)
                return last

            def unit_in(slot, pair):
                st.wait(ring_in[slot], (pair + 1) * 16)

            def act_tile(t, n=None, drain=False):
                if isinstance(t, int) and t < 4:
                    return
                st.wait(s["act_emptied"], t if drain else t - 3)

            def dve_tile(t):
                if isinstance(t, int) and t < 4:
                    return
                st.wait(s["dve_emptied"], t - 3)

            def transposed(src, t0):
                for k in range(KD):
                    for n, (c0, cn, _) in enumerate(SEGS):
                        t = t0 + 3 * k + n
                        act_tile(t)
                        for c in range(cn):
                            last = nc.tensor.transpose(ps[:, t % 4, c * P:(c + 1) * P],
                                                       src[:, c0 + c, k * P:(k + 1) * P], ident[:, :])
                        last.then_inc(s["act_full"], 1)

            def project(t0, pair, drain=False, late=None):
                for slot in range(2):
                    unit_in(slot, pair)
                    for c in range(NC):
                        n = slot * NC + c
                        if drain and n < 4:
                            act_tile(t0, drain=True)
                        else:
                            act_tile(t0 + n)
                        last = group(ps[:, n % 4, :],
                                     [(hT[:, k, c * P:(c + 1) * P], ring[:, slot, k, :])
                                      for k in range(KD)])
                        last.then_inc(s["act_full"], 1)
                        if late is not None and c in LATE_AFTER:
                            m = 4 * slot + LATE_AFTER.index(c)
                            st.wait(s["late_in"], late * 128 + 16 * (m + 1))
                            st.wait(s["dve_emptied"], late * 8 + (D_LATE + m - 3))
                            for b in range(2):
                                last = group(ps[:, 4 + m % 4, 2 * b:2 * b + 2],
                                             [(late_mod[:, k, b * P:(b + 1) * P], scond[:, k, :])
                                              for k in range(KD)])
                            last.then_inc(s["dve_full"], 1)

            pe.wait_ge(s["silu_done"], 1)
            for n in range(4):
                st.wait(mod_in[n], 16)
                for b in range(4):
                    last = group(ps[:, 4 + n % 4, 2 * b:2 * b + 2],
                                 [(mod_slots[n][:, k, b * P:(b + 1) * P], scond[:, k, :])
                                  for k in range(KD)])
                last.then_inc(s["dve_full"], 1)
            pe.wait_ge(s["pool_consts"], 1)
            pe.wait_ge(s["x_normed"], 1)
            transposed(A, T_HT)
            pe.wait_ge(s["act_emptied"], T_A)
            project(T_A, U_A // 2)
            with st.loop(2, 0) as i:
                project(i * 20 + (T_A + 20), i + (U_A // 2 + 1), late=i)
            pe.wait_ge(s["ln_done"], 1)
            for c in range(NC):
                for j in range(2):
                    t = D_MIX + 2 * c + j
                    dve_tile(t)
                    for b in range(2):
                        g = 2 * j + b
                        last = mm(ps[:, 4 + t % 4, b * GW:(b + 1) * GW], mix[:, g * P:(g + 1) * P],
                                  Z[:, c, g * GW:(g + 1) * GW], start=True, stop=True)
                    last.then_inc(s["dve_full"], 1)
            pe.wait_ge(s["dve_emptied"], D_PW)
            with st.loop(HEADS, 0) as h:
                base = h * HEAD_TILES + T_C
                sbase = h * (2 * NC)
                unit_in(0, h + U_HEAD // 2)
                for n in range(6):
                    c0, cn, _ = SEGS[n % 3]
                    act_tile(base if n < 4 else base + n, drain=n < 4)
                    group(ps[:, n % 4, 0:cn * P],
                          [(ring[:, 0, k, (n // 3) * P:(n // 3 + 1) * P], hT[:, k, c0 * P:(c0 + cn) * P])
                           for k in range(KD)]).then_inc(s["act_full"], 1)
                for n in range(6, 11):
                    act_tile(base + n)
                    for c in (2 * (n - 6), 2 * (n - 6) + 1):
                        last = group(ps[:, n % 4, (c % 2) * DV:(c % 2 + 1) * DV],
                                     [(hT[:, k, c * P:(c + 1) * P], ring[:, 0, k, 2 * P:4 * P])
                                      for k in range(KD)])
                    last.then_inc(s["act_full"], 1)
                st.wait(s["act_emptied"], base + 11)
                for it in range(NC):
                    for r in range(2):
                        n = sbase + (2 * it + r)
                        c = scan_chunk(it, r)
                        if it >= 1:
                            st.wait(s["kd_done"], n - 1)
                        nc.tensor.transpose(ps[:, r, 0:P], kT[:, c * P:(c + 1) * P],
                                            ident[:, :]).then_inc(s["kt_full"], 1)
                        if it >= 1:
                            st.wait(s["sm_done"], n - 1)
                        mm(ps[:, 4 + r, 0:P], kT[:, c * P:(c + 1) * P], qT[:, c * P:(c + 1) * P],
                           start=True, stop=True).then_inc(s["sc_full"], 1)
                    for r in range(2):
                        n = sbase + (2 * it + r)
                        c = scan_chunk(it, r)
                        seg = 0 if it < CC else 1
                        st.wait(s["sm_done"], n + 1)
                        st.wait(s["qd_done"], n + 1)
                        if it == 0:
                            st.wait(s["s_init"], h + 1)
                        elif it == CC:
                            st.wait(s["in_state"], (h + 1) * 32)
                        if it >= 1:
                            st.wait(s["state_done"], n - 1)
                            st.wait(s["o_done"], n - 1)
                        mm(ps[:, 2 + r, 0:DV], sm[:, r, :], vv[:, c, :], start=True, stop=False)
                        mm(ps[:, 2 + r, 0:DV], qd[:, r, :], S[:, seg, r, it % 2, :],
                           start=False, stop=True).then_inc(s["o_full"], 1)
                        st.wait(s["kd_done"], n + 1)
                        mm(ps[:, 6 + r, 0:DV], kd[:, r, :], vv[:, c, :],
                           start=True, stop=True).then_inc(s["kv_full"], 1)
                st.wait(s["kd_done"], sbase + 2 * NC)
                st.wait(s["o_done"], sbase + 2 * NC)
                st.wait(s["state_done"], sbase + 2 * NC)
                unit_in(1, h + U_HEAD // 2)
                for c in range(NC):
                    n = 11 + c
                    if c >= 4:
                        act_tile(base + n)
                    group(ps[:, n % 4, :], [(hT[:, k, c * P:(c + 1) * P], ring[:, 1, k, :])
                                            for k in range(KD)]).then_inc(s["act_full"], 1)
                st.wait(s["in_gc"], (h + 1) * 16)
                for n in range(21, 26):
                    act_tile(base + n)
                    for c in (2 * (n - 21), 2 * (n - 21) + 1):
                        last = group(ps[:, n % 4, (c % 2) * DV:(c % 2 + 1) * DV],
                                     [(hT[:, k, c * P:(c + 1) * P], gcb[:, k, :]) for k in range(KD)])
                    last.then_inc(s["act_full"], 1)
            project(T_Z, U_Z // 2, drain=True)
            pe.wait_ge(s["act_emptied"], T_POOL)
            pe.wait_ge(s["in_mctx"], 16)
            pe.wait_ge(s["in_pw"], 16)
            pe.wait_ge(s["state_done"], HEADS * 2 * NC)
            for g in range(G):
                t = T_POOL + 5 * g
                act_tile(t)
                for b in range(2):
                    ch = slice(g * GW + b * P, g * GW + (b + 1) * P)
                    last = group(ps[:, t % 4, b * CTX:(b + 1) * CTX],
                                 [(Z[:, c, ch], mctx[:, g, c, :]) for c in range(CC)])
                last.then_inc(s["act_full"], 1)
                for half in range(2):
                    unit_in(half, U_POOL // 2 + g)
                    for b in range(2):
                        t = T_POOL + 5 * g + 1 + 2 * half + b
                        ch = slice(g * GW + b * P, g * GW + (b + 1) * P)
                        act_tile(t)
                        group(ps[:, t % 4, :],
                              [(Z[:, CC + c, ch], ring[:, half, c, :]) for c in pool_sources(g, half)]
                              ).then_inc(s["act_full"], 1)
                pe.wait_ge(s["act_emptied"], T_POOL + 5 * g + 5)
                for n in range(5):
                    t = D_PW + 5 * g + n
                    dve_tile(t)
                    for c in (2 * n, 2 * n + 1):
                        last = group(ps[:, 4 + t % 4, (c % 2) * GW:(c % 2 + 1) * GW],
                                     [(PT[:, b, c * P:(c + 1) * P], pw[:, g, b, :]) for b in range(2)])
                    last.then_inc(s["dve_full"], 1)
            project(T_GB, U_GB // 2)
            for n in range(16):
                act_tile(T_BC + n)
                pe.wait_ge(s["row_diag"], n + 1)
                mm(ps[:, n % 4, :], ones[:, :], tmp[:, n % 4, :], start=True,
                   stop=True).then_inc(s["act_full"], 1)
            pe.wait_ge(s["merged"], 1)
            transposed(A, T_MT)
            pe.wait_ge(s["act_emptied"], T_END)

            def out_chunk(c):
                for j in range(2):
                    n = 2 * c + j
                    if n >= 2:
                        st.wait(s["dve_emptied"], D_OUT + n - 1)
                    group(ps[:, j, :], [(hT[:, k, c * P:(c + 1) * P], ring[:, j, k, :])
                                        for k in range(KD)]).then_inc(s["dve_full"], 1)

            for j in range(2):
                unit_in(j, U_OUT // 2)
            for c in range(CC):
                out_chunk(c)

            pe.sem_inc(s["v_free"], SLOTS)
            pe.wait_ge(s["in_wq"], 16 * KD)
            pe.wait_ge(s["in_subk"], 16)
            pe.wait_ge(s["dve_emptied"], D_OUT)

            def phase(p, par, k):
                prep, dots, sums = does(p)
                if sums:
                    st.wait(s["dve_emptied"], D_END)
                    st.wait(s["vacc_free"], p - 2)
                    for half in range(2):
                        mm(ps[:, half, :], ident[:, :], zeros[:, :], start=True, stop=False)
                if prep:
                    st.wait(s["h2_done"], p + 1)
                    st.wait(s["h2T_done"], p * 2)
                    for k in range(KD):
                        last = nc.tensor.transpose(ps[:, 6 + k // 4, (k % 4) * P:(k % 4 + 1) * P],
                                                   hbuf(p, par)[:, k * P:(k + 1) * P], ident[:, :])
                        if k % 4 == 3:
                            last.then_inc(s["h2_trans"], 1)
                    st.wait(s["h2T_done"], p * 2 + 2)

                def sum_rows(hd, j0, j1):
                    for j in range(j0, j1):
                        st.wait(v_in[j % SLOTS], ((p - 2) * (P // SLOTS) + hd * 2 + (j // SLOTS + 1)) * 16)
                        st.wait(s["v_diag"], (p - 2) * P + hd * TOP + (j + 1))
                        for half in range(2):
                            last = mm(ps[:, half, :], diag[:, j % SLOTS, :],
                                      vslot[:, j % SLOTS, half * UW:(half + 1) * UW],
                                      start=False, stop=False)
                        last.then_inc(s["v_free"], 1)

                def head(hd, odd):
                    n = p * PH + hd
                    if prep:
                        st.wait(s["qp_done"], n + 1)
                        group(ps[:, 2, 0:256], [(h2T[:, k, :], wq[:, k, ds(hd * 256, 256)])
                                                for k in range(KD)]).then_inc(s["qp_full"], 1)
                    if sums:
                        sum_rows(hd, 0, 4)
                    elif not dots:
                        out_chunk(CC + hd)
                    if prep:
                        st.wait(s["qp_done"], n + 2)
                        st.wait(s["qpT_done"], n + 1)
                        for side in range(2):
                            last = nc.tensor.transpose(ps[:, 3, side * P:(side + 1) * P],
                                                       qp[:, side * P:(side + 1) * P], ident[:, :])
                        last.then_inc(s["qpT_full"], 1)
                    if sums:
                        sum_rows(hd, 4, 8)
                    if prep:
                        st.wait(s["qpT_done"], n + 2)
                        st.wait(s["sc2_free"], n + 1)
                        for side in range(2):
                            last = mm(ps[:, 4 + odd, side * NK:(side + 1) * NK], qpT[:, side, :],
                                      subk[:, ds(hd * 256 + side * NK, NK)], start=True, stop=True)
                        last.then_inc(s["sc2_full"], 1)
                    if sums:
                        sum_rows(hd, 8, TOP)

                if prep and not dots:
                    for hd in range(PH):
                        head(hd, hd % 2)
                elif prep or sums:
                    with st.loop(PH // 2, 0) as pair:
                        for odd in range(2):
                            head(pair * 2 + odd, odd)
                if sums:
                    for half in range(2):
                        last = mm(ps[:, half, :], ident[:, :], zeros[:, :], start=False, stop=True)
                    last.then_inc(s["vacc_full"], 1)

            phases(st, phase, 0)

        @block.vector
        def _(dve):
            st = Steps(dve, s["dve_step"], s["dve_gate"])
            v = nc.vector

            def full(t):
                st.wait(s["dve_full"], t + 1)

            dve.wait_ge(s["in_const"], 16 * 7)
            dve.wait_ge(s["x_squared"], 1)
            v.tensor_scalar(rms[:, NC:2 * NC], ssq[:, 0:NC], 1.0 / D, EPS, ALU.mult,
                            ALU.add).then_inc(s["x_ms"], 1)
            dve.wait_ge(s["x_std"], 1)
            st.link(v.reciprocal(rst[:, 0:NC], rms[:, 0:NC]))
            for c in range(NC):
                st.step(v.tensor_scalar(A[:, c, :], A[:, c, :], rst[:, c:c + 1], None, ALU.mult))
            st.settle()
            dve.sem_inc(s["x_normed"], 1)

            def mod_columns(t, at, blocks):
                full(t)
                v.tensor_tensor(mod[:, at:at + blocks, :],
                                ps[:, 4 + t % 4, 0:2 * blocks].rearrange("p (b j) -> p b j", b=blocks),
                                bmod[:, at:at + blocks].unsqueeze(2).to_broadcast([P, blocks, 2]),
                                ALU.add).then_inc(s["dve_emptied"], 1)

            def scaled_norm(n):
                st.link(v.scalar_tensor_tensor(
                    out=s12[:, n], in0=mod[:, 8 + 24 * n:16 + 24 * n, :], scalar=1.0,
                    in1=ng[:, 8 * n:8 * n + 8].unsqueeze(2).to_broadcast([P, KD, 2]),
                    op0=ALU.add, op1=ALU.mult))

            def late_columns(m):
                mod_columns(D_LATE + m, 16 + 2 * m, 2)

            for t in range(4):
                mod_columns(D_MOD + t, 4 * t, 4)
            dve.wait_ge(s["dve_emptied"], D_LATE)
            scaled_norm(0)
            dve.sem_inc(s["mod_done"], 1)

            dve.wait_ge(s["in_const"], 16 * 7)
            st.link(v.tensor_scalar(lg[:, 4, :], decay[:, :], -1.0, None, ALU.mult))
            st.link(v.tensor_tensor(lg[:, 0, :], lg[:, 4, :], decay[:, :], ALU.max))
            dve.sem_inc(s["decay_in"], 1)
            dve.wait_ge(s["lg_exp"], 1)
            st.link(v.tensor_scalar(lg[:, 2, :], lg[:, 1, :], 1.0, None, ALU.add))
            dve.sem_inc(s["lg_u"], 1)
            st.link(v.tensor_scalar(lg[:, 4, :], lg[:, 2, :], 1.0, None, ALU.subtract))
            st.link(v.tensor_tensor(lg[:, 4, :], lg[:, 1, :], lg[:, 4, :], ALU.subtract))
            st.link(v.reciprocal(lg[:, 0, :], lg[:, 2, :]))
            st.link(v.tensor_tensor(lg[:, 4, :], lg[:, 4, :], lg[:, 0, :], ALU.mult))
            dve.wait_ge(s["lg_ln"], 1)
            st.link(v.tensor_tensor(lg[:, 4, :], lg[:, 4, :], lg[:, 3, :], ALU.add))
            st.link(v.tensor_scalar(lg[:, 0, :], decay[:, :], 0.0, None, ALU.min))
            st.link(v.tensor_tensor(lg[:, 5, :], lg[:, 0, :], lg[:, 4, :], ALU.subtract))
            dve.sem_inc(s["lg_done"], 1)

            for j in range(2):
                for c in range(NC):
                    dve.wait_ge(s["act_emptied"], T_A + j * NC + c + 1)
                    st.step(v.bn_stats(bst[:, c, 6 * j:6 * j + 6], Z[:, c, j * UW:(j + 1) * UW]))
            st.settle()
            for c in range(NC):
                st.step(v.bn_aggr(mv[:, c, :], bst[:, c, :]))
            st.settle()
            v.tensor_scalar(rms[:, NC:2 * NC], mv[:, :, 1], EPS, None, ALU.add).then_inc(s["ln_var"], 1)
            dve.wait_ge(s["ln_std"], 1)
            st.link(v.reciprocal(rst[:, 0:NC], rms[:, 0:NC]))
            for c in range(NC):
                st.step(v.tensor_scalar(Z[:, c, :], Z[:, c, :], mv[:, c, 0:1], rst[:, c:c + 1],
                                        ALU.subtract, ALU.mult))
            st.settle()
            for c in range(NC):
                st.step(v.tensor_tensor(Z[:, c, :], Z[:, c, :], rowbc[:, :], ALU.mult))
            st.settle()
            dve.sem_inc(s["ln_done"], 1)
            for m in range(8):
                late_columns(m)
            for n in range(20):
                j, c = n // NC, n % NC
                dve.wait_ge(s["act_emptied"], T_A + 40 + n + 1)
                dst = A[:, c, j * UW:(j + 1) * UW]
                v.tensor_tensor(dst, dst, tmp[:, n % 4, :], ALU.mult).then_inc(s["tmp_free"], 1)
                if c in LATE_AFTER:
                    late_columns(8 + 4 * j + LATE_AFTER.index(c))
            dve.wait_ge(s["tmp_free"], 20)
            dve.wait_ge(s["dve_emptied"], D_MIX)
            scaled_norm(1)
            for c in range(NC):
                for j in range(2):
                    t = D_MIX + 2 * c + j
                    full(t)
                    for b in range(2):
                        g = 2 * j + b
                        dst = A[:, c, g * GW:(g + 1) * GW]
                        last = v.scalar_tensor_tensor(out=dst, in0=ps[:, 4 + t % 4, b * GW:(b + 1) * GW],
                                                      scalar=bsp[:, g:g + 1], in1=dst,
                                                      op0=ALU.add, op1=ALU.mult)
                    last.then_inc(s["dve_emptied"], 1)

            dve.wait_ge(s["dve_emptied"], D_PW)
            dve.wait_ge(s["mask_done"], 1)
            with st.loop(HEADS, 1 + NC + NC // 2) as h:
                base = h * HEAD_TILES + T_C
                sbase = h * (2 * NC)
                for r in range(2):
                    last = v.memset(S[:, 0, r, 0, :], 0.0)
                last.then_inc(s["s_init"], 1)
                st.wait(s["act_emptied"], base + 6)
                for it in range(NC):
                    for r in range(2):
                        n = sbase + (2 * it + r)
                        c = scan_chunk(it, r)
                        if it >= 1:
                            st.wait(s["o_full"], n - 1)
                        at = ds(h + r * HEADS, 1)
                        v.tensor_tensor(qd[:, r, :], qT[:, c * P:(c + 1) * P],
                                        m8[:, ds(h * P + (D + r * HEADS * P), P)],
                                        ALU.mult).then_inc(s["qd_done"], 1)
                        st.wait(s["sc_full"], n + 1)
                        v.tensor_tensor(sm[:, r, :], ps[:, 4 + r, 0:P],
                                        m8[:, ds(h * P + r * HEADS * P, P)],
                                        ALU.mult).then_inc(s["sm_done"], 1)
                    for r in range(2):
                        n = sbase + (2 * it + r)
                        seg = 0 if it < CC else 1
                        st.wait(s["kv_full"], n + 1)
                        if it == 0:
                            st.wait(s["s_init"], h + 1)
                        elif it == CC:
                            st.wait(s["in_state"], (h + 1) * 32)
                        else:
                            st.wait(s["state_done"], n - 1)
                        v.scalar_tensor_tensor(out=S[:, seg, r, (it + 1) % 2, :],
                                               in0=S[:, seg, r, it % 2, :],
                                               scalar=gch[:, ds(h + r * HEADS, 1)],
                                               in1=ps[:, 6 + r, 0:DV], op0=ALU.mult,
                                               op1=ALU.add).then_inc(s["state_done"], 1)
                st.wait(s["o_done"], sbase + 2 * NC)
                v.tensor_scalar(rms[:, :], ssq[:, :], 1.0 / DV, EPS, ALU.mult,
                                ALU.add).then_inc(s["o_ms"], 1)
                st.wait(s["o_std"], h + 1)
                st.link(v.reciprocal(rst[:, :], rms[:, :]))
                for c in range(NC):
                    st.wait(s["act_emptied"], base + (11 + c + 1))
                    for r in range(2):
                        last = v.scalar_tensor_tensor(
                            out=O[:, c, r, :], in0=O[:, c, r, :], scalar=rst[:, 2 * c + r:2 * c + r + 1],
                            in1=tmp[:, c % 4, r * DV:(r + 1) * DV], op0=ALU.mult, op1=ALU.mult)
                    last.then_inc(s["tmp_free"], 1)
                    st.wait(s["tmp_free"], h * TMP_HEAD + (TMP_C + c + 1))
                    st.step(v.tensor_tensor(O[:, c, 0, :], O[:, c, 0, :], O[:, c, 1, :], ALU.add))
                st.settle()
                for n in range(5):
                    c = 2 * n
                    slot = (10 + n) % 4
                    st.wait(s["act_emptied"], base + (21 + n + 1))
                    dst = A[:, c:c + 2, ds(h * DV, DV)]
                    gate = tmp[:, slot, :].rearrange("p (c d) -> p c d", c=2)
                    v.tensor_tensor(O[:, c:c + 2, 0, :], O[:, c:c + 2, 0, :], gate,
                                    ALU.mult).then_inc(s["tmp_free"], 1)
                    st.wait(s["tmp_free"], h * TMP_HEAD + (TMP_C + 10 + n + 1))
                    st.step(v.tensor_tensor(dst, dst, O[:, c:c + 2, 0, :], ALU.add))
                st.wait(s["state_out"], h * 32 + 32)
            st.settle()
            dve.sem_inc(s["o_ready"], 1)

            dve.wait_ge(s["in_psc"], 16)
            for g in range(G):
                for n in range(5):
                    t = D_PW + 5 * g + n
                    full(t)
                    scale = rowbc[:, g * GW:(g + 1) * GW].unsqueeze(1).to_broadcast([P, 2, GW])
                    v.tensor_tensor(Z[:, 2 * n:2 * n + 2, g * GW:(g + 1) * GW],
                                    ps[:, 4 + t % 4, :].rearrange("p (c d) -> p c d", c=2),
                                    scale, ALU.mult).then_inc(s["dve_emptied"], 1)
            dve.wait_ge(s["dve_emptied"], D_OUT)
            for n in range(20):
                j, c = n // NC, n % NC
                dve.wait_ge(s["act_emptied"], T_GB + n + 1)
                gate, dst = tmp[:, n % 4, :], A[:, c, j * UW:(j + 1) * UW]
                st.link(v.tensor_tensor(gate, gate, Z[:, c, j * UW:(j + 1) * UW], ALU.mult))
                v.tensor_tensor(dst, dst, gate, ALU.add).then_inc(s["tmp_free"], 1)
            dve.wait_ge(s["tmp_free"], TMP_GB + 20)
            dve.sem_inc(s["merged"], 1)

            for n in range(16):
                vec, j, half = n // 4, (n // 2) % 2, n % 2
                b0 = 4 * half
                src = (mod[:, 40 + b0:44 + b0, j], s12[:, 1, b0:b0 + 4, j],
                       mod[:, 24 + b0:28 + b0, j], mod[:, 16 + b0:20 + b0, j])[vec]
                if n >= 4:
                    dve.wait_ge(s["act_full"], T_BC + n - 3)
                v.tensor_tensor(tmp[:, n % 4, :].rearrange("p (b n) -> p b n", b=4),
                                ident[:, :].unsqueeze(1).to_broadcast([P, 4, P]),
                                src.unsqueeze(2).to_broadcast([P, 4, P]),
                                ALU.mult).then_inc(s["row_diag"], 1)

            dve.wait_ge(s["act_emptied"], T_END)

            def x1_tile(n):
                c, j = n // 2, n % 2
                full(D_OUT + n)
                if n >= 4:
                    dve.wait_ge(x1_stored[n % 4], 16 * (n // 4))
                slot = tmp[:, n % 4, :]
                v.tensor_tensor(slot, ps[:, j, :], bc[:, 2, 0 if c < CC else 1, j * UW:(j + 1) * UW],
                                ALU.mult).then_inc(s["dve_emptied"], 1)
                dve.wait_ge(s["dve_emptied"], D_OUT + n + 1)
                dve.wait_ge(xr_in[n % 2], 16 * (n // 2 + 1))
                v.tensor_tensor(slot, slot, xr[:, n % 2, :], ALU.add).then_inc(s["x1_done"], 1)

            for n in range(2 * CC):
                x1_tile(n)

            dve.sem_inc(s["u_free"], SLOTS)
            dve.sem_inc(s["sc2_free"], 2)

            def top16(values, spare, out_v, out_i):
                st.link(v.max(out_v[:, 0:8], values))
                st.step(v.max_index(out_i[:, 0:8], out_v[:, 0:8], values))
                st.link(v.match_replace(spare, out_v[:, 0:8], values, LOWEST))
                st.link(v.max(out_v[:, 8:16], spare))
                st.link(v.max_index(out_i[:, 8:16], out_v[:, 8:16], spare))

            def dots_of(p, par, hd, j0):
                last_h2 = rowbc[:, :] if isinstance(p, int) and p == 1 else h2[:, 1 - par, :]
                for j in range(j0, j0 + TOP // 2):
                    st.wait(u_in[j % SLOTS], ((p - 1) * (P // SLOTS) + hd * 2 + (j // SLOTS + 1)) * 16)
                    row = uslot[:, j % SLOTS, :]
                    v.tensor_tensor_reduce(out=row, in0=row, in1=last_h2, scale=1.0, scalar=0.0,
                                           op0=ALU.mult, op1=ALU.add,
                                           accum_out=act16[:, j:j + 1]).then_inc(s["u_free"], 1)
                if j0 == 0:
                    return
                st.wait(s["u_free"], (p - 1) * P + hd * TOP + (SLOTS + TOP))
                st.link(v.tensor_copy(act[:, ds(hd * TOP, TOP)], act16[:, :]))

            def experts_of(p, hd, odd):
                n = p * PH + hd
                st.wait(s["sc2_full"], n + 1)
                for side in range(2):
                    top16(ps[:, 4 + odd, side * NK:(side + 1) * NK], rest, tv[:, side, :],
                          ti[:, side, :])
                dve.sem_inc(s["sc2_free"], 1)
                st.step(v.tensor_copy(tf[:, :, :], ti[:, :, :]))
                st.link(v.tensor_tensor(cand, tv[:, 0, :].unsqueeze(2).to_broadcast([P, TOP, TOP]),
                                        tv[:, 1, :].unsqueeze(1).to_broadcast([P, TOP, TOP]), ALU.add))
                flat = cand.rearrange("p a b -> p (a b)")
                top16(flat, cand2, bv[:, :], bp[:, :])
                st.step(v.tensor_copy(logit[:, ds(hd * TOP, TOP)], bv[:, :]))
                st.step(v.tensor_scalar(ab[:, 0, :], bp[:, :], 4, None, ALU.logical_shift_right))
                st.link(v.tensor_scalar(ab[:, 1, :], bp[:, :], 15, None, ALU.bitwise_and))
                st.link(v.tensor_copy(abf[:, :, :], ab[:, :, :]))
                st.link(v.tensor_tensor(hot, abf[:, :, :].unsqueeze(3).to_broadcast([P, 2, TOP, TOP]),
                                        iota16[:, :].unsqueeze(1).unsqueeze(1).to_broadcast(
                                            [P, 2, TOP, TOP]), ALU.is_equal))
                st.link(v.tensor_tensor(hot, hot, tf[:, :, :].unsqueeze(2).to_broadcast([P, 2, TOP, TOP]),
                                        ALU.mult))
                st.link(v.tensor_reduce(picked[:, :, :], hot, AX.X, ALU.add))
                v.scalar_tensor_tensor(out=idx[:, p, ds(hd * TOP, TOP)], in0=picked[:, 0, :],
                                       scalar=float(NK), in1=picked[:, 1, :], op0=ALU.mult,
                                       op1=ALU.add).then_inc(s["idx_done"], 1)
                st.wait(s["idx_done"], n + 1)

            def phase(p, par, k):
                prep, dots, sums = does(p)
                j = 1 if not isinstance(p, int) else (0 if p < CC else 1)
                if prep:
                    st.wait(s["h2_sq"], p * 2 + 2)
                    st.link(v.tensor_tensor(one[:, 8:9], one[:, 0:1], one[:, 1:2], ALU.add))
                    v.tensor_scalar(one[:, 2:3], one[:, 8:9], 1.0 / D, EPS, ALU.mult,
                                    ALU.add).then_inc(s["h2_ms"], 1)
                    st.wait(s["h2_std"], p + 1)
                    st.link(v.reciprocal(one[:, 9:10], one[:, 3:4]))
                    hb = hbuf(p, par)
                    st.link(v.scalar_tensor_tensor(out=hb, in0=hb,
                                                   scalar=one[:, 9:10], in1=bc[:, 0, j, :],
                                                   op0=ALU.mult, op1=ALU.mult))
                    v.tensor_tensor(hb, hb, bc[:, 1, j, :],
                                    ALU.add).then_inc(s["h2_done"], 1)
                    st.wait(s["h2_done"], p + 1)
                if prep and not dots:
                    for hd in range(PH):
                        for n in (2 * (CC + hd), 2 * (CC + hd) + 1):
                            x1_tile(n)
                        experts_of(p, hd, hd % 2)
                elif prep or dots:
                    with st.loop(PH // 2, 2 * (HEAD_PREP * prep + 1 * dots)) as pair:
                        for odd in range(2):
                            hd = pair * 2 + odd
                            if dots:
                                dots_of(p, par, hd, 0)
                            if prep:
                                experts_of(p, hd, odd)
                            if dots:
                                dots_of(p, par, hd, TOP // 2)
                if dots:
                    dve.sem_inc(s["act_done"], 1)
                if prep:
                    lv = logit.rearrange("p (h k) -> p h k", h=PH)
                    v.tensor_tensor(expd.rearrange("p (h k) -> p h k", h=PH), lv,
                                    lv[:, :, 0:1].to_broadcast([P, PH, TOP]),
                                    ALU.subtract).then_inc(s["ls_done"], 1)
                if sums:
                    jo = 1 if not isinstance(p, int) else (0 if p - 2 < CC else 1)
                    st.wait(s["gt2_back"], 16)
                    st.wait(s["y_stored"], (p - 2) * 16)
                    st.wait(s["vacc_full"], p - 1)
                    st.link(v.tensor_tensor(yb, ps[:, 0:2, :].rearrange("p b n -> p (b n)"),
                                            bc[:, 2, jo, :], ALU.mult))
                    dve.sem_inc(s["vacc_free"], 1)
                    st.wait(s["xo_in"], (p - 1) * 16)
                    st.link(v.tensor_tensor(yb, yb, xo, ALU.add))
                    dve.sem_inc(s["y_sum"], 1)
                if dots:
                    if sums:
                        st.wait(s["v_diag"], (p - 1) * P)
                    st.wait(s["gelu_done"], p)
                    v.tensor_tensor(wgt, gsm, gelud, ALU.mult).then_inc(s["w_done"], 1)
                    st.wait(s["w_done"], p)
                if prep:
                    ev = expd.rearrange("p (h k) -> p h k", h=PH)
                    st.wait(s["exp_done"], p + 1)
                    st.link(v.tensor_reduce(rsum[:, 0, :], ev, AX.X, ALU.add))
                    st.link(v.reciprocal(rsum[:, 1, :], rsum[:, 0, :]))
                    st.link(v.tensor_tensor(gsm.rearrange("p (h k) -> p h k", h=PH), ev,
                                            rsum[:, 1, :].unsqueeze(2).to_broadcast([P, PH, TOP]),
                                            ALU.mult))
                if sums:
                    st.wait(s["y_sq"], p - 1)
                    v.tensor_scalar(one[:, 6:7], one[:, 4:5], 1.0 / D, EPS, ALU.mult,
                                    ALU.add).then_inc(s["y_ms"], 1)
                    st.wait(s["y_std"], p - 1)
                    st.wait(s["in_fg"], 16)
                    st.link(v.reciprocal(one[:, 5:6], one[:, 7:8]))
                    v.scalar_tensor_tensor(out=yb, in0=yb, scalar=one[:, 5:6], in1=rowbc[:, :],
                                           op0=ALU.mult, op1=ALU.mult).then_inc(s["y_done"], 1)
                    st.wait(s["y_done"], p - 1)

            HEAD_PREP = 3 * 5 + 2 + 1 + 2 + 1 + 3
            per_phase = 3 + PH * (HEAD_PREP + 1) + 2 + 3 + 1
            phases(st, phase, 2 * per_phase)


def scan_chunk(it, r):
    if it < CC:
        return it if r == 0 else CC - 1 - it
    return it if r == 0 else NC - 1 + CC - it


def units_of(w):
    n = w.shape[1] // UW
    return np.ascontiguousarray(w.reshape(KD, P, n, UW).transpose(2, 1, 0, 3)).reshape(n, P, KD * UW)


def columns_of(x):
    x = x.reshape(-1, x.shape[-1] // P, P)
    return np.ascontiguousarray(x.transpose(2, 0, 1)).reshape(P, -1)


def spread(x):
    return np.ascontiguousarray(np.broadcast_to(x.reshape(1, -1), (P, x.size)))


def kernel(x_prompt, x_sample, state_ret, c, c_ctx, w_mod, b_mod, norm_g, w_in, w_out,
           gmlp_ws, gmlp_b, gmlp_ln_g, pool_w, pool_scale, ret_decay, peer_wq, peer_subkeys,
           peer_u, peer_v, final_norm_g):
    import concourse.bacc as bacc
    from concourse.bass_utils import run_bass_kernel_spmd

    arr = np.asarray
    w = arr(w_in)[0]
    u0, v0, z0, q0, k0, rv0, rf0, rb0, gm0 = (0, 1024, 2048, 3072, 3584, 4096, 5120, 6144, 7168)
    wa = np.concatenate([w[:, v0:v0 + D], w[:, u0:u0 + D], w[:, gm0:gm0 + D]], axis=1)
    heads, gcs = [], []
    for h in range(HEADS):
        heads += [w[:, q0 + h * DK:q0 + (h + 1) * DK], w[:, k0 + h * DK:k0 + (h + 1) * DK],
                  w[:, rv0 + h * DV:rv0 + (h + 1) * DV], w[:, rf0 + h * DV:rf0 + (h + 1) * DV],
                  w[:, rb0 + h * DV:rb0 + (h + 1) * DV]]
        at = gm0 + 2 * D + h * DV
        gcs.append(w[:, at:at + DV].reshape(KD, P, DV).transpose(1, 0, 2).reshape(P, KD * DV))
    mlat, mctx = pool_constants()
    x = np.concatenate([arr(x_prompt).reshape(CTX, D), arr(x_sample).reshape(LAT, D)])
    conds = np.stack([arr(c_ctx).reshape(D), arr(c).reshape(D)])
    host = {
        "x": x.reshape(NC, P, D),
        "cond": np.ascontiguousarray(conds.reshape(2, KD, P).transpose(2, 1, 0)).reshape(P, KD * 2),
        "wmod": units_of(arr(w_mod)[0][:, 0:2 * D]),
        "wlate": np.ascontiguousarray(
            arr(w_mod)[0][:, 2 * D:].reshape(KD, P, 16, UW // 2).transpose(2, 1, 0, 3)
        ).reshape(16, P, KD * UW // 2),
        "bmod": columns_of(arr(b_mod)[0]),
        "ng": columns_of(arr(norm_g)[0]),
        "decay": spread(arr(ret_decay)[0]),
        "lng": spread(arr(gmlp_ln_g)[0]),
        "mix": np.ascontiguousarray(arr(gmlp_ws)[0].transpose(2, 0, 1)).reshape(P, G * P),
        "bsp": np.ascontiguousarray(arr(gmlp_b)[0].T),
        "wa": units_of(wa),
        "whead": units_of(np.concatenate(heads, axis=1)),
        "wgc": np.ascontiguousarray(np.stack(gcs)),
        "state": arr(state_ret)[0, 0],
        "wz": units_of(w[:, z0:z0 + D]),
        "mctx": mctx,
        "mlat": mlat,
        "poolw": np.ascontiguousarray(arr(pool_w)[0].reshape(G, 2, P, GW).transpose(2, 0, 1, 3)
                                      ).reshape(P, G * 2 * GW),
        "psc": spread(arr(pool_scale)[0]),
        "wgb": units_of(w[:, gm0 + D:gm0 + 2 * D]),
        "wout": units_of(arr(w_out)[0]),
        "subk": np.ascontiguousarray(arr(peer_subkeys)[0].transpose(3, 0, 1, 2)).reshape(P, 2 * PH * NK),
        "fg": spread(arr(final_norm_g)),
        "wq": arr(peer_wq)[0].reshape(KD, P, 2 * D),
        "peer_u": arr(peer_u)[0],
        "peer_v": arr(peer_v)[0],
    }
    nc = bacc.Bacc("TRN2", target_bir_lowering=False, num_devices=1)
    a = {}
    for name, value in host.items():
        host[name] = np.ascontiguousarray(value)
        a[name] = nc.dram_tensor(f"in_{name}", value.shape, F32, kind="ExternalInput").ap()
    a["y"] = nc.dram_tensor("out_y", [NC, P, D], F32, kind="ExternalOutput").ap()
    a["new_state"] = nc.dram_tensor("out_state", [2, HEADS, DK, DV], F32, kind="ExternalOutput").ap()
    build(nc, a)
    r = run_bass_kernel_spmd(nc, [{f"in_{n}": v for n, v in host.items()}], core_ids=[0])
    y = r.results[0]["out_y"].reshape(T, D)
    new_state = r.results[0]["out_state"].reshape(1, 1, 2, HEADS, DK, DV)
    return (np.ascontiguousarray(y[:CTX]).reshape(1, CTX, D),
            np.ascontiguousarray(y[CTX:]).reshape(1, LAT, D), new_state)
```

```python
from contextlib import ExitStack, contextmanager

import numpy as np

import concourse.bass as bass
from concourse import mybir

ALU = mybir.AluOpType
ACT = mybir.ActivationFunctionType
AX = mybir.AxisListType
F32 = mybir.dt.float32
U32 = mybir.dt.uint32
ds = bass.ds

P = 128
D = 1024
KD = D // P
CTX = 256
LAT = 1024
T = CTX + LAT
NC = T // P
CC = CTX // P
EPS = 1e-6
GRID_W = 64
WINDOWS = (2, 4, 8, 16)
G = len(WINDOWS)
GW = D // G
HEADS = 4
DK = 128
DV = 256
PH = 8
NK = 128
TOP = 16
SLOTS = 8
UW = 512
LOWEST = -3.0e38

U_MOD, U_A, U_HEAD, U_Z, U_POOL, U_GB, U_OUT = 0, 2, 8, 16, 18, 26, 28

T_HT = 0
T_A = T_HT + 24
T_C = T_A + 60
HEAD_TILES = 26
T_Z = T_C + HEADS * HEAD_TILES
T_POOL = T_Z + 20
T_GB = T_POOL + 20
T_BC = T_GB + 20
T_MT = T_BC + 16
T_END = T_MT + 24
D_MOD = 0
D_LATE = D_MOD + 4
D_MIX = D_LATE + 16
D_PW = D_MIX + 20
D_OUT = D_PW + 20
D_END = D_OUT + 20
TMP_A = 0
TMP_C = TMP_A + 20
TMP_HEAD = 15
TMP_GB = TMP_C + HEADS * TMP_HEAD

LATE_AFTER = (1, 3, 5, 7)
SEGS = ((0, 2, 0), (2, 4, 1), (6, 4, 1))


def box_matrix(n, w):
    a, b = w // 2, w - 1 - w // 2
    at = np.arange(n)
    return ((at[:, None] >= at[None, :] - a) & (at[:, None] <= at[None, :] + b)).astype(np.float64)


def pool_constants():
    rows = LAT // GRID_W
    lat = np.zeros((G, 2, P, LAT // P, UW), np.float32)
    ctx = np.zeros((P, G, CC, CTX), np.float32)
    for g, w in enumerate(WINDOWS):
        r, c = box_matrix(rows, w), box_matrix(GRID_W, w)
        m = np.kron(r / r.sum(0), c / c.sum(0)) - np.eye(LAT)
        lat[g] = m.reshape(LAT // P, P, 2, UW).transpose(2, 1, 0, 3)
        m = box_matrix(CTX, w)
        m = m / m.sum(0) - np.eye(CTX)
        ctx[:, g] = m.reshape(CC, P, CTX).transpose(1, 0, 2)
    return lat.reshape(2 * G, P, KD * UW), ctx.reshape(P, G * CC * CTX)


def pool_sources(g, half):
    w = WINDOWS[g]
    a, b = w // 2, w - 1 - w // 2
    rows = LAT // GRID_W
    first, last = half * rows // 2 - a, (half + 1) * rows // 2 - 1 + b
    return range(max(first, 0) // 2, min(last, rows - 1) // 2 + 1)


class Steps:

    def __init__(self, eng, sem, gate):
        self.eng, self.sem, self.gate, self.base, self.n = eng, sem, gate, 0, 0

    def wait(self, sem, value):
        if isinstance(value, int):
            if value > 0:
                self.eng.wait_ge(sem, value)
        else:
            self.eng.wait_ge(sem, value)
            self.eng.sem_inc(self.gate, 1)

    def step(self, ins):
        self.n += 1
        return ins.then_inc(self.sem, 1)

    def settle(self):
        self.wait(self.sem, self.base + self.n)

    def link(self, ins):
        self.step(ins)
        self.settle()

    @contextmanager
    def loop(self, trips, per_trip):
        base, n = self.base, self.n
        with self.eng.Fori(0, trips) as i:
            if per_trip:
                self.base = base + i * per_trip
            yield i
            assert self.n - n == per_trip, (self.n - n, per_trip)
        self.base, self.n = base, n + per_trip * trips


def build(nc, a):
    with ExitStack() as ctx:
        def sb(name, shape, dt=F32):
            return ctx.enter_context(nc.sbuf_tensor(name, shape, dt))

        def sem(name):
            return ctx.enter_context(nc.semaphore(name))

        HT0, RING0, GC0, A0, R0, AEND = 0, 10240, 18432, 20480, 30720, 43776
        arena = sb("arena", [P, AEND])

        def view(at, n, text=None, **kw):
            v = arena[:, at:at + n]
            return v.rearrange(text, **kw) if text else v

        hT = view(HT0, KD * T, "p (k t) -> p k t", k=KD)
        ring = view(RING0, 2 * KD * UW, "p (s k n) -> p s k n", s=2, k=KD)
        gcb = view(GC0, KD * DV, "p (k n) -> p k n", k=KD)
        late_mod = view(GC0, KD * UW // 2, "p (k n) -> p k n", k=KD)
        mctx = view(GC0, G * CC * CTX, "p (g s t) -> p g s t", g=G, s=CC)
        A = view(A0, NC * D, "p (c d) -> p c d", c=NC)
        Z = view(R0, NC * D, "p (c d) -> p c d", c=NC)
        PT = view(R0 + NC * D, 2 * T, "p (b t) -> p b t", b=2)
        qT = view(R0, T)
        kT = view(R0 + T, T)
        vv = view(R0 + 2 * T, NC * DV, "p (c d) -> p c d", c=NC)
        O = view(R0 + 2 * T + NC * DV, NC * 2 * DV, "p (c r d) -> p c r d", c=NC, r=2)
        r1 = R0 + 2 * T + 3 * NC * DV
        kd = view(r1, 2 * P, "p (r n) -> p r n", r=2)
        sm = view(r1 + 256, 2 * P, "p (r n) -> p r n", r=2)
        qd = view(r1 + 512, 2 * P, "p (r n) -> p r n", r=2)
        S = view(r1 + 768, 8 * DV, "p (g r b d) -> p g r b d", g=2, r=2, b=2)
        slots = view(0, SLOTS * 2 * D, "p (s d) -> p s d", s=SLOTS)
        h2 = view(16384, 2 * D, "p (b d) -> p b d", b=2)
        subk = view(GC0, 2 * PH * NK)
        wq = view(A0, KD * 2 * D, "p (k n) -> p k n", k=KD)
        bc = view(A0 + KD * 2 * D, 6 * D, "p (v j d) -> p v j d", v=3, j=2)
        small = view(43008, 3 * P, "p (v n) -> p v n", v=3)
        logit, expd, gsm = (small[:, i, :] for i in range(3))

        ident = sb("ident", [P, P])
        ones = sb("ones", [P, P])
        zeros = sb("zeros", [P, UW])
        rowbc = sb("rowbc", [P, D])
        mix = sb("mix", [P, G * P])
        m8 = sb("m8", [P, 2 * D])
        mask = m8[:, 0:D].rearrange("p (r h n) -> p r h n", r=2, h=HEADS)
        qdec = m8[:, D:2 * D].rearrange("p (r h n) -> p r h n", r=2, h=HEADS)
        pw = m8[:, :].rearrange("p (g b n) -> p g b n", g=G, b=2)
        h2T = m8[:, 0:D].rearrange("p (k t) -> p k t", k=KD)
        qp = m8[:, D:D + 256]
        qpT = m8[:, D + 256:D + 512].rearrange("p (s t) -> p s t", s=2)
        hot = m8[:, D + 512:2 * D].rearrange("p (s a b) -> p s a b", s=2, a=TOP)
        tmp = sb("tmp", [P, 4, UW])
        early_slots = view(HT0, 2 * KD * UW, "p (s k n) -> p s k n", s=2, k=KD)
        mod_slots = [early_slots[:, 0], early_slots[:, 1], ring[:, 0], ring[:, 1]]
        xo = tmp[:, 0:2, :].rearrange("p a n -> p (a n)")
        yb = tmp[:, 2:4, :].rearrange("p a n -> p (a n)")
        diag = sb("diag", [P, SLOTS, P])
        xr = diag[:, :, :].rearrange("p (s a) n -> p s (a n)", s=2)
        scr = diag[:, 0:8, :]
        bst = scr[:, 0, 0:120].rearrange("p (c s) -> p c s", c=NC)
        mv = scr[:, 1, 0:20].rearrange("p (c s) -> p c s", c=NC)
        relf, relb, rowf, rowb = (scr[:, i, :] for i in range(2, 6))
        late = sb("late", [P, NC * P])
        idx = late[:, :].bitcast(U32).rearrange("p (c n) -> p c n", c=NC)
        stage = sb("stage", [P, 2, TOP], U32)
        rest = ones[:, :]
        cand = mix[:, 0:256].rearrange("p (a b) -> p a b", a=TOP)
        cand2 = mix[:, 256:512]
        tv = sb("tv", [P, 2, TOP])
        ti = sb("ti", [P, 2, TOP], U32)
        tf = sb("tf", [P, 2, TOP])
        bv = sb("bv", [P, TOP])
        bp = sb("bp", [P, TOP], U32)
        ab = sb("ab", [P, 2, TOP], U32)
        abf = sb("abf", [P, 2, TOP])
        picked = sb("picked", [P, 2, TOP])
        iota16 = sb("iota16", [P, TOP])
        dot16 = sb("dot16", [P, TOP])
        gelu16 = sb("gelu16", [P, TOP])
        wgt16 = sb("wgt16", [P, TOP])
        early_at = [0]

        def early(n):
            early_at[0] += n
            assert early_at[0] <= NC * P
            return late[:, early_at[0] - n:early_at[0]]

        cond = early(KD * 2)
        scond = early(KD * 2).rearrange("p (k j) -> p k j", k=KD)
        bmod = early(48)
        ng = early(2 * KD)
        mod = early(96).rearrange("p (b j) -> p b j", b=48)
        s12 = early(4 * KD).rearrange("p (n k j) -> p n k j", n=2, k=KD)
        bsp = early(G)
        decay = early(2 * HEADS)
        lg = early(6 * 2 * HEADS).rearrange("p (v n) -> p v n", v=6)
        kdec = early(2 * HEADS)
        gch = early(2 * HEADS)
        colf = early(2)
        ssq = early(2 * NC)
        rms = early(2 * NC)
        rst = early(2 * NC)
        one = sb("one", [P, 12])
        rsum = sb("rsum", [P, 2, PH])
        ps = ctx.enter_context(nc.psum_tensor("ps", [P, 8, 512], F32))

        names = """in_x in_const ring_0 ring_1 mod_0 mod_1 late_in in_gc in_mctx in_pw in_psc in_state in_fg
            in_subk in_wq xo_in state_out y_stored gt2_stored gt2_back y_sum y_sq
            act_full act_emptied dve_full dve_emptied tmp_free
            silu_done mod_done x_squared x_ms x_std x_normed
            ln_var ln_std ln_done pool_consts decay_in lg_exp lg_u lg_ln lg_done exps_done
            mask_done s_init kt_full kd_done sc_full sm_done qd_done o_full o_done kv_full
            state_done o_ms o_std o_ready row_diag merged
            x1_done idx_done row_free dot_done diag_done ls_done exp_done
            gsm_done vacc_full vacc_free y_ms y_std y_done h2_done h2_trans h2T_done h2_sq
            h2_ms h2_std qp_full qp_done qpT_full qpT_done sc2_full sc2_free
            pe_gate act_gate dve_gate pool_gate sp_gate act_step dve_step pool_step""".split()
        s = {n: sem(n) for n in names}
        row_in = [sem(f"row_in_{i}") for i in range(SLOTS)]
        xr_in = [sem(f"xr_in_{i}") for i in range(2)]
        x1_stored = [sem(f"x1_stored_{i}") for i in range(4)]
        x1_in = [sem(f"x1_in_{i}") for i in range(2)]
        ring_in = [s["ring_0"], s["ring_1"]]
        mod_in = [s["mod_0"], s["mod_1"]] + ring_in

        x1d = nc.dram_tensor("x1_scratch", [NC, P, D], F32, kind="Internal").ap()
        gt2d = nc.dram_tensor("gt2_scratch", [P, 2 * D], F32, kind="Internal").ap()
        block = ctx.enter_context(nc.Block())

        def phases(eng_steps, phase, per_pair):
            for p in range(4):
                phase(p, p % 2, p // 2)
            with eng_steps.loop((NC - 6) // 2, per_pair) as m:
                for par in range(2):
                    phase(m * 2 + 4 + par, par, m + 2)
            for p in range(NC - 2, NC + 1):
                phase(p, p % 2, p // 2)

        def does(p):
            if not isinstance(p, int):
                return True, True
            return p < NC, p >= 1

        def hbuf(p, par):
            return rowbc[:, :] if isinstance(p, int) and p == 0 else h2[:, par, :]

        @block.sync
        def _(sp):
            st = Steps(sp, s["sp_gate"], s["sp_gate"])
            def unit(src, slot, used_by, count):
                sp.wait_ge(s[used_by], count)
                sp.dma_start(ring[:, slot].rearrange("p k n -> p (k n)"), src).then_inc(ring_in[slot], 16)

            def mod_unit(n):
                sp.dma_start(mod_slots[n].rearrange("p k n -> p (k n)"), a["wmod"][n]).then_inc(mod_in[n], 16)

            mod_unit(0)
            for c in range(NC):
                sp.dma_start(A[:, c, :], a["x"][c]).then_inc(s["in_x"], 16)
            for n in range(1, 4):
                mod_unit(n)

            def late(m):
                sp.wait_ge(s["dve_full"], D_LATE + m)
                sp.dma_start(late_mod.rearrange("p k n -> p (k n)"), a["wlate"][m]).then_inc(s["late_in"], 16)

            for slot in range(2):
                unit(a["wa"][slot], slot, "dve_full", D_MOD + 3 + slot)
            unit(a["wa"][2], 0, "act_full", T_A + 10)
            late(0)
            for n in range(3, 6):
                unit(a["wa"][n], n % 2, "act_full", T_A + 10 * (n - 1))
                for m in range(4 * n - 11, 4 * n - 7):
                    late(m)
            for m in range(13, 16):
                late(m)
            with sp.Fori(0, HEADS) as h:
                for slot in range(2):
                    unit(a["whead"][h * 2 + slot], slot, "act_full",
                         h * HEAD_TILES + (T_C - (10, 0)[slot]))
                sp.wait_ge(s["act_full"], h * HEAD_TILES + T_C)
                sp.dma_start(gcb.rearrange("p k n -> p (k n)"), a["wgc"][h]).then_inc(s["in_gc"], 16)
                sp.wait_ge(s["dve_emptied"], D_PW)
                for r in range(2):
                    sp.dma_start(S[:, 1, r, 0, :], a["state"][r, h]).then_inc(s["in_state"], 16)
                sp.wait_ge(s["state_done"], h * (2 * NC) + 2 * CC)
                for r in range(2):
                    sp.dma_start(a["new_state"][r, h], S[:, 0, r, 0, :]).then_inc(s["state_out"], 16)
            sp.wait_ge(s["ln_done"], 1)
            sp.dma_start(rowbc[:, :], a["psc"]).then_inc(s["in_psc"], 16)
            unit(a["wz"][0], 0, "act_full", T_Z - 5)
            unit(a["wz"][1], 1, "act_full", T_Z - 5)
            sp.wait_ge(s["act_full"], T_Z)
            sp.dma_start(mctx.rearrange("p g s t -> p (g s t)"), a["mctx"]).then_inc(s["in_mctx"], 16)
            sp.wait_ge(s["sm_done"], HEADS * 2 * NC)
            sp.wait_ge(s["qd_done"], HEADS * 2 * NC)
            sp.dma_start(m8[:, :], a["poolw"]).then_inc(s["in_pw"], 16)
            for g in range(G):
                for half in range(2):
                    unit(a["mlat"][2 * g + half], half, "act_full",
                         T_POOL + 5 * (g - 1) + 3 + 2 * half if g else T_Z + 10 * (half + 1))
            for slot in range(2):
                unit(a["wgb"][slot], slot, "act_full", T_POOL + 5 * (G - 1) + 3 + 2 * slot)
            for slot in range(2):
                unit(a["wout"][slot], slot, "act_full", T_GB + 10 * (slot + 1))
            sp.wait_ge(s["dve_emptied"], D_OUT)
            sp.dma_start(subk, a["subk"]).then_inc(s["in_subk"], 16)
            sp.wait_ge(s["act_emptied"], T_BC + 4)
            sp.dma_start(gt2d, bc[:, 2].rearrange("p j d -> p (j d)")).then_inc(s["gt2_stored"], 16)

            def load_xr(n):
                sp.dma_start(xr[:, n % 2, :], a["x"][n // 2][:, (n % 2) * UW:(n % 2 + 1) * UW]
                             ).then_inc(xr_in[n % 2], 16)

            def store_x1(n):
                sp.wait_ge(s["x1_done"], n + 1)
                sp.dma_start(x1d[n // 2][:, (n % 2) * UW:(n % 2 + 1) * UW],
                             tmp[:, n % 4, :]).then_inc(x1_stored[n % 4], 16)
                if n + 2 < 2 * NC:
                    load_xr(n + 2)

            sp.wait_ge(s["act_emptied"], T_END)
            load_xr(0)
            load_xr(1)
            for k in range(KD):
                sp.dma_start(wq[:, k, :], a["wq"][k]).then_inc(s["in_wq"], 16)
            for n in range(2):
                store_x1(n)
            for n in range(2):
                sp.wait_ge(x1_stored[n], 16)
            sp.dma_start(hbuf(0, 0), x1d[0]).then_inc(x1_in[0], 16)
            for n in range(2, 2 * NC):
                store_x1(n)
            for n in range(4):
                sp.wait_ge(x1_stored[n], 16 * 2 * NC // 4)
            sp.dma_start(bc[:, 2].rearrange("p j d -> p (j d)"), gt2d).then_inc(s["gt2_back"], 16)

            def phase(p, par, k):
                _, rows = does(p)
                if rows:
                    if not isinstance(p, int) or p > 1:
                        sp.wait_ge(s["y_done"], p - 1)
                    sp.dma_start(xo, x1d[p - 1]).then_inc(s["xo_in"], 16)
                if not isinstance(p, int) or p + 1 < NC:
                    if rows:
                        sp.wait_ge(s["dot_done"], p * P)
                    sp.dma_start(h2[:, 1 - par, :], x1d[p + 1]).then_inc(x1_in[1 - par], 16)
                if isinstance(p, int) and p == 1:
                    sp.dma_start(rowbc[:, :], a["fg"]).then_inc(s["in_fg"], 16)
                if rows:
                    sp.wait_ge(s["y_done"], p)
                    sp.dma_start(a["y"][p - 1], yb).then_inc(s["y_stored"], 16)

            phases(st, phase, 0)
            sp.wait_ge(s["y_stored"], 16 * NC)
            sp.wait_ge(s["state_out"], 16 * 2 * HEADS)

        @block.gpsimd
        def _(pool):
            st = Steps(pool, s["pool_step"], s["pool_gate"])
            g = nc.gpsimd
            st.step(g.memset(ident[:, :], 0.0))
            st.step(g.memset(ones[:, :], 1.0))
            st.step(g.memset(zeros[:, :], 0.0))
            st.step(g.iota(relf, [[1, P]], base=0, channel_multiplier=-1,
                           allow_small_or_imprecise_dtypes=True))
            st.step(g.iota(relb, [[-1, P]], base=0, channel_multiplier=1,
                           allow_small_or_imprecise_dtypes=True))
            st.step(g.iota(rowf, [[1, P]], base=1, channel_multiplier=0,
                           allow_small_or_imprecise_dtypes=True))
            st.step(g.iota(rowb, [[-1, P]], base=P, channel_multiplier=0,
                           allow_small_or_imprecise_dtypes=True))
            st.step(g.iota(colf[:, 0:1], [[0, 1]], base=P - 1, channel_multiplier=-1,
                           allow_small_or_imprecise_dtypes=True))
            st.step(g.iota(colf[:, 1:2], [[0, 1]], base=0, channel_multiplier=1,
                           allow_small_or_imprecise_dtypes=True))
            st.step(g.iota(iota16[:, :], [[1, TOP]], base=0, channel_multiplier=0,
                           allow_small_or_imprecise_dtypes=True))
            st.settle()
            st.step(g.affine_select(out=ident[:, :], in_=ident[:, :], compare_op=ALU.not_equal, fill=1.0,
                                    base=0, pattern=[[-1, P]], channel_multiplier=1))
            st.step(g.tensor_scalar(relf, relf, 0.0, None, ALU.max))
            st.step(g.tensor_scalar(relb, relb, 0.0, None, ALU.max))
            st.settle()
            pool.sem_inc(s["pool_consts"], 1)
            pool.wait_ge(s["exps_done"], 1)
            for h in range(HEADS):
                st.step(g.affine_select(out=mask[:, 0, h, :], in_=mask[:, 0, h, :], compare_op=ALU.is_ge,
                                        fill=0.0, base=0, pattern=[[1, P]], channel_multiplier=-1))
                st.step(g.affine_select(out=mask[:, 1, h, :], in_=mask[:, 1, h, :], compare_op=ALU.is_ge,
                                        fill=0.0, base=0, pattern=[[-1, P]], channel_multiplier=1))
            st.settle()
            pool.sem_inc(s["mask_done"], 1)

            pool.wait_ge(s["dve_full"], D_END)

            def phase(p, par, k):
                if not does(p)[1]:
                    return
                st.wait(s["idx_done"], (p - 1) * PH + PH)
                with st.loop(PH // 2, 2) as pair:
                    for odd in range(2):
                        st.link(g.tensor_copy(
                            stage[:, odd, :],
                            idx[:, p - 1, ds(pair * (2 * TOP) + odd * TOP, TOP)]))
                        for j in range(TOP):
                            st.wait(s["row_free"], (p - 1) * P + pair * (2 * TOP) + (odd * TOP + j + 1))
                            g.indirect_dma_start(
                                out=slots[:, j % SLOTS, :], out_offset=None, in_=a["peer"],
                                in_offset=bass.IndirectOffsetOnAxis(ap=stage[:, odd, j:j + 1], axis=0),
                            ).then_inc(row_in[j % SLOTS], 16)

            phases(st, phase, 2 * PH)

        @block.scalar
        def _(eng):
            st = Steps(eng, s["act_step"], s["act_gate"])
            A_ = nc.scalar.activation
            for dst, name in ((cond[:, :], "cond"), (bmod[:, :], "bmod"), (ng[:, :], "ng"),
                              (decay[:, :], "decay"), (rowbc[:, :], "lng"), (mix[:, :], "mix"),
                              (bsp[:, :], "bsp")):
                eng.dma_start(dst, a[name]).then_inc(s["in_const"], 16)
            eng.wait_ge(s["in_const"], 16 * 7)
            A_(scond.rearrange("p k j -> p (k j)"), cond[:, :], ACT.Silu).then_inc(s["silu_done"], 1)

            eng.wait_ge(s["in_x"], 16 * NC)
            for c in range(NC):
                st.step(A_(Z[:, c, :], A[:, c, :], ACT.Square, accum_out=ssq[:, c:c + 1]))
            st.settle()
            eng.sem_inc(s["x_squared"], 1)
            eng.wait_ge(s["x_ms"], 1)
            A_(rms[:, 0:NC], rms[:, NC:2 * NC], ACT.Sqrt).then_inc(s["x_std"], 1)

            def full(t):
                st.wait(s["act_full"], t + 1)

            eng.wait_ge(s["mod_done"], 1)
            for k in range(KD):
                for n, (c0, cn, j) in enumerate(SEGS):
                    t = T_HT + 3 * k + n
                    full(t)
                    A_(hT[:, k, c0 * P:(c0 + cn) * P], ps[:, t % 4, 0:cn * P], ACT.Identity,
                       scale=s12[:, 0, k, j:j + 1], bias=mod[:, k, j:j + 1]).then_inc(s["act_emptied"], 1)

            eng.wait_ge(s["decay_in"], 1)
            A_(lg[:, 1, :], lg[:, 0, :], ACT.Exp, scale=-1.0).then_inc(s["lg_exp"], 1)
            eng.wait_ge(s["lg_u"], 1)
            A_(lg[:, 3, :], lg[:, 2, :], ACT.Ln).then_inc(s["lg_ln"], 1)
            eng.wait_ge(s["lg_done"], 1)
            eng.wait_ge(s["pool_consts"], 1)
            for r in range(2):
                for h in range(HEADS):
                    at = r * HEADS + h
                    col = lg[:, 5, at:at + 1]
                    st.step(A_(mask[:, r, h, :], (relf, relb)[r], ACT.Exp, scale=col))
                    st.step(A_(qdec[:, r, h, :], (rowf, rowb)[r], ACT.Exp, scale=col))
                    st.step(A_(kdec[:, at:at + 1], colf[:, r:r + 1], ACT.Exp, scale=col))
            st.step(A_(gch[:, :], lg[:, 5, :], ACT.Exp, scale=float(P)))
            st.settle()
            eng.sem_inc(s["exps_done"], 1)

            for j in range(2):
                for c in range(NC):
                    t = T_A + j * NC + c
                    full(t)
                    A_(Z[:, c, j * UW:(j + 1) * UW], ps[:, t % 4, :],
                       ACT.Gelu_apprx_tanh).then_inc(s["act_emptied"], 1)
            eng.wait_ge(s["ln_var"], 1)
            A_(rms[:, 0:NC], rms[:, NC:2 * NC], ACT.Sqrt).then_inc(s["ln_std"], 1)
            for j in range(2):
                for c in range(NC):
                    t = T_A + 20 + j * NC + c
                    full(t)
                    A_(A[:, c, j * UW:(j + 1) * UW], ps[:, t % 4, :],
                       ACT.Gelu_apprx_tanh).then_inc(s["act_emptied"], 1)

            def gates(t0, m0, units, func, drain=False):
                for n in range(units * NC):
                    full(t0 + n)
                    if isinstance(m0, int) and m0 + n < 4:
                        pass
                    elif drain and n < 4:
                        st.wait(s["tmp_free"], m0)
                    else:
                        st.wait(s["tmp_free"], m0 + n - 3)
                    bank = (t0 + n) % 4 if isinstance(t0, int) else None
                    A_(tmp[:, n % 4, :], ps[:, bank, :], func).then_inc(s["act_emptied"], 1)

            gates(T_A + 40, TMP_A, 2, ACT.Sigmoid)

            per_scan = NC * 2
            with st.loop(HEADS, 0) as h:
                base = h * HEAD_TILES + T_C
                eng.wait_ge(s["dve_emptied"], D_PW)
                st.wait(s["tmp_free"], h * TMP_HEAD + TMP_C)
                for n in range(6):
                    c0, cn, _ = SEGS[n % 3]
                    full(base + n)
                    if n < 3:
                        A_(qT[:, c0 * P:(c0 + cn) * P], ps[:, n % 4, 0:cn * P],
                           ACT.Copy).then_inc(s["act_emptied"], 1)
                    else:
                        A_(kT[:, c0 * P:(c0 + cn) * P], ps[:, n % 4, 0:cn * P],
                           ACT.Copy, scale=float(DK ** -0.5)).then_inc(s["act_emptied"], 1)
                for n in range(6, 11):
                    c = 2 * (n - 6)
                    full(base + n)
                    A_(vv[:, c:c + 2, :], ps[:, n % 4, :].rearrange("p (c d) -> p c d", c=2),
                       ACT.Copy).then_inc(s["act_emptied"], 1)
                for it in range(NC):
                    for r in range(2):
                        n = h * per_scan + (2 * it + r)
                        st.wait(s["kt_full"], n + 1)
                        if it >= 1:
                            st.wait(s["kv_full"], n - 1)
                        A_(kd[:, r, :], ps[:, r, 0:P], ACT.Copy,
                           scale=kdec[:, ds(h + r * HEADS, 1)]).then_inc(s["kd_done"], 1)
                    for r in range(2):
                        n = h * per_scan + (2 * it + r)
                        c = scan_chunk(it, r)
                        st.wait(s["o_full"], n + 1)
                        A_(O[:, c, r, :], ps[:, 2 + r, 0:DV], ACT.Copy)
                        A_(ps[:, 2 + r, 0:DV], ps[:, 2 + r, 0:DV], ACT.Square,
                           accum_out=ssq[:, 2 * c + r:2 * c + r + 1]).then_inc(s["o_done"], 1)
                st.wait(s["o_ms"], h + 1)
                A_(rms[:, :], rms[:, :], ACT.Sqrt).then_inc(s["o_std"], 1)
                for n in range(15):
                    loc = 11 + n
                    full(base + loc)
                    if n >= 4:
                        st.wait(s["tmp_free"], h * TMP_HEAD + (TMP_C + n - 3))
                    A_(tmp[:, n % 4, :], ps[:, loc % 4, :],
                       ACT.Silu if n < 10 else ACT.Sigmoid).then_inc(s["act_emptied"], 1)

            eng.wait_ge(s["o_ready"], 1)
            eng.wait_ge(s["state_out"], 16 * 2 * HEADS)
            for n in range(20):
                full(T_Z + n)
                A_(Z[:, n % NC, (n // NC) * UW:(n // NC + 1) * UW], ps[:, n % 4, :],
                   ACT.Copy).then_inc(s["act_emptied"], 1)
            for g in range(G):
                for n in range(5):
                    full(T_POOL + 5 * g + n)
                    if n == 0 and g:
                        st.wait(s["dve_full"], D_PW + 5 * g)
                    src = ps[:, (T_POOL + 5 * g + n) % 4, :]
                    if n == 0:
                        dst, src = PT[:, :, 0:CTX], src.rearrange("p (b t) -> p b t", b=2)
                    else:
                        half, b = (n - 1) // 2, (n - 1) % 2
                        dst = PT[:, b, CTX + half * UW:CTX + (half + 1) * UW]
                    A_(dst, src, ACT.Copy).then_inc(s["act_emptied"], 1)
            gates(T_GB, TMP_GB, 2, ACT.Sigmoid, drain=True)

            st.wait(s["tmp_free"], TMP_GB + 20)
            for n in range(16):
                v, j, half = n // 4, (n // 2) % 2, n % 2
                full(T_BC + n)
                if n == 12:
                    eng.wait_ge(s["gt2_stored"], 16)
                dst = bc[:, (2, 0, 1, 2)[v], j, half * UW:(half + 1) * UW]
                A_(dst, ps[:, n % 4, :], ACT.Copy).then_inc(s["act_emptied"], 1)
            for k in range(KD):
                for n, (c0, cn, _) in enumerate(SEGS):
                    t = T_MT + 3 * k + n
                    full(t)
                    A_(hT[:, k, c0 * P:(c0 + cn) * P], ps[:, t % 4, 0:cn * P],
                       ACT.Copy).then_inc(s["act_emptied"], 1)

            eng.sem_inc(s["qp_done"], 1)
            eng.sem_inc(s["qpT_done"], 1)
            eng.wait_ge(s["dve_emptied"], D_OUT)

            def phase(p, par, k):
                prep, rows = does(p)
                if prep:
                    st.wait(x1_in[par], (k + 1) * 16)
                    st.wait(s["h2_done"], p)
                    for half in range(2):
                        A_(ps[:, 6 + half, :], hbuf(p, par)[:, half * UW:(half + 1) * UW], ACT.Square,
                           accum_out=one[:, half:half + 1]).then_inc(s["h2_sq"], 1)
                    st.wait(s["h2_ms"], p + 1)
                    A_(one[:, 3:4], one[:, 2:3], ACT.Sqrt).then_inc(s["h2_std"], 1)
                    for half in range(2):
                        st.wait(s["h2_trans"], p * 2 + (half + 1))
                        A_(h2T[:, 4 * half:4 * half + 4, :],
                           ps[:, 6 + half, :].rearrange("p (k t) -> p k t", k=4),
                           ACT.Copy).then_inc(s["h2T_done"], 1)
                if rows:
                    st.wait(s["gsm_done"], p)

                def weights(hd, j0, j1):
                    for j in range(j0, j1):
                        n = (p - 1) * P + hd * TOP + j
                        st.wait(s["dot_done"], n + 1)
                        st.link(A_(gelu16[:, j:j + 1], dot16[:, j:j + 1], ACT.Gelu_apprx_tanh))
                        st.link(A_(wgt16[:, j:j + 1], gelu16[:, j:j + 1], ACT.Copy,
                                   scale=gsm[:, ds(hd * TOP + j, 1)]))
                        st.wait(s["row_free"], n + 1)
                        A_(diag[:, j % SLOTS, :], ident[:, :], ACT.Copy,
                           scale=wgt16[:, j:j + 1]).then_inc(s["diag_done"], 1)

                with st.loop(PH, 2 * TOP * rows) as hd:
                    if rows:
                        weights(hd, 0, 2)
                    if prep:
                        st.wait(s["qp_full"], p * PH + hd + 1)
                        A_(qp, ps[:, 2, 0:256], ACT.Copy).then_inc(s["qp_done"], 1)
                    if rows:
                        weights(hd, 2, 4)
                    if prep:
                        st.wait(s["qpT_full"], p * PH + hd + 1)
                        A_(qpT.rearrange("p s t -> p (s t)"), ps[:, 3, 0:256],
                           ACT.Copy).then_inc(s["qpT_done"], 1)
                    if rows:
                        weights(hd, 4, TOP)
                if prep:
                    st.wait(s["ls_done"], p + 1)
                    A_(expd, expd, ACT.Exp).then_inc(s["exp_done"], 1)
                if rows:
                    st.wait(s["y_sum"], p)
                    A_(xo, yb, ACT.Square, accum_out=one[:, 4:5]).then_inc(s["y_sq"], 1)
                    st.wait(s["y_ms"], p)
                    A_(one[:, 7:8], one[:, 6:7], ACT.Sqrt).then_inc(s["y_std"], 1)

            phases(st, phase, 2 * PH * 2 * TOP)

        @block.tensor
        def _(pe):
            st = Steps(pe, s["pe_gate"], s["pe_gate"])
            mm = nc.tensor.matmul

            def group(out, pairs):
                for n, (lhs, rhs) in enumerate(pairs):
                    last = mm(out, lhs, rhs, start=n == 0, stop=n == len(pairs) - 1)
                return last

            def unit_in(slot, pair):
                st.wait(ring_in[slot], (pair + 1) * 16)

            def act_tile(t, n=None, drain=False):
                if isinstance(t, int) and t < 4:
                    return
                st.wait(s["act_emptied"], t if drain else t - 3)

            def dve_tile(t):
                if isinstance(t, int) and t < 4:
                    return
                st.wait(s["dve_emptied"], t - 3)

            def transposed(src, t0):
                for k in range(KD):
                    for n, (c0, cn, _) in enumerate(SEGS):
                        t = t0 + 3 * k + n
                        act_tile(t)
                        for c in range(cn):
                            last = nc.tensor.transpose(ps[:, t % 4, c * P:(c + 1) * P],
                                                       src[:, c0 + c, k * P:(k + 1) * P], ident[:, :])
                        last.then_inc(s["act_full"], 1)

            def project(t0, pair, drain=False, late=None):
                for slot in range(2):
                    unit_in(slot, pair)
                    for c in range(NC):
                        n = slot * NC + c
                        if drain and n < 4:
                            act_tile(t0, drain=True)
                        else:
                            act_tile(t0 + n)
                        last = group(ps[:, n % 4, :],
                                     [(hT[:, k, c * P:(c + 1) * P], ring[:, slot, k, :])
                                      for k in range(KD)])
                        last.then_inc(s["act_full"], 1)
                        if late is not None and c in LATE_AFTER:
                            m = 4 * slot + LATE_AFTER.index(c)
                            st.wait(s["late_in"], late * 128 + 16 * (m + 1))
                            st.wait(s["dve_emptied"], late * 8 + (D_LATE + m - 3))
                            for b in range(2):
                                last = group(ps[:, 4 + m % 4, 2 * b:2 * b + 2],
                                             [(late_mod[:, k, b * P:(b + 1) * P], scond[:, k, :])
                                              for k in range(KD)])
                            last.then_inc(s["dve_full"], 1)

            pe.wait_ge(s["silu_done"], 1)
            for n in range(4):
                st.wait(mod_in[n], 16)
                for b in range(4):
                    last = group(ps[:, 4 + n % 4, 2 * b:2 * b + 2],
                                 [(mod_slots[n][:, k, b * P:(b + 1) * P], scond[:, k, :])
                                  for k in range(KD)])
                last.then_inc(s["dve_full"], 1)
            pe.wait_ge(s["pool_consts"], 1)
            pe.wait_ge(s["x_normed"], 1)
            transposed(A, T_HT)
            pe.wait_ge(s["act_emptied"], T_A)
            project(T_A, U_A // 2)
            with st.loop(2, 0) as i:
                project(i * 20 + (T_A + 20), i + (U_A // 2 + 1), late=i)
            pe.wait_ge(s["ln_done"], 1)
            for c in range(NC):
                for j in range(2):
                    t = D_MIX + 2 * c + j
                    dve_tile(t)
                    for b in range(2):
                        g = 2 * j + b
                        last = mm(ps[:, 4 + t % 4, b * GW:(b + 1) * GW], mix[:, g * P:(g + 1) * P],
                                  Z[:, c, g * GW:(g + 1) * GW], start=True, stop=True)
                    last.then_inc(s["dve_full"], 1)
            pe.wait_ge(s["dve_emptied"], D_PW)
            with st.loop(HEADS, 0) as h:
                base = h * HEAD_TILES + T_C
                sbase = h * (2 * NC)
                unit_in(0, h + U_HEAD // 2)
                for n in range(6):
                    c0, cn, _ = SEGS[n % 3]
                    act_tile(base if n < 4 else base + n, drain=n < 4)
                    group(ps[:, n % 4, 0:cn * P],
                          [(ring[:, 0, k, (n // 3) * P:(n // 3 + 1) * P], hT[:, k, c0 * P:(c0 + cn) * P])
                           for k in range(KD)]).then_inc(s["act_full"], 1)
                for n in range(6, 11):
                    act_tile(base + n)
                    for c in (2 * (n - 6), 2 * (n - 6) + 1):
                        last = group(ps[:, n % 4, (c % 2) * DV:(c % 2 + 1) * DV],
                                     [(hT[:, k, c * P:(c + 1) * P], ring[:, 0, k, 2 * P:4 * P])
                                      for k in range(KD)])
                    last.then_inc(s["act_full"], 1)
                st.wait(s["act_emptied"], base + 11)
                for it in range(NC):
                    for r in range(2):
                        n = sbase + (2 * it + r)
                        c = scan_chunk(it, r)
                        if it >= 1:
                            st.wait(s["kd_done"], n - 1)
                        nc.tensor.transpose(ps[:, r, 0:P], kT[:, c * P:(c + 1) * P],
                                            ident[:, :]).then_inc(s["kt_full"], 1)
                        if it >= 1:
                            st.wait(s["sm_done"], n - 1)
                        mm(ps[:, 4 + r, 0:P], kT[:, c * P:(c + 1) * P], qT[:, c * P:(c + 1) * P],
                           start=True, stop=True).then_inc(s["sc_full"], 1)
                    for r in range(2):
                        n = sbase + (2 * it + r)
                        c = scan_chunk(it, r)
                        seg = 0 if it < CC else 1
                        st.wait(s["sm_done"], n + 1)
                        st.wait(s["qd_done"], n + 1)
                        if it == 0:
                            st.wait(s["s_init"], h + 1)
                        elif it == CC:
                            st.wait(s["in_state"], (h + 1) * 32)
                        if it >= 1:
                            st.wait(s["state_done"], n - 1)
                            st.wait(s["o_done"], n - 1)
                        mm(ps[:, 2 + r, 0:DV], sm[:, r, :], vv[:, c, :], start=True, stop=False)
                        mm(ps[:, 2 + r, 0:DV], qd[:, r, :], S[:, seg, r, it % 2, :],
                           start=False, stop=True).then_inc(s["o_full"], 1)
                        st.wait(s["kd_done"], n + 1)
                        mm(ps[:, 6 + r, 0:DV], kd[:, r, :], vv[:, c, :],
                           start=True, stop=True).then_inc(s["kv_full"], 1)
                st.wait(s["kd_done"], sbase + 2 * NC)
                st.wait(s["o_done"], sbase + 2 * NC)
                st.wait(s["state_done"], sbase + 2 * NC)
                unit_in(1, h + U_HEAD // 2)
                for c in range(NC):
                    n = 11 + c
                    if c >= 4:
                        act_tile(base + n)
                    group(ps[:, n % 4, :], [(hT[:, k, c * P:(c + 1) * P], ring[:, 1, k, :])
                                            for k in range(KD)]).then_inc(s["act_full"], 1)
                st.wait(s["in_gc"], (h + 1) * 16)
                for n in range(21, 26):
                    act_tile(base + n)
                    for c in (2 * (n - 21), 2 * (n - 21) + 1):
                        last = group(ps[:, n % 4, (c % 2) * DV:(c % 2 + 1) * DV],
                                     [(hT[:, k, c * P:(c + 1) * P], gcb[:, k, :]) for k in range(KD)])
                    last.then_inc(s["act_full"], 1)
            project(T_Z, U_Z // 2, drain=True)
            pe.wait_ge(s["act_emptied"], T_POOL)
            pe.wait_ge(s["in_mctx"], 16)
            pe.wait_ge(s["in_pw"], 16)
            pe.wait_ge(s["state_done"], HEADS * 2 * NC)
            for g in range(G):
                t = T_POOL + 5 * g
                act_tile(t)
                for b in range(2):
                    ch = slice(g * GW + b * P, g * GW + (b + 1) * P)
                    last = group(ps[:, t % 4, b * CTX:(b + 1) * CTX],
                                 [(Z[:, c, ch], mctx[:, g, c, :]) for c in range(CC)])
                last.then_inc(s["act_full"], 1)
                for half in range(2):
                    unit_in(half, U_POOL // 2 + g)
                    for b in range(2):
                        t = T_POOL + 5 * g + 1 + 2 * half + b
                        ch = slice(g * GW + b * P, g * GW + (b + 1) * P)
                        act_tile(t)
                        group(ps[:, t % 4, :],
                              [(Z[:, CC + c, ch], ring[:, half, c, :]) for c in pool_sources(g, half)]
                              ).then_inc(s["act_full"], 1)
                pe.wait_ge(s["act_emptied"], T_POOL + 5 * g + 5)
                for n in range(5):
                    t = D_PW + 5 * g + n
                    dve_tile(t)
                    for c in (2 * n, 2 * n + 1):
                        last = group(ps[:, 4 + t % 4, (c % 2) * GW:(c % 2 + 1) * GW],
                                     [(PT[:, b, c * P:(c + 1) * P], pw[:, g, b, :]) for b in range(2)])
                    last.then_inc(s["dve_full"], 1)
            project(T_GB, U_GB // 2)
            for n in range(16):
                act_tile(T_BC + n)
                pe.wait_ge(s["row_diag"], n + 1)
                mm(ps[:, n % 4, :], ones[:, :], tmp[:, n % 4, :], start=True,
                   stop=True).then_inc(s["act_full"], 1)
            pe.wait_ge(s["merged"], 1)
            transposed(A, T_MT)
            pe.wait_ge(s["act_emptied"], T_END)

            def out_chunk(c):
                for j in range(2):
                    n = 2 * c + j
                    if n >= 2:
                        st.wait(s["dve_emptied"], D_OUT + n - 1)
                    group(ps[:, j, :], [(hT[:, k, c * P:(c + 1) * P], ring[:, j, k, :])
                                        for k in range(KD)]).then_inc(s["dve_full"], 1)

            for j in range(2):
                unit_in(j, U_OUT // 2)
            for c in range(CC):
                out_chunk(c)

            pe.sem_inc(s["row_free"], SLOTS)
            pe.wait_ge(s["in_wq"], 16 * KD)
            pe.wait_ge(s["in_subk"], 16)
            pe.wait_ge(s["dve_emptied"], D_OUT)

            def phase(p, par, k):
                prep, rows = does(p)
                if rows:
                    st.wait(s["dve_emptied"], D_END)
                    st.wait(s["vacc_free"], p - 1)
                    for half in range(2):
                        mm(ps[:, half, :], ident[:, :], zeros[:, :], start=True, stop=False)
                if prep:
                    st.wait(s["h2_done"], p + 1)
                    st.wait(s["h2T_done"], p * 2)
                    for k in range(KD):
                        last = nc.tensor.transpose(ps[:, 6 + k // 4, (k % 4) * P:(k % 4 + 1) * P],
                                                   hbuf(p, par)[:, k * P:(k + 1) * P], ident[:, :])
                        if k % 4 == 3:
                            last.then_inc(s["h2_trans"], 1)
                    st.wait(s["h2T_done"], p * 2 + 2)

                def sum_rows(hd, j0, j1):
                    for j in range(j0, j1):
                        st.wait(s["diag_done"], (p - 1) * P + hd * TOP + (j + 1))
                        for half in range(2):
                            last = mm(ps[:, half, :], diag[:, j % SLOTS, :],
                                      slots[:, j % SLOTS, D + half * UW:D + (half + 1) * UW],
                                      start=False, stop=False)
                        last.then_inc(s["row_free"], 1)

                def head(hd, odd):
                    n = p * PH + hd
                    if prep:
                        st.wait(s["qp_done"], n + 1)
                        group(ps[:, 2, 0:256], [(h2T[:, k, :], wq[:, k, ds(hd * 256, 256)])
                                                for k in range(KD)]).then_inc(s["qp_full"], 1)
                    if rows:
                        sum_rows(hd, 0, 2)
                    else:
                        out_chunk(CC + hd)
                    if prep:
                        st.wait(s["qp_done"], n + 2)
                        st.wait(s["qpT_done"], n + 1)
                        for side in range(2):
                            last = nc.tensor.transpose(ps[:, 3, side * P:(side + 1) * P],
                                                       qp[:, side * P:(side + 1) * P], ident[:, :])
                        last.then_inc(s["qpT_full"], 1)
                    if rows:
                        sum_rows(hd, 2, 4)
                    if prep:
                        st.wait(s["qpT_done"], n + 2)
                        st.wait(s["sc2_free"], n + 1)
                        for side in range(2):
                            last = mm(ps[:, 4 + odd, side * NK:(side + 1) * NK], qpT[:, side, :],
                                      subk[:, ds(hd * 256 + side * NK, NK)], start=True, stop=True)
                        last.then_inc(s["sc2_full"], 1)
                    if rows:
                        sum_rows(hd, 4, TOP)

                if not rows:
                    for hd in range(PH):
                        head(hd, hd % 2)
                else:
                    with st.loop(PH // 2, 0) as pair:
                        for odd in range(2):
                            head(pair * 2 + odd, odd)
                if rows:
                    for half in range(2):
                        last = mm(ps[:, half, :], ident[:, :], zeros[:, :], start=False, stop=True)
                    last.then_inc(s["vacc_full"], 1)

            phases(st, phase, 0)

        @block.vector
        def _(dve):
            st = Steps(dve, s["dve_step"], s["dve_gate"])
            v = nc.vector

            def full(t):
                st.wait(s["dve_full"], t + 1)

            dve.wait_ge(s["in_const"], 16 * 7)
            dve.wait_ge(s["x_squared"], 1)
            v.tensor_scalar(rms[:, NC:2 * NC], ssq[:, 0:NC], 1.0 / D, EPS, ALU.mult,
                            ALU.add).then_inc(s["x_ms"], 1)
            dve.wait_ge(s["x_std"], 1)
            st.link(v.reciprocal(rst[:, 0:NC], rms[:, 0:NC]))
            for c in range(NC):
                st.step(v.tensor_scalar(A[:, c, :], A[:, c, :], rst[:, c:c + 1], None, ALU.mult))
            st.settle()
            dve.sem_inc(s["x_normed"], 1)

            def mod_columns(t, at, blocks):
                full(t)
                v.tensor_tensor(mod[:, at:at + blocks, :],
                                ps[:, 4 + t % 4, 0:2 * blocks].rearrange("p (b j) -> p b j", b=blocks),
                                bmod[:, at:at + blocks].unsqueeze(2).to_broadcast([P, blocks, 2]),
                                ALU.add).then_inc(s["dve_emptied"], 1)

            def scaled_norm(n):
                st.link(v.scalar_tensor_tensor(
                    out=s12[:, n], in0=mod[:, 8 + 24 * n:16 + 24 * n, :], scalar=1.0,
                    in1=ng[:, 8 * n:8 * n + 8].unsqueeze(2).to_broadcast([P, KD, 2]),
                    op0=ALU.add, op1=ALU.mult))

            def late_columns(m):
                mod_columns(D_LATE + m, 16 + 2 * m, 2)

            for t in range(4):
                mod_columns(D_MOD + t, 4 * t, 4)
            dve.wait_ge(s["dve_emptied"], D_LATE)
            scaled_norm(0)
            dve.sem_inc(s["mod_done"], 1)

            dve.wait_ge(s["in_const"], 16 * 7)
            st.link(v.tensor_scalar(lg[:, 4, :], decay[:, :], -1.0, None, ALU.mult))
            st.link(v.tensor_tensor(lg[:, 0, :], lg[:, 4, :], decay[:, :], ALU.max))
            dve.sem_inc(s["decay_in"], 1)
            dve.wait_ge(s["lg_exp"], 1)
            st.link(v.tensor_scalar(lg[:, 2, :], lg[:, 1, :], 1.0, None, ALU.add))
            dve.sem_inc(s["lg_u"], 1)
            st.link(v.tensor_scalar(lg[:, 4, :], lg[:, 2, :], 1.0, None, ALU.subtract))
            st.link(v.tensor_tensor(lg[:, 4, :], lg[:, 1, :], lg[:, 4, :], ALU.subtract))
            st.link(v.reciprocal(lg[:, 0, :], lg[:, 2, :]))
            st.link(v.tensor_tensor(lg[:, 4, :], lg[:, 4, :], lg[:, 0, :], ALU.mult))
            dve.wait_ge(s["lg_ln"], 1)
            st.link(v.tensor_tensor(lg[:, 4, :], lg[:, 4, :], lg[:, 3, :], ALU.add))
            st.link(v.tensor_scalar(lg[:, 0, :], decay[:, :], 0.0, None, ALU.min))
            st.link(v.tensor_tensor(lg[:, 5, :], lg[:, 0, :], lg[:, 4, :], ALU.subtract))
            dve.sem_inc(s["lg_done"], 1)

            for j in range(2):
                for c in range(NC):
                    dve.wait_ge(s["act_emptied"], T_A + j * NC + c + 1)
                    st.step(v.bn_stats(bst[:, c, 6 * j:6 * j + 6], Z[:, c, j * UW:(j + 1) * UW]))
            st.settle()
            for c in range(NC):
                st.step(v.bn_aggr(mv[:, c, :], bst[:, c, :]))
            st.settle()
            v.tensor_scalar(rms[:, NC:2 * NC], mv[:, :, 1], EPS, None, ALU.add).then_inc(s["ln_var"], 1)
            dve.wait_ge(s["ln_std"], 1)
            st.link(v.reciprocal(rst[:, 0:NC], rms[:, 0:NC]))
            for c in range(NC):
                st.step(v.tensor_scalar(Z[:, c, :], Z[:, c, :], mv[:, c, 0:1], rst[:, c:c + 1],
                                        ALU.subtract, ALU.mult))
            st.settle()
            for c in range(NC):
                st.step(v.tensor_tensor(Z[:, c, :], Z[:, c, :], rowbc[:, :], ALU.mult))
            st.settle()
            dve.sem_inc(s["ln_done"], 1)
            for m in range(8):
                late_columns(m)
            for n in range(20):
                j, c = n // NC, n % NC
                dve.wait_ge(s["act_emptied"], T_A + 40 + n + 1)
                dst = A[:, c, j * UW:(j + 1) * UW]
                v.tensor_tensor(dst, dst, tmp[:, n % 4, :], ALU.mult).then_inc(s["tmp_free"], 1)
                if c in LATE_AFTER:
                    late_columns(8 + 4 * j + LATE_AFTER.index(c))
            dve.wait_ge(s["tmp_free"], 20)
            dve.wait_ge(s["dve_emptied"], D_MIX)
            scaled_norm(1)
            for c in range(NC):
                for j in range(2):
                    t = D_MIX + 2 * c + j
                    full(t)
                    for b in range(2):
                        g = 2 * j + b
                        dst = A[:, c, g * GW:(g + 1) * GW]
                        last = v.scalar_tensor_tensor(out=dst, in0=ps[:, 4 + t % 4, b * GW:(b + 1) * GW],
                                                      scalar=bsp[:, g:g + 1], in1=dst,
                                                      op0=ALU.add, op1=ALU.mult)
                    last.then_inc(s["dve_emptied"], 1)

            dve.wait_ge(s["dve_emptied"], D_PW)
            dve.wait_ge(s["mask_done"], 1)
            with st.loop(HEADS, 1 + NC + NC // 2) as h:
                base = h * HEAD_TILES + T_C
                sbase = h * (2 * NC)
                for r in range(2):
                    last = v.memset(S[:, 0, r, 0, :], 0.0)
                last.then_inc(s["s_init"], 1)
                st.wait(s["act_emptied"], base + 6)
                for it in range(NC):
                    for r in range(2):
                        n = sbase + (2 * it + r)
                        c = scan_chunk(it, r)
                        if it >= 1:
                            st.wait(s["o_full"], n - 1)
                        at = ds(h + r * HEADS, 1)
                        v.tensor_tensor(qd[:, r, :], qT[:, c * P:(c + 1) * P],
                                        m8[:, ds(h * P + (D + r * HEADS * P), P)],
                                        ALU.mult).then_inc(s["qd_done"], 1)
                        st.wait(s["sc_full"], n + 1)
                        v.tensor_tensor(sm[:, r, :], ps[:, 4 + r, 0:P],
                                        m8[:, ds(h * P + r * HEADS * P, P)],
                                        ALU.mult).then_inc(s["sm_done"], 1)
                    for r in range(2):
                        n = sbase + (2 * it + r)
                        seg = 0 if it < CC else 1
                        st.wait(s["kv_full"], n + 1)
                        if it == 0:
                            st.wait(s["s_init"], h + 1)
                        elif it == CC:
                            st.wait(s["in_state"], (h + 1) * 32)
                        else:
                            st.wait(s["state_done"], n - 1)
                        v.scalar_tensor_tensor(out=S[:, seg, r, (it + 1) % 2, :],
                                               in0=S[:, seg, r, it % 2, :],
                                               scalar=gch[:, ds(h + r * HEADS, 1)],
                                               in1=ps[:, 6 + r, 0:DV], op0=ALU.mult,
                                               op1=ALU.add).then_inc(s["state_done"], 1)
                st.wait(s["o_done"], sbase + 2 * NC)
                v.tensor_scalar(rms[:, :], ssq[:, :], 1.0 / DV, EPS, ALU.mult,
                                ALU.add).then_inc(s["o_ms"], 1)
                st.wait(s["o_std"], h + 1)
                st.link(v.reciprocal(rst[:, :], rms[:, :]))
                for c in range(NC):
                    st.wait(s["act_emptied"], base + (11 + c + 1))
                    for r in range(2):
                        last = v.scalar_tensor_tensor(
                            out=O[:, c, r, :], in0=O[:, c, r, :], scalar=rst[:, 2 * c + r:2 * c + r + 1],
                            in1=tmp[:, c % 4, r * DV:(r + 1) * DV], op0=ALU.mult, op1=ALU.mult)
                    last.then_inc(s["tmp_free"], 1)
                    st.wait(s["tmp_free"], h * TMP_HEAD + (TMP_C + c + 1))
                    st.step(v.tensor_tensor(O[:, c, 0, :], O[:, c, 0, :], O[:, c, 1, :], ALU.add))
                st.settle()
                for n in range(5):
                    c = 2 * n
                    slot = (10 + n) % 4
                    st.wait(s["act_emptied"], base + (21 + n + 1))
                    dst = A[:, c:c + 2, ds(h * DV, DV)]
                    gate = tmp[:, slot, :].rearrange("p (c d) -> p c d", c=2)
                    v.tensor_tensor(O[:, c:c + 2, 0, :], O[:, c:c + 2, 0, :], gate,
                                    ALU.mult).then_inc(s["tmp_free"], 1)
                    st.wait(s["tmp_free"], h * TMP_HEAD + (TMP_C + 10 + n + 1))
                    st.step(v.tensor_tensor(dst, dst, O[:, c:c + 2, 0, :], ALU.add))
                st.wait(s["state_out"], h * 32 + 32)
            st.settle()
            dve.sem_inc(s["o_ready"], 1)

            dve.wait_ge(s["in_psc"], 16)
            for g in range(G):
                for n in range(5):
                    t = D_PW + 5 * g + n
                    full(t)
                    scale = rowbc[:, g * GW:(g + 1) * GW].unsqueeze(1).to_broadcast([P, 2, GW])
                    v.tensor_tensor(Z[:, 2 * n:2 * n + 2, g * GW:(g + 1) * GW],
                                    ps[:, 4 + t % 4, :].rearrange("p (c d) -> p c d", c=2),
                                    scale, ALU.mult).then_inc(s["dve_emptied"], 1)
            dve.wait_ge(s["dve_emptied"], D_OUT)
            for n in range(20):
                j, c = n // NC, n % NC
                dve.wait_ge(s["act_emptied"], T_GB + n + 1)
                gate, dst = tmp[:, n % 4, :], A[:, c, j * UW:(j + 1) * UW]
                st.link(v.tensor_tensor(gate, gate, Z[:, c, j * UW:(j + 1) * UW], ALU.mult))
                v.tensor_tensor(dst, dst, gate, ALU.add).then_inc(s["tmp_free"], 1)
            dve.wait_ge(s["tmp_free"], TMP_GB + 20)
            dve.sem_inc(s["merged"], 1)

            for n in range(16):
                vec, j, half = n // 4, (n // 2) % 2, n % 2
                b0 = 4 * half
                src = (mod[:, 40 + b0:44 + b0, j], s12[:, 1, b0:b0 + 4, j],
                       mod[:, 24 + b0:28 + b0, j], mod[:, 16 + b0:20 + b0, j])[vec]
                if n >= 4:
                    dve.wait_ge(s["act_full"], T_BC + n - 3)
                v.tensor_tensor(tmp[:, n % 4, :].rearrange("p (b n) -> p b n", b=4),
                                ident[:, :].unsqueeze(1).to_broadcast([P, 4, P]),
                                src.unsqueeze(2).to_broadcast([P, 4, P]),
                                ALU.mult).then_inc(s["row_diag"], 1)

            dve.wait_ge(s["act_emptied"], T_END)

            def x1_tile(n):
                c, j = n // 2, n % 2
                full(D_OUT + n)
                if n >= 4:
                    dve.wait_ge(x1_stored[n % 4], 16 * (n // 4))
                slot = tmp[:, n % 4, :]
                v.tensor_tensor(slot, ps[:, j, :], bc[:, 2, 0 if c < CC else 1, j * UW:(j + 1) * UW],
                                ALU.mult).then_inc(s["dve_emptied"], 1)
                dve.wait_ge(s["dve_emptied"], D_OUT + n + 1)
                dve.wait_ge(xr_in[n % 2], 16 * (n // 2 + 1))
                v.tensor_tensor(slot, slot, xr[:, n % 2, :], ALU.add).then_inc(s["x1_done"], 1)

            for n in range(2 * CC):
                x1_tile(n)

            dve.sem_inc(s["sc2_free"], 2)

            def top16(values, spare, out_v, out_i):
                st.link(v.max(out_v[:, 0:8], values))
                st.step(v.max_index(out_i[:, 0:8], out_v[:, 0:8], values))
                st.link(v.match_replace(spare, out_v[:, 0:8], values, LOWEST))
                st.link(v.max(out_v[:, 8:16], spare))
                st.link(v.max_index(out_i[:, 8:16], out_v[:, 8:16], spare))

            def dots_of(p, par, hd, j0, j1):
                last_h2 = rowbc[:, :] if isinstance(p, int) and p == 1 else h2[:, 1 - par, :]
                for j in range(j0, j1):
                    st.wait(row_in[j % SLOTS], ((p - 1) * (P // SLOTS) + hd * 2 + (j // SLOTS + 1)) * 16)
                    row = slots[:, j % SLOTS, 0:D]
                    v.tensor_tensor_reduce(out=row, in0=row, in1=last_h2, scale=1.0, scalar=0.0,
                                           op0=ALU.mult, op1=ALU.add,
                                           accum_out=dot16[:, j:j + 1]).then_inc(s["dot_done"], 1)

            def side_top(p, hd, odd, side):
                st.wait(s["sc2_full"], p * PH + hd + 1)
                top16(ps[:, 4 + odd, side * NK:(side + 1) * NK], rest, tv[:, side, :], ti[:, side, :])
                if side:
                    dve.sem_inc(s["sc2_free"], 1)

            def square_top(hd):
                st.step(v.tensor_copy(tf[:, :, :], ti[:, :, :]))
                st.link(v.tensor_tensor(cand, tv[:, 0, :].unsqueeze(2).to_broadcast([P, TOP, TOP]),
                                        tv[:, 1, :].unsqueeze(1).to_broadcast([P, TOP, TOP]), ALU.add))
                flat = cand.rearrange("p a b -> p (a b)")
                top16(flat, cand2, bv[:, :], bp[:, :])
                st.step(v.tensor_copy(logit[:, ds(hd * TOP, TOP)], bv[:, :]))

            def expert_numbers(p, hd):
                st.step(v.tensor_scalar(ab[:, 0, :], bp[:, :], 4, None, ALU.logical_shift_right))
                st.link(v.tensor_scalar(ab[:, 1, :], bp[:, :], 15, None, ALU.bitwise_and))
                st.link(v.tensor_copy(abf[:, :, :], ab[:, :, :]))
                st.link(v.tensor_tensor(hot, abf[:, :, :].unsqueeze(3).to_broadcast([P, 2, TOP, TOP]),
                                        iota16[:, :].unsqueeze(1).unsqueeze(1).to_broadcast(
                                            [P, 2, TOP, TOP]), ALU.is_equal))
                st.link(v.tensor_tensor(hot, hot, tf[:, :, :].unsqueeze(2).to_broadcast([P, 2, TOP, TOP]),
                                        ALU.mult))
                st.link(v.tensor_reduce(picked[:, :, :], hot, AX.X, ALU.add))
                v.scalar_tensor_tensor(out=idx[:, p, ds(hd * TOP, TOP)], in0=picked[:, 0, :],
                                       scalar=float(NK), in1=picked[:, 1, :], op0=ALU.mult,
                                       op1=ALU.add).then_inc(s["idx_done"], 1)
                st.wait(s["idx_done"], p * PH + hd + 1)

            def phase(p, par, k):
                prep, rows = does(p)
                j = 1 if not isinstance(p, int) else (0 if p < CC else 1)
                if prep:
                    st.wait(s["h2_sq"], p * 2 + 2)
                    st.link(v.tensor_tensor(one[:, 8:9], one[:, 0:1], one[:, 1:2], ALU.add))
                    v.tensor_scalar(one[:, 2:3], one[:, 8:9], 1.0 / D, EPS, ALU.mult,
                                    ALU.add).then_inc(s["h2_ms"], 1)
                    st.wait(s["h2_std"], p + 1)
                    st.link(v.reciprocal(one[:, 9:10], one[:, 3:4]))
                    hb = hbuf(p, par)
                    st.link(v.scalar_tensor_tensor(out=hb, in0=hb,
                                                   scalar=one[:, 9:10], in1=bc[:, 0, j, :],
                                                   op0=ALU.mult, op1=ALU.mult))
                    v.tensor_tensor(hb, hb, bc[:, 1, j, :],
                                    ALU.add).then_inc(s["h2_done"], 1)
                    st.wait(s["h2_done"], p + 1)
                if not rows:
                    for hd in range(PH):
                        for n in (2 * (CC + hd), 2 * (CC + hd) + 1):
                            x1_tile(n)
                        for side in range(2):
                            side_top(p, hd, hd % 2, side)
                        square_top(hd)
                        expert_numbers(p, hd)
                else:
                    with st.loop(PH // 2, 2 * HEAD_PREP * prep) as pair:
                        for odd in range(2):
                            hd = pair * 2 + odd
                            dots_of(p, par, hd, 0, 5)
                            for side in range(2):
                                if prep:
                                    side_top(p, hd, odd, side)
                                dots_of(p, par, hd, 5 + 2 * side, 7 + 2 * side)
                            if prep:
                                square_top(hd)
                            dots_of(p, par, hd, 9, 11)
                            if prep:
                                expert_numbers(p, hd)
                            dots_of(p, par, hd, 11, TOP)
                if prep:
                    lv = logit.rearrange("p (h k) -> p h k", h=PH)
                    ev = expd.rearrange("p (h k) -> p h k", h=PH)
                    v.tensor_tensor(ev, lv, lv[:, :, 0:1].to_broadcast([P, PH, TOP]),
                                    ALU.subtract).then_inc(s["ls_done"], 1)
                    st.wait(s["exp_done"], p + 1)
                    st.link(v.tensor_reduce(rsum[:, 0, :], ev, AX.X, ALU.add))
                    st.link(v.reciprocal(rsum[:, 1, :], rsum[:, 0, :]))
                    if rows:
                        st.wait(s["diag_done"], p * P)
                    v.tensor_tensor(gsm.rearrange("p (h k) -> p h k", h=PH), ev,
                                    rsum[:, 1, :].unsqueeze(2).to_broadcast([P, PH, TOP]),
                                    ALU.mult).then_inc(s["gsm_done"], 1)
                if rows:
                    jo = 1 if not isinstance(p, int) else (0 if p - 1 < CC else 1)
                    st.wait(s["gt2_back"], 16)
                    st.wait(s["y_stored"], (p - 1) * 16)
                    st.wait(s["vacc_full"], p)
                    st.link(v.tensor_tensor(yb, ps[:, 0:2, :].rearrange("p b n -> p (b n)"),
                                            bc[:, 2, jo, :], ALU.mult))
                    dve.sem_inc(s["vacc_free"], 1)
                    st.wait(s["xo_in"], p * 16)
                    st.link(v.tensor_tensor(yb, yb, xo, ALU.add))
                    dve.sem_inc(s["y_sum"], 1)
                    st.wait(s["y_sq"], p)
                    v.tensor_scalar(one[:, 6:7], one[:, 4:5], 1.0 / D, EPS, ALU.mult,
                                    ALU.add).then_inc(s["y_ms"], 1)
                    st.wait(s["y_std"], p)
                    st.wait(s["in_fg"], 16)
                    st.link(v.reciprocal(one[:, 5:6], one[:, 7:8]))
                    v.scalar_tensor_tensor(out=yb, in0=yb, scalar=one[:, 5:6], in1=rowbc[:, :],
                                           op0=ALU.mult, op1=ALU.mult).then_inc(s["y_done"], 1)
                    st.wait(s["y_done"], p)

            HEAD_PREP = 3 * 5 + 2 + 1 + 2 + 1 + 3
            per_phase = 3 + PH * HEAD_PREP + 2 + 2 + 1
            phases(st, phase, 2 * per_phase)


def scan_chunk(it, r):
    if it < CC:
        return it if r == 0 else CC - 1 - it
    return it if r == 0 else NC - 1 + CC - it


def units_of(w):
    n = w.shape[1] // UW
    return np.ascontiguousarray(w.reshape(KD, P, n, UW).transpose(2, 1, 0, 3)).reshape(n, P, KD * UW)


def columns_of(x):
    x = x.reshape(-1, x.shape[-1] // P, P)
    return np.ascontiguousarray(x.transpose(2, 0, 1)).reshape(P, -1)


def spread(x):
    return np.ascontiguousarray(np.broadcast_to(x.reshape(1, -1), (P, x.size)))


def kernel(x_prompt, x_sample, state_ret, c, c_ctx, w_mod, b_mod, norm_g, w_in, w_out,
           gmlp_ws, gmlp_b, gmlp_ln_g, pool_w, pool_scale, ret_decay, peer_wq, peer_subkeys,
           peer_u, peer_v, final_norm_g):
    import concourse.bacc as bacc
    from concourse.bass_utils import run_bass_kernel_spmd

    arr = np.asarray
    w = arr(w_in)[0]
    u0, v0, z0, q0, k0, rv0, rf0, rb0, gm0 = (0, 1024, 2048, 3072, 3584, 4096, 5120, 6144, 7168)
    wa = np.concatenate([w[:, v0:v0 + D], w[:, u0:u0 + D], w[:, gm0:gm0 + D]], axis=1)
    heads, gcs = [], []
    for h in range(HEADS):
        heads += [w[:, q0 + h * DK:q0 + (h + 1) * DK], w[:, k0 + h * DK:k0 + (h + 1) * DK],
                  w[:, rv0 + h * DV:rv0 + (h + 1) * DV], w[:, rf0 + h * DV:rf0 + (h + 1) * DV],
                  w[:, rb0 + h * DV:rb0 + (h + 1) * DV]]
        at = gm0 + 2 * D + h * DV
        gcs.append(w[:, at:at + DV].reshape(KD, P, DV).transpose(1, 0, 2).reshape(P, KD * DV))
    mlat, mctx = pool_constants()
    x = np.concatenate([arr(x_prompt).reshape(CTX, D), arr(x_sample).reshape(LAT, D)])
    conds = np.stack([arr(c_ctx).reshape(D), arr(c).reshape(D)])
    host = {
        "x": x.reshape(NC, P, D),
        "cond": np.ascontiguousarray(conds.reshape(2, KD, P).transpose(2, 1, 0)).reshape(P, KD * 2),
        "wmod": units_of(arr(w_mod)[0][:, 0:2 * D]),
        "wlate": np.ascontiguousarray(
            arr(w_mod)[0][:, 2 * D:].reshape(KD, P, 16, UW // 2).transpose(2, 1, 0, 3)
        ).reshape(16, P, KD * UW // 2),
        "bmod": columns_of(arr(b_mod)[0]),
        "ng": columns_of(arr(norm_g)[0]),
        "decay": spread(arr(ret_decay)[0]),
        "lng": spread(arr(gmlp_ln_g)[0]),
        "mix": np.ascontiguousarray(arr(gmlp_ws)[0].transpose(2, 0, 1)).reshape(P, G * P),
        "bsp": np.ascontiguousarray(arr(gmlp_b)[0].T),
        "wa": units_of(wa),
        "whead": units_of(np.concatenate(heads, axis=1)),
        "wgc": np.ascontiguousarray(np.stack(gcs)),
        "state": arr(state_ret)[0, 0],
        "wz": units_of(w[:, z0:z0 + D]),
        "mctx": mctx,
        "mlat": mlat,
        "poolw": np.ascontiguousarray(arr(pool_w)[0].reshape(G, 2, P, GW).transpose(2, 0, 1, 3)
                                      ).reshape(P, G * 2 * GW),
        "psc": spread(arr(pool_scale)[0]),
        "wgb": units_of(w[:, gm0 + D:gm0 + 2 * D]),
        "wout": units_of(arr(w_out)[0]),
        "subk": np.ascontiguousarray(arr(peer_subkeys)[0].transpose(3, 0, 1, 2)).reshape(P, 2 * PH * NK),
        "fg": spread(arr(final_norm_g)),
        "wq": arr(peer_wq)[0].reshape(KD, P, 2 * D),
        "peer": np.concatenate([arr(peer_u)[0], arr(peer_v)[0]], axis=1),
    }
    nc = bacc.Bacc("TRN2", target_bir_lowering=False, num_devices=1)
    a = {}
    for name, value in host.items():
        host[name] = np.ascontiguousarray(value)
        a[name] = nc.dram_tensor(f"in_{name}", value.shape, F32, kind="ExternalInput").ap()
    a["y"] = nc.dram_tensor("out_y", [NC, P, D], F32, kind="ExternalOutput").ap()
    a["new_state"] = nc.dram_tensor("out_state", [2, HEADS, DK, DV], F32, kind="ExternalOutput").ap()
    build(nc, a)
    r = run_bass_kernel_spmd(nc, [{f"in_{n}": v for n, v in host.items()}], core_ids=[0])
    y = r.results[0]["out_y"].reshape(T, D)
    new_state = r.results[0]["out_state"].reshape(1, 1, 2, HEADS, DK, DV)
    return (np.ascontiguousarray(y[:CTX]).reshape(1, CTX, D),
            np.ascontiguousarray(y[CTX:]).reshape(1, LAT, D), new_state)
```
